# Optimizing a Trainium2 kernel written in Bass

```python
import jax, jax.numpy as jnp
from jax import lax
import numpy as np

D_MODEL = 2048
BATCH = 1
SEQ = 128
DEPTH = 2
DEC_BATCH = 1
DEC_SEQ = 128
PAST_LEN = 128

GRID_W = 64
D_MIX = D_MODEL
HEAD_DIM = 128
N_HEADS = (D_MIX // 2) // HEAD_DIM
N_KV_HEADS = 2
GROUP = N_HEADS // N_KV_HEADS
D_ATTN = N_HEADS * HEAD_DIM
D_KV = N_KV_HEADS * HEAD_DIM
ROPE_THETA = 10000.0
Q_BLOCK = 128
D_CONV = D_MIX // 4
CONV_WIDTH = 3
D_RWKV = D_MIX // 4
RWKV_HEAD = 64
RWKV_HEADS = D_RWKV // RWKV_HEAD
DECAY_RANK = 32
A_RANK = 32
GATE_RANK = 96
D_RWKV_IN = 3 * D_RWKV + DECAY_RANK + A_RANK + GATE_RANK
D_IN = D_ATTN + 2 * D_KV + 3 * D_CONV + D_RWKV_IN
SPLIT_IN = [D_ATTN, D_ATTN + D_KV, D_ATTN + 2 * D_KV, D_ATTN + 2 * D_KV + D_CONV,
            D_ATTN + 2 * D_KV + 2 * D_CONV, D_ATTN + 2 * D_KV + 3 * D_CONV]
SPLIT_RWKV = [D_RWKV, 2 * D_RWKV, 3 * D_RWKV, 3 * D_RWKV + DECAY_RANK,
              3 * D_RWKV + DECAY_RANK + A_RANK]
D_FF = -(-(8 * D_MODEL) // (3 * 256)) * 256
N_MOD = 6
EPS = 1e-6
GN_EPS = 64e-5

kernel_name = 'hybrid_dit_parallel_heads_step'

def rmsnorm(x, g):
    xf = x.astype(jnp.float32)
    y = xf * lax.rsqrt(jnp.mean(xf * xf, axis=-1, keepdims=True) + EPS)
    return (y * g.astype(jnp.float32)).astype(x.dtype)

def axial_rope(n):
    rows = n // GRID_W
    row = jnp.repeat(jnp.arange(rows), GRID_W).astype(jnp.float32)
    col = jnp.tile(jnp.arange(GRID_W), rows).astype(jnp.float32)
    half = HEAD_DIM // 2
    inv = 1.0 / (ROPE_THETA ** (jnp.arange(0, half, 2, dtype=jnp.float32) / half))
    ar = row[:, None] * inv
    ac = col[:, None] * inv
    ang = jnp.concatenate([ar, ar, ac, ac], axis=-1)
    return jnp.cos(ang), jnp.sin(ang)

def apply_rope(x, cos, sin):
    x1, x2, x3, x4 = jnp.split(x, 4, axis=-1)
    rot = jnp.concatenate([-x2, x1, -x4, x3], axis=-1)
    cos = cos[None, :, None, :].astype(x.dtype)
    sin = sin[None, :, None, :].astype(x.dtype)
    return x * cos + rot * sin

def shift_prev(u):
    return jnp.pad(u, ((0, 0), (1, 0), (0, 0)))[:, :-1]

def shift_next(u):
    return jnp.pad(u, ((0, 0), (0, 1), (0, 0)))[:, 1:]

def short_conv(u, w):
    return shift_prev(u) * w[0] + u * w[1] + shift_next(u) * w[2]

def attention(q, k, v):
    b, n = q.shape[:2]
    nb = n // Q_BLOCK
    qb = q.reshape(b, nb, Q_BLOCK, N_KV_HEADS, GROUP, HEAD_DIM).swapaxes(0, 1)
    scale = HEAD_DIM ** -0.5

    def block(qi):
        s = jnp.einsum('bqkgd,bskd->bkgqs', qi, k).astype(jnp.float32) * scale
        p = jax.nn.softmax(s, axis=-1).astype(v.dtype)
        return jnp.einsum('bkgqs,bskd->bqkgd', p, v)

    o = lax.map(block, qb)
    return o.swapaxes(0, 1).reshape(b, n, D_ATTN)

def rwkv_scan(r, w, k, v, kk, a, s0, reverse):
    xs = tuple(t.swapaxes(0, 1) for t in (r, w, k, v, kk, a))

    def step(S, inp):
        r_t, w_t, k_t, v_t, kk_t, a_t = inp
        sa = jnp.einsum('bhij,bhj->bhi', S, -kk_t)
        S = (S * w_t[:, :, None, :] + sa[..., None] * (kk_t * a_t)[:, :, None, :]
             + v_t[..., None] * k_t[:, :, None, :])
        return S, jnp.einsum('bhij,bhj->bhi', S, r_t)

    S, y = lax.scan(step, s0, xs, reverse=reverse)
    return y.swapaxes(0, 1), S

def rwkv_mixer(u, s0, P, l):
    dt = u.dtype
    b, n = u.shape[:2]
    u = u + P['rwkv_mu'][l] * (0.5 * (shift_prev(u) + shift_next(u)) - u)
    u = u.astype(jnp.float32)
    r, k, v, xw, xa, xg = jnp.split(u, SPLIT_RWKV, axis=-1)

    def hs(t):
        return t.reshape(b, n, RWKV_HEADS, RWKV_HEAD)

    def f(name):
        return P[name][l].astype(jnp.float32)

    g = jax.nn.sigmoid(xg) @ f('rwkv_g_up')
    kk = hs(k * f('rwkv_k_k'))
    kk = kk * lax.rsqrt(jnp.sum(kk * kk, axis=-1, keepdims=True) + 1e-12)
    rh, vh = hs(r), hs(v)
    r_k = f('rwkv_r_k')
    s0 = s0.astype(jnp.float32)
    ys, bonuses, states = [], [], []
    for d in range(2):
        w = -jax.nn.softplus(-(f('rwkv_w0')[d] + jnp.tanh(xw) @ f('rwkv_w_up')[d])) - 0.5
        decay = jnp.exp(-jnp.exp(w))
        a = jax.nn.sigmoid(f('rwkv_a0')[d] + xa @ f('rwkv_a_up')[d])
        kd = hs(k * (1.0 + (a - 1.0) * f('rwkv_k_a')))
        yd, Sd = rwkv_scan(rh, hs(decay), kd, vh, kk, hs(a), s0[:, d], reverse=(d == 1))
        ys.append(yd)
        bonuses.append(jnp.sum(rh * kd * r_k, axis=-1, keepdims=True) * vh)
        states.append(Sd)
    y = ys[0] + ys[1]
    mean = jnp.mean(y, axis=-1, keepdims=True)
    var = jnp.mean(jnp.square(y - mean), axis=-1, keepdims=True)
    yn = ((y - mean) * lax.rsqrt(var + GN_EPS)).reshape(b, n, D_RWKV) * f('rwkv_ln_g') + f('rwkv_ln_b')
    out = (yn + (bonuses[0] + bonuses[1]).reshape(b, n, D_RWKV)) * g
    return out.astype(dt), jnp.stack(states, axis=1)

def layer(x, mod, P, l, rope, ctx_k, ctx_v, s0):
    b, n = x.shape[:2]
    sh_a, sc_a, g_a, sh_f, sc_f, g_f = jnp.split(mod, N_MOD, axis=-1)
    ng = P['norm_g'][l]
    h = rmsnorm(x, ng[0]) * (1 + sc_a) + sh_a
    proj = h @ P['w_in'][l]
    q, k, v, cb, cc, ch, ur = jnp.split(proj, SPLIT_IN, axis=-1)
    q = rmsnorm(q.reshape(b, n, N_HEADS, HEAD_DIM), P['q_norm'][l])
    k = rmsnorm(k.reshape(b, n, N_KV_HEADS, HEAD_DIM), P['k_norm'][l])
    v = v.reshape(b, n, N_KV_HEADS, HEAD_DIM)
    if rope is None:
        keys, vals = k, v
    else:
        q = apply_rope(q, rope[0], rope[1])
        k = apply_rope(k, rope[0], rope[1])
        keys = jnp.concatenate([k, ctx_k], axis=1)
        vals = jnp.concatenate([v, ctx_v], axis=1)
    attn = attention(q.reshape(b, n, N_KV_HEADS, GROUP, HEAD_DIM), keys, vals)
    conv = cb * short_conv(cc * ch, P['conv_w'][l])
    rw, S = rwkv_mixer(ur, s0, P, l)
    o = jnp.concatenate([attn, conv, rw], axis=-1) @ P['w_out'][l]
    x = x + g_a * rmsnorm(o, ng[1])
    h = rmsnorm(x, ng[2]) * (1 + sc_f) + sh_f
    ff = (jax.nn.silu(h @ P['w_gate'][l]) * (h @ P['w_up'][l])) @ P['w_down'][l]
    x = x + g_f * rmsnorm(ff, ng[3])
    return x, k, v, S

def setup_inputs(seed: int = 0) -> dict:
    key = jax.random.key(seed)
    ks = jax.random.split(key, 32)

    def nrm(i, shape, scale):
        return jax.random.normal(ks[i], shape, jnp.float32) * scale

    L, D = DEPTH, D_MODEL
    return {
        'x_prompt': nrm(0, (BATCH, SEQ, D), 1.0),
        'x_sample': nrm(1, (DEC_BATCH, DEC_SEQ, D), 1.0),
        'cache_k': nrm(2, (DEC_BATCH, L, PAST_LEN, N_KV_HEADS, HEAD_DIM), 1.0),
        'cache_v': nrm(3, (DEC_BATCH, L, PAST_LEN, N_KV_HEADS, HEAD_DIM), 1.0),
        'state_rwkv': nrm(4, (DEC_BATCH, L, 2, RWKV_HEADS, RWKV_HEAD, RWKV_HEAD), 0.1),
        'c': nrm(5, (DEC_BATCH, D), 1.0),
        'c_ctx': nrm(6, (D,), 1.0),
        'w_ada': nrm(7, (L, D, N_MOD * D), D ** -0.5),
        'b_ada': nrm(8, (L, N_MOD * D), 0.01),
        'norm_g': 1.0 + nrm(9, (L, 4, D), 0.05),
        'w_in': nrm(10, (L, D, D_IN), D ** -0.5),
        'q_norm': 1.0 + nrm(11, (L, HEAD_DIM), 0.05),
        'k_norm': 1.0 + nrm(12, (L, HEAD_DIM), 0.05),
        'conv_w': nrm(13, (L, CONV_WIDTH, D_CONV), CONV_WIDTH ** -0.5),
        'rwkv_mu': 0.5 + nrm(14, (L, D_RWKV_IN), 0.1),
        'rwkv_w0': nrm(15, (L, 2, D_RWKV), 1.0),
        'rwkv_w_up': nrm(16, (L, 2, DECAY_RANK, D_RWKV), 0.1),
        'rwkv_a0': nrm(17, (L, 2, D_RWKV), 0.1),
        'rwkv_a_up': nrm(18, (L, 2, A_RANK, D_RWKV), 0.1),
        'rwkv_g_up': nrm(19, (L, GATE_RANK, D_RWKV), GATE_RANK ** -0.5),
        'rwkv_k_k': 0.85 + nrm(20, (L, D_RWKV), 0.02),
        'rwkv_k_a': 1.0 + nrm(21, (L, D_RWKV), 0.02),
        'rwkv_r_k': nrm(22, (L, RWKV_HEADS, RWKV_HEAD), 0.1),
        'rwkv_ln_g': 1.0 + nrm(23, (L, D_RWKV), 0.05),
        'rwkv_ln_b': nrm(24, (L, D_RWKV), 0.01),
        'w_out': nrm(25, (L, D_MIX, D), D_MIX ** -0.5),
        'w_gate': nrm(26, (L, D, D_FF), D ** -0.5),
        'w_up': nrm(27, (L, D, D_FF), D ** -0.5),
        'w_down': nrm(28, (L, D_FF, D), D_FF ** -0.5),
    }

def reference(x_prompt, x_sample, cache_k, cache_v, state_rwkv, c, c_ctx, w_ada, b_ada, norm_g,
              w_in, q_norm, k_norm, conv_w, rwkv_mu, rwkv_w0, rwkv_w_up, rwkv_a0, rwkv_a_up,
              rwkv_g_up, rwkv_k_k, rwkv_k_a, rwkv_r_k, rwkv_ln_g, rwkv_ln_b, w_out, w_gate, w_up,
              w_down):
    P = {'norm_g': norm_g, 'w_in': w_in, 'q_norm': q_norm, 'k_norm': k_norm, 'conv_w': conv_w,
         'rwkv_mu': rwkv_mu, 'rwkv_w0': rwkv_w0, 'rwkv_w_up': rwkv_w_up, 'rwkv_a0': rwkv_a0,
         'rwkv_a_up': rwkv_a_up, 'rwkv_g_up': rwkv_g_up, 'rwkv_k_k': rwkv_k_k,
         'rwkv_k_a': rwkv_k_a, 'rwkv_r_k': rwkv_r_k, 'rwkv_ln_g': rwkv_ln_g,
         'rwkv_ln_b': rwkv_ln_b, 'w_out': w_out, 'w_gate': w_gate, 'w_up': w_up,
         'w_down': w_down}

    xp = x_prompt
    s_zero = jnp.zeros((xp.shape[0], 2, RWKV_HEADS, RWKV_HEAD, RWKV_HEAD), jnp.float32)
    ks, vs, ss = [], [], []
    for l in range(DEPTH):
        mod = (jax.nn.silu(c_ctx) @ w_ada[l] + b_ada[l])[None, None, :]
        xp, k_l, v_l, s_l = layer(xp, mod, P, l, None, None, None, s_zero)
        ks.append(k_l)
        vs.append(v_l)
        ss.append(s_l.astype(x_prompt.dtype))
    new_k = jnp.stack(ks, axis=1)
    new_v = jnp.stack(vs, axis=1)
    new_rwkv = jnp.stack(ss, axis=1)

    rope = axial_rope(x_sample.shape[1])
    xs = x_sample
    for l in range(DEPTH):
        mod = (jax.nn.silu(c) @ w_ada[l] + b_ada[l])[:, None, :]
        xs, _, _, _ = layer(xs, mod, P, l, rope, cache_k[:, l], cache_v[:, l], state_rwkv[:, l])

    return (xp, xs, new_k, new_v, new_rwkv)


_drawn_inputs = setup_inputs


def setup_inputs(seed=0):
    import zlib

    import numpy as np

    out = dict(_drawn_inputs(seed))
    spreads = {}
    factors = {'state_rwkv': 8.0, 'q_norm': 8.0, 'rwkv_ln_g': 6.694, 'rwkv_ln_b': 54.455}
    for name, (base, spread) in spreads.items():
        noise = np.random.default_rng([zlib.crc32(name.encode()), seed]).standard_normal(out[name].shape)
        drawn = base * np.exp(spread * noise) if base else spread * noise
        out[name] = __import__('jax').numpy.asarray(drawn.astype(out[name].dtype))
    for name, factor in factors.items():
        out[name] = (out[name] * factor).astype(out[name].dtype)
    return out
```

```python
from contextlib import ExitStack

import numpy as np
import concourse.bass as bass
from concourse import mybir

F32 = mybir.dt.float32
F32R = mybir.dt.float32r
U32 = mybir.dt.uint32
ALU = mybir.AluOpType
ACT = mybir.ActivationFunctionType
AX = mybir.AxisListType.X

P = 128
LAYERS = 2
D = 2048
KT = D // P
NW = 512
HD = 128
NH, NKV = 8, 2
D_QK = (NH + NKV) * HD
D_ATT = D_QK + NKV * HD
D_CONV = 512
D_RW = 512
RW_HEADS, RH = 8, 64
FT = D_RW // P
OFF_CONV = D_ATT
OFF_RW = OFF_CONV + 3 * D_CONV
RANK, GATE_RANK = 32, 96
D_RWIN = 3 * D_RW + 2 * RANK + GATE_RANK
D_IN = OFF_RW + D_RWIN
D_FF = 5632
EPS, GN_EPS, KK_EPS = 1e-6, 64e-5, 1e-12
ALPHA = float(np.exp(-0.5))
SCALE = float(HD) ** -0.5
LEVELS = 7

CPT = KT // 2
LEAD = 4
WIN_TILES = -(-D_IN // NW)
WIN_LAST = D_IN - (WIN_TILES - 1) * NW
OUT_TILES = D // NW
FF_TILES = D_FF // NW
Q_ADA01 = 0
Q_WIN = Q_ADA01 + 8 * 2
Q_ADA2 = Q_WIN + WIN_TILES * 2
Q_WOUT = Q_ADA2 + 4 * 2
Q_ADA34 = Q_WOUT + OUT_TILES * 2
Q_FFN = Q_ADA34 + 8 * 2
Q_ADA5 = Q_FFN + FF_TILES * 6
Q_LAYER = Q_ADA5 + 4 * 2

C_ID, C_BO, C_BM, C_LV = 0, 128, 256, 384
C_TRI = C_LV + LEVELS * P
C_COS = C_TRI + 2 * 256
C_SIN = C_COS + P
C_SELT = C_SIN + P
C_SELB = C_SELT + 2
C_ONE = C_SELB + 256
C_HALF = C_ONE + P
C_ALL = C_HALF + 1

COL_MU, COL_W0, COL_A0, COL_KK, COL_KA, COL_RK, COL_LG, COL_LB, COL_CV = 0, 14, 22, 30, 34, 38, 42, 46, 50
ROWS_P = 62
COL_NG = ROWS_P
COL_B = COL_NG + 4 * KT
COLS = COL_B + 6 * KT
VSTEPS, FSTEPS = 84, 25
BARS = 16


def constants():
    c = np.zeros((P, C_ALL), np.float32)
    i = np.arange(P)
    same = lambda b: (i[:, None] // b == i[None, :] // b).astype(np.float32)
    c[:, C_ID:C_ID + P] = np.eye(P)
    c[:, C_BO:C_BO + P] = same(RH)
    c[:, C_BM:C_BM + P] = same(RH) / RH
    for n in range(LEVELS):
        c[:, C_LV + n * P:C_LV + (n + 1) * P] = same(1 << n) - same(2 << n)
    s, t = i[:, None], i[None, :]
    for d, (excl, incl) in enumerate([(s < t, s <= t), (s > t, s >= t)]):
        c[:, C_TRI + d * 256:C_TRI + d * 256 + P] = excl
        c[:, C_TRI + d * 256 + P:C_TRI + (d + 1) * 256] = incl
    half = HD // 2
    inv = (np.float32(1.0) / (np.float32(10000.0) ** (np.arange(0, half, 2, dtype=np.float32) / np.float32(half))))
    ar = (i // 64).astype(np.float32)[:, None] * inv
    ac = (i % 64).astype(np.float32)[:, None] * inv
    ang = np.concatenate([ar, ar, ac, ac], axis=-1).astype(np.float32)
    sign = np.repeat(np.array([-1, 1, -1, 1], np.float32), 32)
    c[:, C_COS:C_COS + P] = np.cos(ang)
    c[:, C_SIN:C_SIN + P] = np.sin(ang) * sign
    for row in range(4):
        c[row, C_SELT + row % 2] = 1
        c[row, C_SELB + (row % 2) * P:C_SELB + (row % 2 + 1) * P] = 1
    c[:, C_ONE:C_ONE + P] = 1
    c[:, C_HALF] = -0.5
    return c


def hybrid_trunk(nc, A, O):
    ctx = ExitStack()
    with ctx:
        def sb(name, shape, dt=F32, at=ctx):
            return at.enter_context(nc.sbuf_tensor(name, shape, dt))

        def sem(name):
            return ctx.enter_context(nc.semaphore(name))

        x = sb("x", [P, 2, D])
        actH = sb("actH", [P, KT, 256], F32R)
        actL = sb("actL", [P, KT, 256], F32R)
        rawW = sb("rawW", [P, LEAD, 2, NW])
        hiW = sb("hiW", [P, LEAD, 2, NW], F32R)
        loW = sb("loW", [P, LEAD, 2, NW], F32R)
        con = sb("con", [P, C_ALL])
        col = sb("col", [P, COLS])
        muh = sb("muh", [P, 14])
        omu = sb("omu", [P, 14])
        oka = sb("oka", [P, 4])
        wla = sb("wla", [64, 2, D_RW])
        wg = sb("wg", [GATE_RANK, D_RW])
        ctxk = sb("ctxk", [P, NKV, HD])
        ctxv = sb("ctxv", [P, NKV, HD])
        qkw = sb("qkw", [P, 2, HD])
        s0all = sb("s0all", [P, 2, FT, RH])
        s0bd = sb("s0bd", [P, 2, P])
        csR = sb("csR", [P, 192], F32R)
        modT = sb("modT", [P, 4, KT, 2])
        st = sb("st", [P, 8])
        ss, ms, rstd = st[:, 0:2], st[:, 2:4], st[:, 4:6]
        bank = [ctx.enter_context(nc.psum_tensor(f"bank{i}", [P, NW], F32)) for i in range(8)]

        ident = con[:, C_ID:C_ID + P]
        blk1 = con[:, C_BO:C_BO + P]
        blkm = con[:, C_BM:C_BM + P]
        ones = con[:, C_ONE:C_ONE + P]
        mhalf = con[:, C_HALF:C_HALF + 1]

        with ExitStack() as ph:
            prm = sb("prm", [P, 3, P], F32, ph)
            rows1 = sb("rows1", [4, 2, NW], F32, ph)
            xs1 = sb("xs1", [P, 2, D], F32, ph)
            tf1 = sb("tf1", [P, 2, NW], F32, ph)
            csf = sb("csf", [P, 3, P], F32, ph)
        with ExitStack() as ph:
            uT = sb("uT", [P, 14, 2, 130], F32, ph)
            with ExitStack() as ph2:
                proj = sb("proj", [P, 2, D_IN], F32, ph2)
                with ExitStack() as ph3:
                    chT = sb("chT", [P, 2, 4, P], F32, ph3)
                    mT = sb("mT", [P, 4, 2, 130], F32, ph3)
                    cv = sb("cv", [P, 4, 2, P], F32, ph3)
                with ExitStack() as ph3:
                    qk = sb("qk", [P, 10, HD], F32, ph3)
                    scr = sb("scr", [P, 20, HD], F32, ph3)
                    qst = sb("qst", [P, 64], F32, ph3)
                    qT = sb("qT", [P, NH, P], F32, ph3)
                    kT = sb("kT", [P, NKV, 256], F32, ph3)
                    pr = sb("pr", [P, NH, 256], F32, ph3)
            with ExitStack() as ph2:
                tmp3 = sb("tmp3", [P, 3, 2, P], F32, ph2)
                rkv = sb("rkv", [P, 3, 2, P], F32, ph2)
                kk = sb("kk", [P, 2, P], F32, ph2)
                ksq = sb("ksq", [P, 2, P], F32, ph2)
                nrm = sb("nrm", [P, 2, P], F32, ph2)
                xwa = sb("xwa", [64, 2, P], F32, ph2)
                xg = sb("xg", [GATE_RANK, 2, P], F32, ph2)
                wS = sb("wS", [64, 2, P], F32, ph2)
                gS = sb("gS", [GATE_RANK, P], F32, ph2)
                sa_ = sb("sigaa", [P, 4, 2, P], F32, ph2)
                gT = sb("gT", [P, 2, P], F32, ph2)
                cs = sb("cs", [P, 2, 2, 129], F32, ph2)
                E1 = sb("E1", [P, 2, 2, 129], F32, ph2)
                E2 = sb("E2", [P, 2, 2, 129], F32, ph2)
                amid = sb("amid", [P, 8], F32, ph2)
                kd = sb("kd", [P, 2, 2, P], F32, ph2)
                KR = sb("KR", [P, 2, 2, 2, P], F32, ph2)
                be = sb("be", [P, 2, 2, P], F32, ph2)
                ga = sb("ga", [P, 2, 2, P], F32, ph2)
                AE = sb("AE", [P, 2, 4, 256], F32, ph2)
                BF = sb("BF", [P, 2, 4, 256], F32, ph2)
                X = sb("X", [P, 2, 4, 256], F32, ph2)
                CT = sb("CT", [P, 2, 4, P], F32, ph2)
                U = sb("U", [P, 2, 4, P], F32, ph2)
                Rs = sb("Rs", [P, 4, P], F32, ph2)
                SA = sb("SA", [P, 4, P], F32, ph2)
                Vt = sb("Vt", [P, 2, P], F32, ph2)
                S0s = sb("S0s", [P, 2, P], F32, ph2)
                STs = sb("STs", [P, 2, RH], F32, ph2)
        with ExitStack() as ph:
            G = sb("G", [P, 2, D], F32, ph)
            o = sb("o", [P, 2, D], F32, ph)
            bB = sb("bB", [P, D], F32, ph)
            nB = sb("nB", [P, D], F32, ph)
            rows2 = sb("rows2", [4, 2, NW], F32, ph)
            with ExitStack() as ph2:
                xs2 = sb("xs2", [P, 2, D], F32, ph2)
                tf2 = sb("tf2", [P, 2, NW], F32, ph2)
            with ExitStack() as ph2:
                sg = sb("sg", [P, 2, NW], F32, ph2)
                ff = sb("ff", [P, 2, NW], F32, ph2)
                ffH = sb("ffH", [P, 4, 256], F32R, ph2)
                ffL = sb("ffL", [P, 4, 256], F32R, ph2)
        qc, qs = scr[:, 0:10], scr[:, 10:20]
        pT = scr[:, 0:16].rearrange("p (k h) t -> p k h t", k=2)
        sig = [sa_[:, d].rearrange("p g t -> p (g t)") for d in range(2)]
        aa = [sa_[:, 2 + d].rearrange("p g t -> p (g t)") for d in range(2)]
        yy = sig + aa
        bg0 = kd
        bgt = cs[:].rearrange("p d g t -> p (d g t)")[:, 0:4 * P].rearrange("p (d n j) -> p d n j", d=2, n=2)

        passed = sem("passed")
        con_in, c_in, x_in = sem("con_in"), sem("c_in"), sem("x_in")
        cs_done = sem("cs_done")
        raw_full = [sem(f"raw_full{n}") for n in range(LEAD)]
        hi_ready, lo_ready = sem("hi_ready"), sem("lo_ready")
        chunk_used = sem("chunk_used")
        rows_out, ada_post = sem("rows_out"), sem("ada_post")
        evac_v, evac_s = sem("evac_v"), sem("evac_s")
        par_rows, par_tabs = sem("par_rows"), sem("par_tabs")
        prm_zero, cols_T = sem("prm_zero"), sem("cols_T")
        end_pe, end_act, end_dve, end_pool = sem("end_pe"), sem("end_act"), sem("end_dve"), sem("end_pool")
        vsteps, fsteps = sem("vsteps"), sem("fsteps")
        sq_in, ms_in, rs_in, xs_in = sem("sq_in"), sem("ms_in"), sem("rs_in"), sem("xs_in")
        nt_T, nt_f, nt_hi = sem("nt_T"), sem("nt_f"), sem("nt_hi")
        gb_in = sem("gb_in")
        cv_T, cv_ch, cv_z, cv_out, cv_hi = sem("cv_T"), sem("cv_ch"), sem("cv_z"), sem("cv_out"), sem("cv_hi")
        at_ms, at_rs, at_qk, at_T = sem("at_ms"), sem("at_rs"), sem("at_qk"), sem("at_T")
        at_ca, at_cv, at_S, at_mx = sem("at_ca"), sem("at_cv"), sem("at_S"), sem("at_mx")
        at_P, at_Pn, at_PT, at_pa, at_pv = sem("at_P"), sem("at_Pn"), sem("at_PT"), sem("at_pa"), sem("at_pv")
        at_O, at_hi, kv_out = sem("at_O"), sem("at_hi"), sem("kv_out")
        u_T = sem("u_T")
        lr_mix, lr_act, ab_z = sem("lr_mix"), sem("lr_act"), sem("ab_z")
        rw_v, rw_sq, rw_nrm, rw_ns, rw_rs = sem("rw_v"), sem("rw_sq"), sem("rw_nrm"), sem("rw_ns"), sem("rw_rs")
        rw_stage, rw_lr, rw_sig, rw_aa = sem("rw_stage"), sem("rw_lr"), sem("rw_sig"), sem("rw_aa")
        rw_s0, rw_VS, rw_Vt, rw_c, rw_E = sem("rw_s0"), sem("rw_VS"), sem("rw_Vt"), sem("rw_c"), sem("rw_E")
        rw_kr, rw_A, rw_m, rw_S0s = sem("rw_kr"), sem("rw_A"), sem("rw_m"), sem("rw_S0s")
        rw_bo, rw_bon, rw_bg, rw_bgT, rw_bgs = sem("rw_bo"), sem("rw_bon"), sem("rw_bg"), sem("rw_bgT"), sem("rw_bgs")
        rw_bv = sem("rw_bv")
        rw_R, rw_Rs, rw_SA, rw_SAs = sem("rw_R"), sem("rw_Rs"), sem("rw_SA"), sem("rw_SAs")
        lv_X0, lv_C, lv_U, lv_Us, lv_XM, lv_X = (sem(n) for n in ("lv_X0", "lv_C", "lv_U", "lv_Us", "lv_XM", "lv_X"))
        rw_Y, rw_ST, rw_y, rw_mean, rw_yc, rw_y2 = (sem(n) for n in ("rw_Y", "rw_ST", "rw_y", "rw_mean", "rw_yc", "rw_y2"))
        rw_var, rw_vs, rw_vr, rw_o, rw_hi = (sem(n) for n in ("rw_var", "rw_vs", "rw_vr", "rw_o", "rw_hi"))
        ST_v, st_out, y_out = sem("ST_v"), sem("st_out"), sem("y_out")
        ff_s, ff_g, ff_u, ff_T, ff_hi, ff_lo, dn_out = (sem(n) for n in (
            "ff_s", "ff_g", "ff_u", "ff_T", "ff_hi", "ff_lo", "dn_out"))
        ENDS = {"pe": end_pe, "act": end_act, "dve": end_dve, "pool": end_pool}

        def settle(eng):
            eng.sem_inc(passed, 1)

        def phase_end(eng, who, l, k):
            settle(eng)
            eng.drain().then_inc(ENDS[who], 1)
            for name, s in ENDS.items():
                if name != who:
                    eng.wait_ge(s, l * BARS + k + 1)
            settle(eng)

        class Steps:

            def __init__(self, eng, s, per):
                self.eng, self.s, self.per, self.n = eng, s, per, 0

            def start(self, it):
                self.base, self.n = it * self.per, 0

            def mark(self, ins):
                ins.then_inc(self.s, 1)
                self.n += 1

            def sync(self):
                self.eng.wait_ge(self.s, self.base + self.n)

            def step(self, ins):
                self.mark(ins)
                self.sync()

            def end(self):
                assert self.n == self.per, (self.n, self.per)

        def col1(c):
            return col[:, c:c + 1]

        def dyn(ap, start, size):
            return ap[:, bass.ds(start, size)]

        block = ctx.enter_context(nc.Block())

        @block.sync
        def _(sp):
            sp.dma_start(con[:], A["consts"]).then_inc(con_in, 16)
            sp.dma_start(csf[0:KT, 0, :], A["c_ctx"].rearrange("(k p) -> k p", p=P)).then_inc(c_in, 16)
            sp.dma_start(csf[KT:2 * KT, 0, :], A["c"][0].rearrange("(k p) -> k p", p=P)).then_inc(c_in, 16)
            sp.dma_start(x[:, 0, :], A["x_prompt"][0]).then_inc(x_in, 16)
            sp.dma_start(x[:, 1, :], A["x_sample"][0]).then_inc(x_in, 16)

            def load(q, c, src, width=NW):
                sp.wait_ge(lo_ready, q * 4 + (c + 1))
                sp.dma_start(rawW[:, c % LEAD, :, 0:width], src).then_inc(raw_full[c % LEAD], 16)

            def load_tile(q, w, n0, width=NW):
                for c in range(CPT):
                    load(q, c, w[:, 2 * c:2 * c + 2, bass.ds(n0, width)], width)

            def load_down(q, w, j):
                for c in range(2 * OUT_TILES):
                    n0 = (c // 2) * NW
                    load(q, c, w[:, bass.ds(j * 4 + 2 * (c % 2), 2), n0:n0 + NW])

            with sp.Fori(0, LAYERS) as l:
                wada, win, wout, wgate, wup, wdown = (A[n][l].rearrange("(k p) n -> p k n", p=P) for n in (
                    "w_ada", "w_in", "w_out", "w_gate", "w_up", "w_down"))
                ql = l * Q_LAYER
                with sp.Fori(0, 8) as i:
                    load_tile(ql + Q_ADA01 + i * 2, wada, i * NW)
                with sp.Fori(0, WIN_TILES - 1) as i:
                    load_tile(ql + Q_WIN + i * 2, win, i * NW)
                load_tile(ql + Q_WIN + (WIN_TILES - 1) * 2, win, (WIN_TILES - 1) * NW, WIN_LAST)
                with sp.Fori(0, 4) as i:
                    load_tile(ql + Q_ADA2 + i * 2, wada, i * NW + 2 * D)
                with sp.Fori(0, OUT_TILES) as i:
                    load_tile(ql + Q_WOUT + i * 2, wout, i * NW)
                with sp.Fori(0, 8) as i:
                    load_tile(ql + Q_ADA34 + i * 2, wada, i * NW + 3 * D)
                load_tile(ql + Q_FFN, wgate, 0)
                load_tile(ql + Q_FFN + 2, wup, 0)
                with sp.Fori(1, FF_TILES) as j:
                    qb = ql + (Q_FFN - 2) + j * 6
                    load_tile(qb, wgate, j * NW)
                    load_tile(qb + 2, wup, j * NW)
                    load_down(qb + 4, wdown, j - 1)
                load_down(ql + (Q_FFN + 4 + 6 * (FF_TILES - 1)), wdown, FF_TILES - 1)
                with sp.Fori(0, 4) as i:
                    load_tile(ql + Q_ADA5 + i * 2, wada, i * NW + 5 * D)

        @block.scalar
        def _(act):
            def hi(q, c0, c1, width=NW):
                for c in range(c0, c1):
                    s = c % LEAD
                    act.wait_ge(raw_full[s], q * 16 + 16 * (c // LEAD + 1))
                    act.wait_ge(chunk_used, q * 4 + (c + 1))
                    act.activation(hiW[:, s, :, 0:width], rawW[:, s, :, 0:width], ACT.Copy).then_inc(hi_ready, 1)

            def tile_done(q):
                act.wait_ge(chunk_used, q * 4 + (CPT + LEAD))

            def evac(q, out, b, width=NW):
                tile_done(q)
                act.activation(out, bank[b][:, 0:width], ACT.Copy).then_inc(evac_s, 1)

            def ada(q, last=False):
                hi(q, 4, 12)
                hi(q + 2, 4, 8 if last else 12)

            def norm(it, xs, tf):
                for g in range(2):
                    act.activation(xs[:, g], x[:, g], ACT.Square, accum_out=ss[:, g:g + 1]).then_inc(sq_in, 1)
                for b in range(8):
                    g, kq = b // 4, b % 4
                    act.wait_ge(nt_f, it * 8 + (b + 1))
                    act.activation(actH[:, 4 * kq:4 * kq + 4, g * P:(g + 1) * P],
                                   tf[:, b % 2].rearrange("p (k t) -> p k t", k=4), ACT.Copy).then_inc(nt_hi, 1)

            def residual(it, part, ng, l):
                act.dma_start(bB[:], A["b_ada"][l][part * D:(part + 1) * D].partition_broadcast(P)).then_inc(gb_in, 16)
                act.dma_start(nB[:], A["norm_g"][l][ng].partition_broadcast(P)).then_inc(gb_in, 16)
                for g in range(2):
                    act.activation(xs2[:, g], o[:, g], ACT.Square, accum_out=ss[:, g:g + 1]).then_inc(sq_in, 1)

            def parameters(l):
                act.wait_ge(prm_zero, l + 1)
                put = lambda dst, src: act.dma_start(dst, src).then_inc(par_rows, 16)
                row = lambda ap: ap.rearrange("(r c) -> r c", c=P)
                mu = A["rwkv_mu"][l]
                put(prm[0:12, 0, :], row(mu[0:12 * P]))
                put(prm[12:13, 0, 0:64], mu[12 * P:12 * P + 64].unsqueeze(0))
                put(prm[13:14, 0, 0:GATE_RANK], mu[12 * P + 64:D_RWIN].unsqueeze(0))
                for c, name in ((COL_W0, "rwkv_w0"), (COL_A0, "rwkv_a0")):
                    put(prm[c:c + 8, 0, :], A[name][l].rearrange("d (r c) -> (d r) c", c=P))
                for c, name in ((COL_KK, "rwkv_k_k"), (COL_KA, "rwkv_k_a"), (COL_LG, "rwkv_ln_g"), (COL_LB, "rwkv_ln_b")):
                    put(prm[c:c + 4, 0, :], row(A[name][l]))
                put(prm[COL_RK:COL_RK + 4, 0, :], A["rwkv_r_k"][l].rearrange("(r a) b -> r (a b)", a=2))
                put(prm[COL_CV:COL_CV + 12, 0, :], A["conv_w"][l].rearrange("w (r c) -> (w r) c", c=P))
                put(prm[0:64, 1, :], A["norm_g"][l].rearrange("n (r c) -> (n r) c", c=P))
                put(prm[0:96, 2, :], row(A["b_ada"][l]))
                put = lambda dst, src: act.dma_start(dst, src).then_inc(par_tabs, 16)
                put(wla[0:32], A["rwkv_w_up"][l].rearrange("d r n -> r d n"))
                put(wla[32:64], A["rwkv_a_up"][l].rearrange("d r n -> r d n"))
                put(wg[:], A["rwkv_g_up"][l])
                put(ctxk[:], A["cache_k"][0][l])
                put(ctxv[:], A["cache_v"][0][l])
                put(qkw[:, 0], A["q_norm"][l].partition_broadcast(P))
                put(qkw[:, 1], A["k_norm"][l].partition_broadcast(P))
                for d in range(2):
                    put(s0all[:, d], A["state_rwkv"][0][l][d].rearrange("(f h) i j -> (h i) f j", h=2))

            def conv(l):
                for g in range(2):
                    act.wait_ge(cv_T, l * 6 + (g + 1))
                    act.activation(chT[:, g], bank[4 + g][:].rearrange("p (f t) -> p f t", f=4), ACT.Copy).then_inc(cv_ch, 1)
                for g in range(2):
                    act.wait_ge(cv_out, l * 2 + (g + 1))
                    act.activation(actH[:, 8:12, g * P:(g + 1) * P], cv[:, :, g], ACT.Copy).then_inc(cv_hi, 1)

            def attention(l, g):
                it = l * 2 + g
                nk = P if g == 0 else 2 * P
                if g == 0:
                    act.wait_ge(at_qk, it + 1)
                    act.dma_start(O["new_k"][0][l], qk[:, NH:NH + NKV]).then_inc(kv_out, 16)
                    act.dma_start(O["new_v"][0][l], proj[:, 0, D_QK:D_ATT].rearrange("p (h d) -> p h d", h=NKV)).then_inc(kv_out, 16)
                act.wait_ge(at_T, it * 3 + 1)
                act.activation(qT[:, 0:4], bank[0][:].rearrange("p (h t) -> p h t", h=4), ACT.Copy).then_inc(at_ca, 1)
                act.wait_ge(at_T, it * 3 + 3)
                act.activation(kT[:, :, 0:nk].rearrange("p v (s t) -> p s v t", t=P),
                               bank[2][:, 0:2 * nk].rearrange("p (s v t) -> p s v t", v=2, t=P), ACT.Copy).then_inc(at_ca, 1)
                act.wait_ge(at_mx, it + 1)
                for h in range(NH):
                    e = act.activation(pr[:, h, 0:nk], bank[3 + h // 2][:, (h % 2) * 256:(h % 2) * 256 + nk], ACT.Exp,
                                       bias=qst[:, 40 + h:41 + h], scale=SCALE, accum_out=qst[:, 48 + h:49 + h])
                e.then_inc(at_P, 1)
                act.wait_ge(at_PT, it * 2 + 1)
                for k in range(nk // P):
                    e = act.activation(pT[:, k, 0:4], bank[2 * k][:].rearrange("p (h t) -> p h t", h=4), ACT.Copy)
                e.then_inc(at_pa, 1)
                for v in range(NKV):
                    act.wait_ge(at_O, it * 2 + (v + 1))
                    act.activation(actH[:, 4 * v:4 * v + 4, g * P:(g + 1) * P],
                                   bank[4 + v][:].rearrange("p (h t) -> p h t", h=4), ACT.Copy).then_inc(at_hi, 1)
                if g == 0:
                    act.wait_ge(kv_out, l * 32 + 32)

            def turn_u(l):
                for b in range(3):
                    act.wait_ge(u_T, l * 7 + (b + 1))
                    act.activation(uT[:, 4 * b:4 * b + 4, 0, 1:129], bank[b][:].rearrange("p (f t) -> p f t", f=4), ACT.Copy)
                act.wait_ge(u_T, l * 7 + 7)
                act.activation(uT[0:64, 12, :, 1:129], bank[6][0:64, 0:256].rearrange("p (g t) -> p g t", g=2), ACT.Copy)
                act.activation(uT[0:GATE_RANK, 13, :, 1:129],
                               bank[6][0:GATE_RANK, 256:512].rearrange("p (g t) -> p g t", g=2), ACT.Copy)

            def rwkv(l):
                act.wait_ge(lr_mix, l + 1)
                act.activation(xwa[0:32], xwa[0:32], ACT.Tanh)
                act.activation(xg[:], xg[:], ACT.Sigmoid).then_inc(lr_act, 1)
                with act.Fori(0, FT) as f:
                    it = act.snap(l * FT + f)
                    act.activation(wS[:], wla[:, :, bass.ds(f * P, P)], ACT.Copy)
                    act.activation(gS[:], wg[:, bass.ds(f * P, P)], ACT.Copy).then_inc(rw_stage, 1)
                    act.wait_ge(rw_lr, it + 1)
                    for d in range(2):
                        e = act.activation(sig[d], bank[1][:, d * 256:(d + 1) * 256], ACT.Sigmoid,
                                           bias=dyn(col, f + (COL_W0 + 4 * d), 1))
                    e.then_inc(rw_sig, 1)
                    for d in range(2):
                        e = act.activation(aa[d], bank[2][:, d * 256:(d + 1) * 256], ACT.Sigmoid,
                                           bias=dyn(col, f + (COL_A0 + 4 * d), 1))
                    e.then_inc(rw_aa, 1)
                    act.wait_ge(rw_VS, it + 1)
                    act.activation(Vt[:], bank[3][:, 0:256].rearrange("p (g c) -> p g c", g=2), ACT.Copy).then_inc(rw_Vt, 1)
                    act.wait_ge(rw_c, it + 1)
                    for d in range(2):
                        for g in range(2):
                            n = 2 * d + g
                            act.activation(E1[:, d, g], cs[:, d, g], ACT.Exp, bias=amid[:, n:n + 1], scale=-ALPHA)
                            e = act.activation(E2[:, d, g], cs[:, d, g], ACT.Exp, bias=amid[:, 4 + n:5 + n], scale=ALPHA)
                    e.then_inc(rw_E, 1)
                    act.wait_ge(rw_R, it + 1)
                    act.activation(Rs[:], bank[6][:].rearrange("p (n i) -> p n i", n=4), ACT.Copy).then_inc(rw_Rs, 1)
                    act.wait_ge(rw_bgT, it + 1)
                    act.activation(bgt, bank[7][:].rearrange("p (d n j) -> p d n j", d=2, n=2), ACT.Copy).then_inc(rw_bgs, 1)
                    with act.Fori(0, LEVELS) as v:
                        n = it * (2 * LEVELS) + v * 2
                        for d in range(2):
                            act.wait_ge(lv_U, n + (d + 3))
                            act.activation(U[:, d], bank[d][:].rearrange("p (s t) -> p s t", s=4), ACT.Copy).then_inc(lv_Us, 1)
                    act.wait_ge(rw_SA, it + 1)
                    act.activation(SA[:], bank[6][:].rearrange("p (n i) -> p n i", n=4), ACT.Copy, scale=-1.0).then_inc(rw_SAs, 1)
                    act.wait_ge(rw_ST, it + 1)
                    act.activation(STs[:], bank[1][:, 0:2 * RH].rearrange("p (d j) -> p d j", d=2), ACT.Copy).then_inc(ST_v, 1)
                    act.wait_ge(ST_v, it + 1)
                    for d in range(2):
                        act.dma_start(O["new_rwkv"][0][l][d].rearrange("(f h) i j -> f (h i) j", h=2)[f],
                                      STs[:, d]).then_inc(st_out, 16)
                    act.wait_ge(rw_yc, it + 1)
                    act.activation(yy[1], yy[0], ACT.Square).then_inc(rw_y2, 1)
                    act.wait_ge(rw_o, it + 1)
                    act.activation(actH[:, bass.ds(f + 12, 1), :], yy[0].unsqueeze(1), ACT.Copy).then_inc(rw_hi, 1)
                    act.wait_ge(st_out, it * 32 + 32)
                    settle(act)

            def ffn(l):
                ql = l * Q_LAYER

                def gate(q, j):
                    tile_done(q)
                    for g in range(2):
                        act.activation(sg[:, g], bank[g][:], ACT.Sigmoid).then_inc(ff_s, 1)

                def turned(j):
                    for g in range(2):
                        act.wait_ge(ff_T, l * (2 * FF_TILES) + j * 2 + (g + 1))
                        act.activation(ffH[:, :, g * P:(g + 1) * P],
                                       bank[4 + g][:].rearrange("p (k t) -> p k t", k=4), ACT.Copy).then_inc(ff_hi, 1)

                hi(ql + Q_FFN, 4, 12)
                gate(ql + Q_FFN, 0)
                hi(ql + Q_FFN + 2, 4, 12)
                with act.Fori(1, FF_TILES) as j:
                    qb = act.snap(ql + (Q_FFN - 2) + j * 6)
                    hi(qb, 4, 12)
                    act.wait_ge(ff_u, l * FF_TILES + j)
                    gate(qb, j)
                    turned(j - 1)
                    hi(qb + 2, 4, 12)
                    hi(qb + 4, 4, 12)
                turned(FF_TILES - 1)
                hi(ql + (Q_FFN + 4 + 6 * (FF_TILES - 1)), 4, 12)

            act.wait_ge(c_in, 32)
            act.activation(csf[0:2 * KT, 1], csf[0:2 * KT, 0], ACT.Sigmoid).then_inc(cs_done, 1)
            act.wait_ge(cs_done, 4)
            csv = csR[:, 0:4 * KT].rearrange("p (k c) -> p c k", c=4)
            act.activation(csv[:, 0:2], bank[0][:, 0:2 * KT].rearrange("p (g k) -> p g k", g=2), ACT.Copy).then_inc(cs_done, 1)
            act.wait_ge(x_in, 32)
            with act.Fori(0, LAYERS) as l:
                ql = act.snap(l * Q_LAYER)
                parameters(l)
                hi(ql, 0, 4)
                phase_end(act, "act", l, 0)
                with act.Fori(0, 4) as i:
                    ada(act.snap(ql + Q_ADA01 + i * 4))
                phase_end(act, "act", l, 1)
                norm(l * 2, xs1, tf1)
                phase_end(act, "act", l, 2)
                with act.Fori(0, 4) as i:
                    q = act.snap(ql + Q_WIN + i * 4)
                    hi(q, 4, 12)
                    evac(q, proj[:, 1, bass.ds(i * (2 * NW), NW)], 1)
                    hi(q + 2, 4, 12)
                    evac(q + 2, proj[:, 1, bass.ds(i * (2 * NW) + NW, NW)], 3)
                q = ql + Q_WIN + 16
                hi(q, 4, 8)
                hi(q, 8, 12, WIN_LAST)
                evac(q, proj[:, 1, 8 * NW:9 * NW], 1)
                hi(q + 2, 4, 8, WIN_LAST)
                hi(q + 2, 8, 12)
                evac(q + 2, proj[:, 1, 9 * NW:D_IN], 3, WIN_LAST)
                phase_end(act, "act", l, 3)
                act.wait_ge(par_tabs, l * (9 * 16) + 9 * 16)
                conv(l)
                phase_end(act, "act", l, 4)
                for g in range(2):
                    attention(l, g)
                    phase_end(act, "act", l, 5 + g)
                turn_u(l)
                phase_end(act, "act", l, 7)
                rwkv(l)
                phase_end(act, "act", l, 8)
                for i in range(2):
                    ada(ql + Q_ADA2 + i * 4)
                for i in range(2):
                    q = ql + Q_WOUT + i * 4
                    hi(q, 4, 12)
                    evac(q, o[:, 1, 2 * i * NW:(2 * i + 1) * NW], 1)
                    hi(q + 2, 4, 12)
                    evac(q + 2, o[:, 1, (2 * i + 1) * NW:(2 * i + 2) * NW], 3)
                phase_end(act, "act", l, 9)
                residual(l * 2, 2, 1, l)
                phase_end(act, "act", l, 10)
                with act.Fori(0, 4) as i:
                    ada(act.snap(ql + Q_ADA34 + i * 4))
                phase_end(act, "act", l, 11)
                norm(l * 2 + 1, xs2, tf2)
                phase_end(act, "act", l, 12)
                ffn(l)
                phase_end(act, "act", l, 13)
                ada(ql + Q_ADA5)
                ada(ql + Q_ADA5 + 4, last=True)
                phase_end(act, "act", l, 14)
                residual(l * 2 + 1, 5, 3, l)
                phase_end(act, "act", l, 15)
            act.dma_start(O["y_prompt"][0], x[:, 0, :]).then_inc(y_out, 16)
            act.dma_start(O["y_sample"][0], x[:, 1, :]).then_inc(y_out, 16)
            act.wait_ge(y_out, 32)

        @block.gpsimd
        def _(pool):
            def power(out, in_):
                n = in_.shape[1]
                return pool.tensor_tensor(out, in_, mhalf.to_broadcast([P, n]), ALU.pow)

            def stats(n, l):
                pool.wait_ge(ms_in, l * 4 + (n + 1))
                power(rstd, ms).then_inc(rs_in, 1)

            pool.wait_ge(con_in, 16)
            pool.memset(s0bd[:], 0.0).then_inc(rw_s0, 1)
            with pool.Fori(0, LAYERS) as l:
                phase_end(pool, "pool", l, 0)
                phase_end(pool, "pool", l, 1)
                stats(0, l)
                phase_end(pool, "pool", l, 2)
                phase_end(pool, "pool", l, 3)
                pool.memset(mT[:], 0.0).then_inc(cv_z, 1)
                phase_end(pool, "pool", l, 4)
                for g in range(2):
                    pool.wait_ge(at_ms, l * 2 + (g + 1))
                    power(qst[:, 20:30], qst[:, 10:20]).then_inc(at_rs, 1)
                    phase_end(pool, "pool", l, 5 + g)
                pool.memset(uT[:, :, :, 0:1], 0.0)
                pool.memset(uT[:, :, :, 129:130], 0.0)
                phase_end(pool, "pool", l, 7)
                pool.memset(AE[:], 0.0)
                pool.memset(BF[:], 0.0).then_inc(ab_z, 1)
                pool.wait_ge(ab_z, l + 1)
                settle(pool)
                with pool.Fori(0, FT) as f:
                    it = pool.snap(l * FT + f)
                    for h in range(2):
                        hs = slice(RH * h, RH * h + RH)
                        e = pool.tensor_copy(s0bd[hs, :, hs], s0all[hs, :, bass.ds(f, 1), :].rearrange("p d f j -> p (d f) j"))
                    e.then_inc(rw_s0, 1)
                    pool.wait_ge(rw_s0, it + 2)
                    pool.wait_ge(rw_ns, it + 1)
                    power(ksq[:].rearrange("p g t -> p (g t)"), nrm[:].rearrange("p g t -> p (g t)")).then_inc(rw_rs, 1)
                    for d in range(2):
                        e = pool.tensor_copy(X[:, d].rearrange("p s (a t) -> p (s a) t", a=2),
                                             ident.unsqueeze(1).broadcast_to([P, 8, P]))
                    e.then_inc(lv_X0, 1)
                    with pool.Fori(0, LEVELS) as v:
                        n = pool.snap(it * (2 * LEVELS) + v * 2)
                        for d in range(2):
                            pool.wait_ge(rw_m, it * 2 + (d + 1))
                            pool.wait_ge(lv_U, n + (d + 1))
                            settle(pool)
                            pool.tensor_tensor(CT[:, d], AE[:, d, :, 0:P],
                                               con[:, bass.ds(v * P + C_LV, P)].unsqueeze(1).broadcast_to([P, 4, P]),
                                               ALU.mult).then_inc(lv_C, 1)
                    pool.wait_ge(rw_vs, it + 1)
                    power(yy[3], yy[2]).then_inc(rw_vr, 1)
                    pool.wait_ge(rw_vr, it + 1)
                    settle(pool)
                phase_end(pool, "pool", l, 8)
                phase_end(pool, "pool", l, 9)
                stats(1, l)
                phase_end(pool, "pool", l, 10)
                pool.memset(o[:], 0.0)
                phase_end(pool, "pool", l, 11)
                stats(2, l)
                phase_end(pool, "pool", l, 12)
                phase_end(pool, "pool", l, 13)
                phase_end(pool, "pool", l, 14)
                stats(3, l)
                phase_end(pool, "pool", l, 15)

        @block.tensor
        def _(pe):
            def mm(out, a, b, start=True, stop=True):
                return pe.matmul(out, a, b, start=start, stop=stop, skip_group_check=True)

            def gemm(q, banks, H=actH, L=actL, width=NW):
                for c in range(CPT):
                    s = c % LEAD
                    pe.wait_ge(lo_ready, q * 4 + (c + 1 + LEAD))
                    for n in range(2):
                        k = 2 * c + n
                        for g in range(2):
                            out = bank[banks[g]][:, 0:width]
                            Hk, Lk = H[:, k, g * P:(g + 1) * P], L[:, k, g * P:(g + 1) * P]
                            mm(out, Hk, hiW[:, s, n, 0:width], k == 0, False)
                            mm(out, Hk, loW[:, s, n, 0:width], False, False)
                            e = mm(out, Lk, hiW[:, s, n, 0:width], False, k == KT - 1)
                    e.then_inc(chunk_used, 1)

            def free(l, t):
                pe.wait_ge(evac_v, l * (WIN_TILES + OUT_TILES) + (t + 1))
                pe.wait_ge(evac_s, l * (WIN_TILES + OUT_TILES) + (t + 1))

            def ada(q, a, rows, turned):
                for t in range(2):
                    pe.wait_ge(rows_out, a + (t + 1))
                    for c in range(CPT):
                        s = c % LEAD
                        pe.wait_ge(lo_ready, q * 4 + (8 * t + c + 1 + LEAD))
                        for n in range(2):
                            k = 2 * c + n
                            mm(bank[2 * t][:], csR[:, 4 * k:4 * k + P], hiW[:, s, n], k == 0, False)
                            e = mm(bank[2 * t][:], csR[:, 4 * k:4 * k + P], loW[:, s, n], False, k == KT - 1)
                        e.then_inc(chunk_used, 1)
                for t in range(2):
                    pe.wait_ge(rows_out, a + (t + 3))
                    if turned:
                        for j in range(4):
                            e = mm(bank[4 + t][:, 2 * j:2 * j + 2], rows[0:4, t, j * P:(j + 1) * P], con[0:4, C_SELT:C_SELT + 2])
                    else:
                        for g in range(2):
                            e = mm(bank[4 + 2 * t + g][:], con[0:4, C_SELB + g * P:C_SELB + (g + 1) * P], rows[0:4, t])
                    e.then_inc(ada_post, 1)

            def norm(it, xs):
                for b in range(8):
                    g, kq = b // 4, b % 4
                    if kq == 0:
                        pe.wait_ge(xs_in, it * 2 + (g + 1))
                    if g == 1:
                        pe.wait_ge(nt_f, it * 8 + (b - 3))
                    for j in range(4):
                        e = pe.transpose(bank[4 + kq][:, j * P:(j + 1) * P], xs[:, g, (4 * kq + j) * P:(4 * kq + j + 1) * P], ident)
                    e.then_inc(nt_T, 1)

            def conv(l):
                for which, b0 in ((2, 4), (1, 2), (0, 0)):
                    for g in range(2):
                        for f in range(4):
                            c = OFF_CONV + which * D_CONV + f * P
                            e = pe.transpose(bank[b0 + g][:, f * P:(f + 1) * P], proj[:, g, c:c + P], ident)
                        e.then_inc(cv_T, 1)

            def attention(l, g):
                it = l * 2 + g
                pe.wait_ge(at_qk, it + 1)
                for b in range(2):
                    for j in range(4):
                        e = pe.transpose(bank[b][:, j * P:(j + 1) * P], qk[:, 4 * b + j], ident)
                    e.then_inc(at_T, 1)
                for v in range(NKV):
                    e = pe.transpose(bank[2][:, v * P:(v + 1) * P], qk[:, NH + v], ident)
                if g == 1:
                    for v in range(NKV):
                        e = pe.transpose(bank[2][:, (2 + v) * P:(3 + v) * P], ctxk[:, v], ident)
                e.then_inc(at_T, 1)
                nk = P if g == 0 else 2 * P
                pe.wait_ge(at_ca, it * 2 + 2)
                for h in range(NH):
                    if h == 4:
                        pe.wait_ge(at_cv, it + 1)
                    e = mm(bank[3 + h // 2][:, (h % 2) * 256:(h % 2) * 256 + nk], qT[:, h], kT[:, h // 4, 0:nk])
                    if h % 2:
                        e.then_inc(at_S, 1)
                pe.wait_ge(at_Pn, it + 1)
                for b in range(2):
                    for k in range(nk // P):
                        for j in range(4):
                            e = pe.transpose(bank[2 * k + b][:, j * P:(j + 1) * P], pr[:, 4 * b + j, k * P:(k + 1) * P], ident)
                    e.then_inc(at_PT, 1)
                for v in range(NKV):
                    pe.wait_ge((at_pa, at_pv)[v], it + 1)
                    for k in range(nk // P):
                        V = proj[:, g, D_QK + v * HD:D_QK + (v + 1) * HD] if k == 0 else ctxv[:, v]
                        e = mm(bank[4 + v][:], V, pT[:, k, 4 * v:4 * v + 4].rearrange("p h t -> p (h t)"), k == 0, k == nk // P - 1)
                    e.then_inc(at_O, 1)

            def turn_u(l):
                for g in range(2):
                    for b in range(3):
                        for j in range(4):
                            c = OFF_RW + (4 * b + j) * P
                            e = pe.transpose(bank[3 * g + b][:, j * P:(j + 1) * P], proj[:, g, c:c + P], ident)
                        e.then_inc(u_T, 1)
                for g in range(2):
                    c = OFF_RW + 12 * P
                    pe.transpose(bank[6][0:64, g * P:(g + 1) * P], proj[:, g, c:c + 64], ident)
                    e = pe.transpose(bank[6][0:GATE_RANK, 256 + g * P:256 + (g + 1) * P], proj[:, g, c + 64:c + 160], ident)
                e.then_inc(u_T, 1)

            def rwkv(l):
                pe.wait_ge(lr_act, l + 1)
                settle(pe)
                with pe.Fori(0, FT) as f:
                    it = pe.snap(l * FT + f)
                    flat = lambda t: t.rearrange("p g t -> p (g t)")
                    pe.wait_ge(rw_sq, it + 1)
                    mm(bank[0][:, 0:256], blk1, flat(ksq[:])).then_inc(rw_nrm, 1)
                    pe.wait_ge(rw_stage, it + 1)
                    for d in range(2):
                        mm(bank[1][:, d * 256:(d + 1) * 256], wS[0:32, d], flat(xwa[0:32]))
                        mm(bank[2][:, d * 256:(d + 1) * 256], wS[32:64, d], flat(xwa[32:64]))
                    pe.wait_ge(rw_ns, it + 1)
                    mm(bank[0][:, 256:512], gS[:], flat(xg[:])).then_inc(rw_lr, 1)
                    pe.wait_ge(rw_v, it + 1)
                    pe.wait_ge(rw_s0, it + 2)
                    for g in range(2):
                        pe.transpose(bank[3][:, g * P:(g + 1) * P], rkv[:, 2, g], ident)
                    for d in range(2):
                        e = pe.transpose(bank[3][:, 256 + d * P:256 + (d + 1) * P], s0bd[:, d], ident)
                    e.then_inc(rw_VS, 1)
                    for d in range(2):
                        pe.wait_ge(rw_kr, it * 2 + (d + 1))
                        if d == 1:
                            pe.wait_ge(rw_m, it * 2 + 1)
                        for m, left in ((4, be), (6, ga)):
                            for g in range(2):
                                for h in range(2):
                                    hs = slice(RH * h, RH * h + RH)
                                    e = mm(bank[m + h][:, g * 256:(g + 1) * 256], left[hs, d, g],
                                           KR[hs, d, g].rearrange("p a t -> p (a t)"))
                        e.then_inc(rw_A, 1)
                    pe.wait_ge(rw_bo, it + 1)
                    pe.wait_ge(rw_Vt, it + 1)
                    mm(bank[3][:, 0:256], blk1, flat(nrm[:])).then_inc(rw_bon, 1)
                    pe.wait_ge(rw_m, it * 2 + 2)
                    pe.wait_ge(rw_S0s, it + 1)
                    for d in range(2):
                        for g in range(2):
                            n = 2 * d + g
                            if g == 1:
                                mm(bank[6][:, n * P:(n + 1) * P], KR[:, d, g, 0], S0s[:, d], True, False)
                            for h in range(2):
                                e = mm(bank[6][:, n * P + h * RH:n * P + (h + 1) * RH], BF[:, d, 2 * g + h, 0:P],
                                       Vt[:, g, h * RH:(h + 1) * RH], g == 0, True)
                    e.then_inc(rw_R, 1)
                    pe.wait_ge(rw_bg, it + 1)
                    for d in range(2):
                        for n in range(2):
                            e = pe.transpose(bank[7][:, (2 * d + n) * P:(2 * d + n + 1) * P], bg0[:, d, n], ident)
                    e.then_inc(rw_bgT, 1)
                    pe.wait_ge(lv_X0, it + 1)
                    pe.wait_ge(rw_bv, it + 1)
                    settle(pe)
                    with pe.Fori(0, LEVELS) as v:
                        n = pe.snap(it * (2 * LEVELS) + v * 2)
                        for d in range(2):
                            pe.wait_ge(lv_C, n + (d + 1))
                            pe.wait_ge(lv_X, n + (d + 1))
                            for s in range(4):
                                e = mm(bank[d][:, s * P:(s + 1) * P], CT[:, d, s], X[:, d, s, 0:P])
                            e.then_inc(lv_U, 1)
                        for d in range(2):
                            pe.wait_ge(lv_Us, n + (d + 1))
                            for s in range(4):
                                out = bank[2 + 2 * d + s // 2]
                                c = (s % 2) * 256
                                mm(out[:, c:c + P], X[:, d, s, P:256], U[:, d, s])
                                e = mm(out[:, c + P:c + 256], U[:, d, s], X[:, d, s, P:256])
                            e.then_inc(lv_XM, 1)
                    pe.wait_ge(lv_X, it * (2 * LEVELS) + (2 * LEVELS + 2))
                    pe.wait_ge(rw_Rs, it + 1)
                    for d in range(2):
                        for g in range(2):
                            for h in range(2):
                                n = 2 * d + g
                                e = mm(bank[6][:, n * P + h * RH:n * P + (h + 1) * RH], X[:, d, 2 * g + h, P:256],
                                       Rs[:, n, h * RH:(h + 1) * RH])
                    e.then_inc(rw_SA, 1)
                    pe.wait_ge(rw_SAs, it + 1)
                    for g in range(2):
                        if g == 1:
                            mm(bank[0][:, P:256], S0s[:, 0], KR[:, 0, 1, 1], True, False)
                            mm(bank[0][:, P:256], S0s[:, 1], KR[:, 1, 1, 1], False, False)
                        for h in range(2):
                            hs = slice(RH * h, RH * h + RH)
                            for d in range(2):
                                mm(bank[0][hs, g * P:(g + 1) * P], SA[:, 2 * d + g, hs], AE[:, d, 2 * g + h, P:256],
                                   g == 0 and d == 0, False)
                                e = mm(bank[0][hs, g * P:(g + 1) * P], Vt[:, g, hs], BF[:, d, 2 * g + h, P:256], False, d == 1)
                    e.then_inc(rw_Y, 1)
                    pe.wait_ge(rw_bgs, it + 1)
                    for d in range(2):
                        for h in range(2):
                            hs = slice(RH * h, RH * h + RH)
                            mm(bank[1][hs, d * RH:(d + 1) * RH], SA[:, 2 * d, hs], bgt[:, d, 0, hs], True, False)
                            e = mm(bank[1][hs, d * RH:(d + 1) * RH], Vt[:, 0, hs], bgt[:, d, 1, hs], False, True)
                    e.then_inc(rw_ST, 1)
                    pe.wait_ge(rw_y, it + 1)
                    mm(bank[2][:, 0:256], blkm, yy[0]).then_inc(rw_mean, 1)
                    pe.wait_ge(rw_y2, it + 1)
                    mm(bank[2][:, 256:512], blkm, yy[1]).then_inc(rw_var, 1)

            def ffn(l):
                ql = l * Q_LAYER

                def turn(j):
                    pe.wait_ge(ff_u, l * FF_TILES + (j + 1))
                    for g in range(2):
                        for k in range(4):
                            e = pe.transpose(bank[4 + g][:, k * P:(k + 1) * P], ff[:, g, k * P:(k + 1) * P], ident)
                        e.then_inc(ff_T, 1)

                def down(q, j):
                    pe.wait_ge(ff_hi, l * (2 * FF_TILES) + (j * 2 + 2))
                    pe.wait_ge(ff_lo, l * (2 * FF_TILES) + (j * 2 + 2))
                    for n in range(4):
                        if n >= 2:
                            pe.wait_ge(dn_out, l * (4 * FF_TILES) + (j * 4 + (n + 3)))
                        for c in range(2):
                            i = 2 * n + c
                            s = i % LEAD
                            pe.wait_ge(lo_ready, q * 4 + (i + 1 + LEAD))
                            for m in range(2):
                                k = 2 * c + m
                                for g in range(2):
                                    out = bank[(6 if n % 2 == 0 else 4) + g][:]
                                    Hk, Lk = ffH[:, k, g * P:(g + 1) * P], ffL[:, k, g * P:(g + 1) * P]
                                    mm(out, Hk, hiW[:, s, m], k == 0, False)
                                    mm(out, Hk, loW[:, s, m], False, False)
                                    e = mm(out, Lk, hiW[:, s, m], False, k == 3)
                            e.then_inc(chunk_used, 1)

                gemm(ql + Q_FFN, (0, 1))
                gemm(ql + Q_FFN + 2, (2, 3))
                with pe.Fori(1, FF_TILES) as j:
                    qb = pe.snap(ql + (Q_FFN - 2) + j * 6)
                    pe.wait_ge(ff_g, l * FF_TILES + j)
                    gemm(qb, (0, 1))
                    pe.wait_ge(dn_out, l * (4 * FF_TILES) + j * 4)
                    turn(j - 1)
                    gemm(qb + 2, (2, 3))
                    down(qb + 4, j - 1)
                pe.wait_ge(dn_out, l * (4 * FF_TILES) + 4 * FF_TILES)
                turn(FF_TILES - 1)
                down(ql + (Q_FFN + 4 + 6 * (FF_TILES - 1)), FF_TILES - 1)

            pe.sem_inc(chunk_used, LEAD)
            pe.sem_inc(lv_U, 2)
            pe.wait_ge(con_in, 16)
            pe.wait_ge(cs_done, 3)
            pe.transpose(bank[0][:, 0:2 * KT], csf[0:2 * KT, 2], con[0:2 * KT, C_ID:C_ID + 2 * KT]).then_inc(cs_done, 1)
            pe.wait_ge(cs_done, 6)
            with pe.Fori(0, LAYERS) as l:
                ql = pe.snap(l * Q_LAYER)
                ada_l = pe.snap(l * 24)
                pe.wait_ge(par_rows, l * (13 * 16) + 13 * 16)
                settle(pe)
                for r, n, c in ((0, ROWS_P, 0), (1, 64, COL_NG), (2, 96, COL_B)):
                    e = pe.transpose(bank[0][:, c:c + n], prm[0:n, r], con[0:n, C_ID:C_ID + n])
                e.then_inc(cols_T, 1)
                phase_end(pe, "pe", l, 0)
                with pe.Fori(0, 4) as i:
                    ada(pe.snap(ql + Q_ADA01 + i * 4), pe.snap(ada_l + i * 2), rows1, True)
                phase_end(pe, "pe", l, 1)
                norm(l * 2, xs1)
                phase_end(pe, "pe", l, 2)
                with pe.Fori(0, 4) as i:
                    q = pe.snap(ql + Q_WIN + i * 4)
                    free(l, i * 2)
                    gemm(q, (0, 1))
                    free(l, i * 2 + 1)
                    gemm(q + 2, (2, 3))
                free(l, 8)
                gemm(ql + Q_WIN + 16, (0, 1))
                free(l, 9)
                gemm(ql + Q_WIN + 18, (2, 3), width=WIN_LAST)
                phase_end(pe, "pe", l, 3)
                conv(l)
                phase_end(pe, "pe", l, 4)
                for g in range(2):
                    attention(l, g)
                    phase_end(pe, "pe", l, 5 + g)
                turn_u(l)
                phase_end(pe, "pe", l, 7)
                rwkv(l)
                phase_end(pe, "pe", l, 8)
                for i in range(2):
                    ada(ql + Q_ADA2 + i * 4, ada_l + (8 + 2 * i), rows2, False)
                for i in range(4):
                    free(l, WIN_TILES + i)
                    gemm(ql + Q_WOUT + i * 2, (0, 1) if i % 2 == 0 else (2, 3))
                phase_end(pe, "pe", l, 9)
                phase_end(pe, "pe", l, 10)
                with pe.Fori(0, 4) as i:
                    ada(pe.snap(ql + Q_ADA34 + i * 4), pe.snap(ada_l + 12 + i * 2), rows2, True)
                phase_end(pe, "pe", l, 11)
                norm(l * 2 + 1, xs2)
                phase_end(pe, "pe", l, 12)
                ffn(l)
                phase_end(pe, "pe", l, 13)
                for i in range(2):
                    ada(ql + Q_ADA5 + i * 4, ada_l + (20 + 2 * i), rows2, False)
                phase_end(pe, "pe", l, 14)
                phase_end(pe, "pe", l, 15)

        @block.vector
        def _(dve):
            S = Steps(dve, vsteps, VSTEPS)
            R = Steps(dve, fsteps, FSTEPS)
            TT, TS, STT = dve.tensor_tensor, dve.tensor_scalar, dve.scalar_tensor_tensor

            def lo(q, c0, c1, width=NW):
                for c in range(c0, c1):
                    s = c % LEAD
                    dve.wait_ge(hi_ready, q * 4 + (c + 1))
                    TT(loW[:, s, :, 0:width], rawW[:, s, :, 0:width], hiW[:, s, :, 0:width].bitcast(F32),
                       ALU.subtract).then_inc(lo_ready, 1)

            def tile_done(q):
                dve.wait_ge(chunk_used, q * 4 + (CPT + LEAD))

            def evac(q, out, b, width=NW):
                tile_done(q)
                dve.tensor_copy(out, bank[b][:, 0:width]).then_inc(evac_v, 1)

            def ada(q, a, rows, out, last=False):
                for t in range(2):
                    qt = q + 2 * t
                    lo(qt, 4, 8 if last and t == 1 else 12)
                    tile_done(qt)
                    dve.tensor_copy(rows[0:4, t], bank[2 * t][0:4, :]).then_inc(rows_out, 1)
                for t in range(2):
                    dve.wait_ge(ada_post, a + (t + 1))
                    out(t)

            def norm(it, xs, tf, sh, part, ng):
                bias = lambda p: col[:, COL_B + p * KT:COL_B + (p + 1) * KT].unsqueeze(2).broadcast_to([P, KT, 2])
                S.step(TT(modT[:, sh], modT[:, sh], bias(part), ALU.add))
                S.step(TT(modT[:, sh + 1], modT[:, sh + 1], bias(part + 1), ALU.add))
                S.step(TS(modT[:, sh + 1], modT[:, sh + 1], 1.0, None, ALU.add))
                S.step(TT(modT[:, sh + 1], modT[:, sh + 1],
                          col[:, COL_NG + ng * KT:COL_NG + (ng + 1) * KT].unsqueeze(2).broadcast_to([P, KT, 2]), ALU.mult))
                dve.wait_ge(sq_in, it * 4 + 2)
                TS(ms, ss, 1.0 / D, EPS, ALU.mult, ALU.add).then_inc(ms_in, 1)
                dve.wait_ge(rs_in, it * 2 + 1)
                for g in range(2):
                    TS(xs[:, g], x[:, g], rstd[:, g:g + 1], None, ALU.mult).then_inc(xs_in, 1)

                def low(b):
                    g, kq = b // 4, b % 4
                    dve.wait_ge(nt_hi, it * 8 + (b + 1))
                    a = slice(4 * kq, 4 * kq + 4), slice(g * P, (g + 1) * P)
                    S.mark(TT(actL[:, a[0], a[1]], tf[:, b % 2].rearrange("p (k t) -> p k t", k=4),
                              actH[:, a[0], a[1]].bitcast(F32), ALU.subtract))

                for b in range(8):
                    g, kq = b // 4, b % 4
                    dve.wait_ge(nt_T, it * 8 + (b + 1))
                    if b >= 2:
                        S.sync()
                    for j in range(4):
                        k = 4 * kq + j
                        e = TS(tf[:, b % 2, j * P:(j + 1) * P], bank[4 + kq][:, j * P:(j + 1) * P],
                               modT[:, sh + 1, k, g:g + 1], modT[:, sh, k, g:g + 1], ALU.mult, ALU.add)
                    e.then_inc(nt_f, 1)
                    if b:
                        low(b - 1)
                low(7)

            def residual(it, l):
                dve.wait_ge(gb_in, it * 32 + 32)
                for g in range(2):
                    S.mark(TT(G[:, g], G[:, g], bB[:], ALU.add))
                S.sync()
                for g in range(2):
                    S.mark(TT(G[:, g], G[:, g], nB[:], ALU.mult))
                dve.wait_ge(sq_in, it * 4 + 4)
                TS(ms, ss, 1.0 / D, EPS, ALU.mult, ALU.add).then_inc(ms_in, 1)
                dve.wait_ge(rs_in, it * 2 + 2)
                S.sync()
                for g in range(2):
                    S.mark(STT(xs2[:, g], o[:, g], rstd[:, g:g + 1], G[:, g], ALU.mult, ALU.mult))
                S.sync()
                for g in range(2):
                    S.mark(TT(x[:, g], x[:, g], xs2[:, g], ALU.add))
                S.sync()

            def conv(l):
                dve.wait_ge(cv_z, l + 1)
                for g in range(2):
                    dve.wait_ge(cv_T, l * 6 + (3 + g))
                    dve.wait_ge(cv_ch, l * 2 + (g + 1))
                    S.mark(TT(mT[:, :, g, 1:129], bank[2 + g][:].rearrange("p (f t) -> p f t", f=4), chT[:, g], ALU.mult))
                S.sync()
                for f in range(4):
                    S.mark(TS(cv[:, f], mT[:, f, :, 0:128], col1(COL_CV + f), None, ALU.mult))
                for w in (1, 2):
                    S.sync()
                    for f in range(4):
                        S.mark(STT(cv[:, f], mT[:, f, :, w:w + 128], col1(COL_CV + 4 * w + f), cv[:, f], ALU.mult, ALU.add))
                S.sync()
                for g in range(2):
                    dve.wait_ge(cv_T, l * 6 + (5 + g))
                    TT(cv[:, :, g], cv[:, :, g], bank[g][:].rearrange("p (f t) -> p f t", f=4), ALU.mult).then_inc(cv_out, 1)
                for g in range(2):
                    dve.wait_ge(cv_hi, l * 2 + (g + 1))
                    TT(actL[:, 8:12, g * P:(g + 1) * P], cv[:, :, g], actH[:, 8:12, g * P:(g + 1) * P].bitcast(F32), ALU.subtract)

            def attention(l, g):
                it = l * 2 + g
                nk = P if g == 0 else 2 * P
                raw = proj[:, g, 0:D_QK].rearrange("p (h d) -> p h d", d=HD)
                per_head = lambda v, n, w: v.unsqueeze(2).broadcast_to([P, n, w])
                S.step(TT(qc, raw, raw, ALU.mult))
                S.step(dve.tensor_reduce(qst[:, 0:10], qc, AX, ALU.add))
                TS(qst[:, 10:20], qst[:, 0:10], 1.0 / HD, EPS, ALU.mult, ALU.add).then_inc(at_ms, 1)
                dve.wait_ge(at_rs, it + 1)
                S.step(TT(qk[:], raw, per_head(qst[:, 20:30], 10, HD), ALU.mult))
                S.mark(TT(qk[:, 0:NH], qk[:, 0:NH], qkw[:, 0:1].broadcast_to([P, NH, HD]), ALU.mult))
                e = TT(qk[:, NH:], qk[:, NH:], qkw[:, 1:2].broadcast_to([P, NKV, HD]), ALU.mult)
                if g == 1:
                    S.step(e)
                    table = lambda c: con[:, c:c + HD].unsqueeze(1).broadcast_to([P, 10, HD])
                    S.mark(TT(qc, qk[:], table(C_COS), ALU.mult))
                    for b in range(2):
                        part = lambda t, b: t.rearrange("p h (a b c) -> p h a b c", a=2, b=2)[:, :, :, b]
                        sin = con[:, C_SIN:C_SIN + HD].rearrange("p (a b c) -> p a b c", a=2, b=2)[:, :, b]
                        S.mark(TT(part(qs, b), part(qk[:], 1 - b), sin.unsqueeze(1).broadcast_to([P, 10, 2, 32]), ALU.mult))
                    S.sync()
                    e = TT(qk[:], qc, qs, ALU.add)
                e.then_inc(at_qk, 1)
                dve.wait_ge(at_T, it * 3 + 2)
                dve.tensor_copy(qT[:, 4:8], bank[1][:].rearrange("p (h t) -> p h t", h=4)).then_inc(at_cv, 1)
                for b in range(4):
                    dve.wait_ge(at_S, it * 4 + (b + 1))
                    S.mark(dve.tensor_reduce(qst[:, 30 + 2 * b:32 + 2 * b],
                                             bank[3 + b][:].rearrange("p (h s) -> p h s", h=2)[:, :, 0:nk], AX, ALU.max))
                S.sync()
                TS(qst[:, 40:48], qst[:, 30:38], -SCALE, None, ALU.mult).then_inc(at_mx, 1)
                dve.wait_ge(at_P, it + 1)
                S.step(dve.reciprocal(qst[:, 56:64], qst[:, 48:56]))
                TT(pr[:, :, 0:nk], pr[:, :, 0:nk], per_head(qst[:, 56:64], NH, nk), ALU.mult).then_inc(at_Pn, 1)
                dve.wait_ge(at_PT, it * 2 + 2)
                for k in range(nk // P):
                    e = dve.tensor_copy(pT[:, k, 4:8], bank[2 * k + 1][:].rearrange("p (h t) -> p h t", h=4))
                e.then_inc(at_pv, 1)
                for v in range(NKV):
                    dve.wait_ge(at_hi, it * 2 + (v + 1))
                    a = slice(4 * v, 4 * v + 4), slice(g * P, (g + 1) * P)
                    TT(actL[:, a[0], a[1]], bank[4 + v][:].rearrange("p (h t) -> p h t", h=4),
                       actH[:, a[0], a[1]].bitcast(F32), ALU.subtract)

            def turn_u(l):
                for b in range(3):
                    dve.wait_ge(u_T, l * 7 + (b + 4))
                    dve.tensor_copy(uT[:, 4 * b:4 * b + 4, 1, 1:129], bank[3 + b][:].rearrange("p (f t) -> p f t", f=4))

            def rwkv(l):
                lr = ((12, 64, xwa), (13, GATE_RANK, xg))
                for n, (k, w, out) in enumerate(lr):
                    S.mark(TT(tmp3[0:w, n], uT[0:w, k, :, 0:128], uT[0:w, k, :, 2:130], ALU.add))
                S.sync()
                for n, (k, w, out) in enumerate(lr):
                    S.mark(TS(tmp3[0:w, n], tmp3[0:w, n], muh[0:w, k:k + 1], None, ALU.mult))
                S.sync()
                for n, (k, w, out) in enumerate(lr):
                    e = STT(out[:], uT[0:w, k, :, 1:129], omu[0:w, k:k + 1], tmp3[0:w, n], ALU.mult, ALU.add)
                e.then_inc(lr_mix, 1)
                dve.wait_ge(lr_mix, l + 1)
                settle(dve)
                flat = lambda t: t.rearrange("p g t -> p (g t)")
                with dve.Fori(0, FT) as f:
                    it = dve.snap(l * FT + f)
                    R.start(it)
                    for n in range(3):
                        a = uT[:, bass.ds(f + 4 * n, 1)]
                        R.mark(TT(tmp3[:, n:n + 1], a[:, :, :, 0:128], a[:, :, :, 2:130], ALU.add))
                    R.sync()
                    for n in range(3):
                        R.mark(TS(tmp3[:, n], tmp3[:, n], dyn(muh, f + 4 * n, 1), None, ALU.mult))
                    R.sync()
                    for n in range(3):
                        a = uT[:, bass.ds(f + 4 * n, 1), :, 1:129].rearrange("p f g t -> p (f g) t")
                        e = STT(rkv[:, n], a, dyn(omu, f + 4 * n, 1), tmp3[:, n], ALU.mult, ALU.add)
                    e.then_inc(rw_v, 1)
                    dve.wait_ge(rw_v, it + 1)
                    r_, k_, v_ = (rkv[:, n] for n in range(3))
                    R.step(TS(kk[:], k_, dyn(col, f + COL_KK, 1), None, ALU.mult))
                    TT(ksq[:], kk[:], kk[:], ALU.mult).then_inc(rw_sq, 1)
                    dve.wait_ge(rw_nrm, it + 1)
                    TS(flat(nrm[:]), bank[0][:, 0:256], KK_EPS, None, ALU.add).then_inc(rw_ns, 1)
                    dve.wait_ge(rw_rs, it + 1)
                    R.step(TT(kk[:], kk[:], ksq[:], ALU.mult))
                    dve.wait_ge(rw_lr, it + 1)
                    R.mark(dve.tensor_copy(flat(gT[:]), bank[0][:, 256:512]))
                    R.mark(dve.memset(cs[:, :, :, 0:1], 0.0))
                    dve.wait_ge(rw_sig, it + 1)
                    for d in range(2):
                        for g in range(2):
                            R.mark(dve.tensor_tensor_scan(cs[:, d, g, 1:129], ones, sig[d][:, g * P:(g + 1) * P], 0.0,
                                                          ALU.mult, ALU.add))
                    R.sync()
                    mid = cs[:, :, :, 64:65].rearrange("p d g o -> p d (g o)")
                    TS(amid[:, 0:4].rearrange("p (d g) -> p d g", d=2), mid, ALPHA, None, ALU.mult)
                    TS(amid[:, 4:8].rearrange("p (d g) -> p d g", d=2), mid, -ALPHA, None, ALU.mult).then_inc(rw_c, 1)
                    dve.wait_ge(rw_aa, it + 1)
                    for d in range(2):
                        R.mark(TS(flat(kd[:, d]), aa[d], dyn(col, f + COL_KA, 1), dyn(oka, f, 1), ALU.mult, ALU.add))
                        R.mark(TT(flat(be[:, d]), flat(kk[:]), aa[d], ALU.mult))
                    R.sync()
                    for d in range(2):
                        R.mark(TT(kd[:, d], kd[:, d], k_, ALU.mult))
                    R.sync()
                    dve.wait_ge(rw_E, it + 1)
                    for d in range(2):
                        Ei, Ex, Ev = ((E1[:, d, :, 1:129], E1[:, d, :, 0:128], E2[:, d, :, 1:129]) if d == 0 else
                                      (E2[:, d, :, 0:128], E2[:, d, :, 1:129], E1[:, d, :, 0:128]))
                        TT(KR[:, d, :, 0], kk[:], Ex, ALU.mult)
                        TT(KR[:, d, :, 1], r_, Ei, ALU.mult)
                        TT(ga[:, d], kd[:, d], Ev, ALU.mult)
                        TT(be[:, d], be[:, d], Ev, ALU.mult).then_inc(rw_kr, 1)
                    for d in range(2):
                        dve.wait_ge(rw_A, it * 2 + (d + 1))
                        if d == 0:
                            dve.wait_ge(ab_z, l + 1)
                        mask = con[:, C_TRI + d * 256:C_TRI + (d + 1) * 256].bitcast(U32).unsqueeze(1).broadcast_to([P, 2, 256])
                        settle(dve)
                        for m, dst in ((4, AE), (6, BF)):
                            for h in range(2):
                                e = dve.copy_predicated(dst[:, d, h:4:2], mask,
                                                        bank[m + h][:].rearrange("p (g t) -> p g t", g=2))
                        e.then_inc(rw_m, 1)
                    dve.wait_ge(rw_Vt, it + 1)
                    for d, mid in ((0, E2[:, 0, 1, 0:1]), (1, E1[:, 1, 1, 128:129])):
                        e = TS(S0s[:, d], bank[3][:, 256 + d * P:256 + (d + 1) * P], mid, None, ALU.mult)
                    e.then_inc(rw_S0s, 1)
                    R.mark(TT(nrm[:], kd[:, 0], kd[:, 1], ALU.add))
                    R.step(TS(ksq[:], r_, dyn(col, f + COL_RK, 1), None, ALU.mult))
                    TT(nrm[:], nrm[:], ksq[:], ALU.mult).then_inc(rw_bo, 1)
                    for d, end in ((0, E1[:, 0, 0, 128:129]), (1, E2[:, 1, 0, 0:1])):
                        TS(bg0[:, d, 0], be[:, d, 0], end, None, ALU.mult)
                        e = TS(bg0[:, d, 1], ga[:, d, 0], end, None, ALU.mult)
                    e.then_inc(rw_bg, 1)
                    dve.wait_ge(rw_bon, it + 1)
                    TT(flat(nrm[:]), bank[3][:, 0:256], flat(v_), ALU.mult).then_inc(rw_bv, 1)
                    dve.wait_ge(lv_X0, it + 1)
                    settle(dve)
                    with dve.Fori(0, LEVELS) as v:
                        n = dve.snap(it * (2 * LEVELS) + v * 2)
                        for d in range(2):
                            dve.wait_ge(lv_XM, n + (d + 1))
                            for b in range(2):
                                e = TT(X[:, d, 2 * b:2 * b + 2], X[:, d, 2 * b:2 * b + 2],
                                       bank[2 + 2 * d + b][:].rearrange("p (s t) -> p s t", s=2), ALU.add)
                            e.then_inc(lv_X, 1)
                    y0, y1, y2, y3 = yy
                    dve.wait_ge(rw_Y, it + 1)
                    dve.tensor_copy(y0, bank[0][:, 0:256]).then_inc(rw_y, 1)
                    dve.wait_ge(rw_y, it + 1)
                    dve.wait_ge(rw_mean, it + 1)
                    TT(y0, y0, bank[2][:, 0:256], ALU.subtract).then_inc(rw_yc, 1)
                    dve.wait_ge(rw_yc, it + 1)
                    dve.wait_ge(rw_var, it + 1)
                    TS(y2, bank[2][:, 256:512], GN_EPS, None, ALU.add).then_inc(rw_vs, 1)
                    dve.wait_ge(rw_vr, it + 1)
                    R.step(TT(y0, y0, y3, ALU.mult))
                    R.step(TS(y0, y0, dyn(col, f + COL_LG, 1), dyn(col, f + COL_LB, 1), ALU.mult, ALU.add))
                    R.step(TT(y0, y0, flat(nrm[:]), ALU.add))
                    TT(y0, y0, flat(gT[:]), ALU.mult).then_inc(rw_o, 1)
                    dve.wait_ge(rw_hi, it + 1)
                    TT(actL[:, bass.ds(f + 12, 1)], y0.unsqueeze(1), actH[:, bass.ds(f + 12, 1)].bitcast(F32), ALU.subtract)
                    R.end()

            def ffn(l):
                ql = l * Q_LAYER

                def gate(q):
                    tile_done(q)
                    for g in range(2):
                        dve.wait_ge(ff_s, gate.base + (g + 1))
                        e = TT(sg[:, g], sg[:, g], bank[g][:], ALU.mult)
                    e.then_inc(ff_g, 1)

                def up(q, j):
                    tile_done(q)
                    dve.wait_ge(ff_g, l * FF_TILES + (j + 1))
                    for g in range(2):
                        e = TT(ff[:, g], sg[:, g], bank[2 + g][:], ALU.mult)
                    e.then_inc(ff_u, 1)

                def turned(j):
                    for g in range(2):
                        dve.wait_ge(ff_hi, l * (2 * FF_TILES) + (j * 2 + (g + 1)))
                        TT(ffL[:, :, g * P:(g + 1) * P], bank[4 + g][:].rearrange("p (k t) -> p k t", k=4),
                           ffH[:, :, g * P:(g + 1) * P].bitcast(F32), ALU.subtract).then_inc(ff_lo, 1)

                def down(q, n):
                    dve.wait_ge(chunk_used, q * 4 + (2 * n + 2 + LEAD))
                    for g in range(2):
                        out = o[:, g, n * NW:(n + 1) * NW]
                        e = TT(out, out, bank[(6 if n % 2 == 0 else 4) + g][:], ALU.add)
                    e.then_inc(dn_out, 1)

                def down_all(q):
                    for n in range(4):
                        lo(q, 4 + 2 * n, 6 + 2 * n)
                        down(q, n)

                lo(ql + Q_FFN, 4, 12)
                gate.base = l * (2 * FF_TILES)
                gate(ql + Q_FFN)
                lo(ql + Q_FFN + 2, 4, 12)
                up(ql + Q_FFN + 2, 0)
                with dve.Fori(1, FF_TILES) as j:
                    qb = dve.snap(ql + (Q_FFN - 2) + j * 6)
                    lo(qb, 4, 12)
                    gate.base = l * (2 * FF_TILES) + j * 2
                    gate(qb)
                    turned(j - 1)
                    lo(qb + 2, 4, 12)
                    up(qb + 2, j)
                    dve.wait_ge(dn_out, l * (4 * FF_TILES) + (j * 4))
                    down_all(qb + 4)
                turned(FF_TILES - 1)
                dve.wait_ge(dn_out, l * (4 * FF_TILES) + 4 * FF_TILES)
                down_all(ql + (Q_FFN + 4 + 6 * (FF_TILES - 1)))

            dve.sem_inc(lo_ready, LEAD)
            dve.sem_inc(rows_out, 2)
            dve.sem_inc(evac_v, 2)
            dve.sem_inc(evac_s, 2)
            dve.sem_inc(lv_X, 2)
            dve.sem_inc(dn_out, 4)
            csv = csR[:, 0:4 * KT].rearrange("p (k c) -> p c k", c=4)
            dve.memset(csR[:].bitcast(F32), 0.0).then_inc(cs_done, 1)
            dve.wait_ge(cs_done, 2)
            TT(csf[0:2 * KT, 2], csf[0:2 * KT, 0], csf[0:2 * KT, 1], ALU.mult).then_inc(cs_done, 1)
            dve.wait_ge(cs_done, 5)
            TT(csv[:, 2:4], bank[0][:, 0:2 * KT].rearrange("p (g k) -> p g k", g=2), csv[:, 0:2].bitcast(F32),
               ALU.subtract).then_inc(cs_done, 1)
            with dve.Fori(0, LAYERS) as l:
                ql = dve.snap(l * Q_LAYER)
                ada_l = dve.snap(l * 24)
                S.start(l)
                dve.memset(prm[:, 0], 0.0).then_inc(prm_zero, 1)
                lo(ql, 0, 4)
                dve.wait_ge(cols_T, l + 1)
                S.step(dve.tensor_copy(col[:], bank[0][:, 0:COLS]))
                S.mark(TS(muh[:], col[:, COL_MU:COL_MU + 14], 0.5, None, ALU.mult))
                S.mark(TS(omu[:], col[:, COL_MU:COL_MU + 14], -1.0, 1.0, ALU.mult, ALU.add))
                S.step(TS(oka[:], col[:, COL_KA:COL_KA + 4], -1.0, 1.0, ALU.mult, ALU.add))
                phase_end(dve, "dve", l, 0)
                mod = modT[:].rearrange("p m k g -> p (m k g)")

                def ada_turned(q, a, rows, base, i):
                    def out(t):
                        dve.tensor_copy(mod[:, bass.ds(i * 16 + (base + 8 * t), 8)], bank[4 + t][:, 0:8])
                    ada(q, a, rows, out)

                def ada_spread(q, a, i, last=False):
                    def out(t):
                        for g in range(2):
                            n = (2 * i + t) * NW
                            dve.tensor_copy(G[:, g, n:n + NW], bank[4 + 2 * t + g][:])
                    ada(q, a, rows2, out, last)

                with dve.Fori(0, 4) as i:
                    ada_turned(dve.snap(ql + Q_ADA01 + i * 4), dve.snap(ada_l + i * 2), rows1, 0, i)
                phase_end(dve, "dve", l, 1)
                norm(l * 2, xs1, tf1, 0, 0, 0)
                phase_end(dve, "dve", l, 2)
                with dve.Fori(0, 4) as i:
                    q = dve.snap(ql + Q_WIN + i * 4)
                    lo(q, 4, 12)
                    evac(q, proj[:, 0, bass.ds(i * (2 * NW), NW)], 0)
                    lo(q + 2, 4, 12)
                    evac(q + 2, proj[:, 0, bass.ds(i * (2 * NW) + NW, NW)], 2)
                q = ql + Q_WIN + 16
                lo(q, 4, 8)
                lo(q, 8, 12, WIN_LAST)
                evac(q, proj[:, 0, 8 * NW:9 * NW], 0)
                lo(q + 2, 4, 8, WIN_LAST)
                lo(q + 2, 8, 12)
                evac(q + 2, proj[:, 0, 9 * NW:D_IN], 2, WIN_LAST)
                phase_end(dve, "dve", l, 3)
                dve.wait_ge(par_tabs, l * (9 * 16) + 9 * 16)
                conv(l)
                phase_end(dve, "dve", l, 4)
                for g in range(2):
                    attention(l, g)
                    phase_end(dve, "dve", l, 5 + g)
                turn_u(l)
                phase_end(dve, "dve", l, 7)
                rwkv(l)
                phase_end(dve, "dve", l, 8)
                for i in range(2):
                    ada_spread(ql + Q_ADA2 + i * 4, ada_l + (8 + 2 * i), i)
                for i in range(2):
                    q = ql + Q_WOUT + i * 4
                    lo(q, 4, 12)
                    evac(q, o[:, 0, 2 * i * NW:(2 * i + 1) * NW], 0)
                    lo(q + 2, 4, 12)
                    evac(q + 2, o[:, 0, (2 * i + 1) * NW:(2 * i + 2) * NW], 2)
                phase_end(dve, "dve", l, 9)
                residual(l * 2, l)
                phase_end(dve, "dve", l, 10)
                with dve.Fori(0, 4) as i:
                    ada_turned(dve.snap(ql + Q_ADA34 + i * 4), dve.snap(ada_l + 12 + i * 2), rows2, 64, i)
                phase_end(dve, "dve", l, 11)
                norm(l * 2 + 1, xs2, tf2, 2, 3, 2)
                phase_end(dve, "dve", l, 12)
                ffn(l)
                phase_end(dve, "dve", l, 13)
                ada_spread(ql + Q_ADA5, ada_l + 20, 0)
                ada_spread(ql + Q_ADA5 + 4, ada_l + 22, 1, last=True)
                phase_end(dve, "dve", l, 14)
                residual(l * 2 + 1, l)
                S.end()
                phase_end(dve, "dve", l, 15)


INS = ["x_prompt", "x_sample", "cache_k", "cache_v", "state_rwkv", "c", "c_ctx", "w_ada", "b_ada", "norm_g", "w_in",
       "q_norm", "k_norm", "conv_w", "rwkv_mu", "rwkv_w0", "rwkv_w_up", "rwkv_a0", "rwkv_a_up", "rwkv_g_up",
       "rwkv_k_k", "rwkv_k_a", "rwkv_r_k", "rwkv_ln_g", "rwkv_ln_b", "w_out", "w_gate", "w_up", "w_down"]
OUTS = {"y_prompt": (1, P, D), "y_sample": (1, P, D), "new_k": (1, LAYERS, P, NKV, HD), "new_v": (1, LAYERS, P, NKV, HD),
        "new_rwkv": (1, LAYERS, 2, RW_HEADS, RH, RH)}


def build(nc, shapes):
    A = {n: nc.dram_tensor(f"in_{n}", shapes[n], F32, kind="ExternalInput").ap() for n in INS + ["consts"]}
    O = {n: nc.dram_tensor(f"out_{n}", s, F32, kind="ExternalOutput").ap() for n, s in OUTS.items()}
    hybrid_trunk(nc, A, O)


def kernel(**inputs):
    import concourse.bacc as bacc
    from concourse.bass_utils import run_bass_kernel_spmd

    nc = bacc.Bacc("TRN2", target_bir_lowering=False, num_devices=1)
    arrays = {n: np.ascontiguousarray(inputs[n]) for n in INS}
    arrays["consts"] = constants()
    build(nc, {n: a.shape for n, a in arrays.items()})
    r = run_bass_kernel_spmd(nc, [{f"in_{n}": a for n, a in arrays.items()}], core_ids=[0])
    return tuple(r.results[0][f"out_{n}"] for n in OUTS)
```

```python
from contextlib import ExitStack

import numpy as np
import concourse.bass as bass
from concourse import mybir

F32 = mybir.dt.float32
F32R = mybir.dt.float32r
U32 = mybir.dt.uint32
ALU = mybir.AluOpType
ACT = mybir.ActivationFunctionType
AX = mybir.AxisListType.X

P = 128
LAYERS = 2
D = 2048
KT = D // P
NW = 512
HD = 128
NH, NKV = 8, 2
D_QK = (NH + NKV) * HD
D_ATT = D_QK + NKV * HD
D_CONV = 512
D_RW = 512
RW_HEADS, RH = 8, 64
FT = D_RW // P
OFF_CONV = D_ATT
OFF_RW = OFF_CONV + 3 * D_CONV
RANK, GATE_RANK = 32, 96
D_RWIN = 3 * D_RW + 2 * RANK + GATE_RANK
D_IN = OFF_RW + D_RWIN
D_FF = 5632
EPS, GN_EPS, KK_EPS = 1e-6, 64e-5, 1e-12
ALPHA = float(np.exp(-0.5))
SCALE = float(HD) ** -0.5
HALF = P // 2
LEVELS = 6

CPT = KT // 2
LEAD = 4
WIN_TILES = -(-D_IN // NW)
WIN_LAST = D_IN - (WIN_TILES - 1) * NW
OUT_TILES = D // NW
FF_TILES = D_FF // NW
Q_ADA01 = 0
Q_WIN = Q_ADA01 + 8 * 2
Q_ADA2 = Q_WIN + WIN_TILES * 2
Q_WOUT = Q_ADA2 + 16 * 2
Q_FFN = Q_WOUT + OUT_TILES * 2
Q_LAYER = Q_FFN + FF_TILES * 6

C_ID, C_BO, C_BM, C_LV = 0, 128, 256, 384
C_I2 = C_LV + LEVELS * HALF
C_TRI = C_I2 + HALF
C_COS = C_TRI + 2 * 256
C_SIN = C_COS + P
C_SELT = C_SIN + P
C_ONE = C_SELT + 2
C_HALF = C_ONE + P
C_ALL = C_HALF + 1

COL_MU, COL_W0, COL_A0, COL_KK, COL_KA, COL_RK, COL_LG, COL_LB, COL_CV = 0, 14, 22, 30, 34, 38, 42, 46, 50
ROWS_P = 62
COL_NG = ROWS_P
COL_B = COL_NG + 4 * KT
COLS = COL_B + 6 * KT
VSTEPS, FSTEPS = 90, 27
BARS = 14


def constants():
    c = np.zeros((P, C_ALL), np.float32)
    i = np.arange(P)
    same = lambda b: (i[:, None] // b == i[None, :] // b).astype(np.float32)
    c[:, C_ID:C_ID + P] = np.eye(P)
    c[:, C_BO:C_BO + P] = same(RH)
    c[:, C_BM:C_BM + P] = same(RH) / RH
    for n in range(LEVELS):
        both = same(1 << n) - same(2 << n)
        c[:, C_LV + n * HALF:C_LV + (n + 1) * HALF] = np.concatenate([both[:HALF, :HALF]] * 2)
    c[:, C_I2:C_I2 + HALF] = np.concatenate([np.eye(HALF)] * 2)
    s, t = i[:, None], i[None, :]
    for d, (excl, incl) in enumerate([(s < t, s <= t), (s > t, s >= t)]):
        c[:, C_TRI + d * 256:C_TRI + d * 256 + P] = excl
        c[:, C_TRI + d * 256 + P:C_TRI + (d + 1) * 256] = incl
    half = HD // 2
    inv = (np.float32(1.0) / (np.float32(10000.0) ** (np.arange(0, half, 2, dtype=np.float32) / np.float32(half))))
    ar = (i // 64).astype(np.float32)[:, None] * inv
    ac = (i % 64).astype(np.float32)[:, None] * inv
    ang = np.concatenate([ar, ar, ac, ac], axis=-1).astype(np.float32)
    sign = np.repeat(np.array([-1, 1, -1, 1], np.float32), 32)
    c[:, C_COS:C_COS + P] = np.cos(ang)
    c[:, C_SIN:C_SIN + P] = np.sin(ang) * sign
    for row in range(4):
        c[row, C_SELT + row % 2] = 1
    c[:, C_ONE:C_ONE + P] = 1
    c[:, C_HALF] = -0.5
    return c


def hybrid_trunk(nc, A, O):
    ctx = ExitStack()
    with ctx:
        def sb(name, shape, dt=F32, at=ctx):
            return at.enter_context(nc.sbuf_tensor(name, shape, dt))

        def sem(name):
            return ctx.enter_context(nc.semaphore(name))

        x = sb("x", [P, 2, D])
        actH = sb("actH", [P, KT, 256], F32R)
        actL = sb("actL", [P, KT, 256], F32R)
        rawW = sb("rawW", [P, LEAD, 2, NW])
        hiW = sb("hiW", [P, LEAD, 2, NW], F32R)
        loW = sb("loW", [P, LEAD, 2, NW], F32R)
        con = sb("con", [P, C_ALL])
        col = sb("col", [P, COLS])
        muh = sb("muh", [P, 14])
        omu = sb("omu", [P, 14])
        oka = sb("oka", [P, 4])
        wla = sb("wla", [64, 2, D_RW])
        wg = sb("wg", [GATE_RANK, D_RW])
        ctxk = sb("ctxk", [P, NKV, HD])
        ctxv = sb("ctxv", [P, NKV, HD])
        qkw = sb("qkw", [P, 2, HD])
        s0all = sb("s0all", [P, 2, FT, RH])
        s0bd = sb("s0bd", [P, 2, P])
        csR = sb("csR", [P, 192], F32R)
        modT = sb("modT", [P, 6, KT, 2])
        st = sb("st", [P, 8])
        ss, ms, rstd = st[:, 0:2], st[:, 2:4], st[:, 4:6]
        bank = [ctx.enter_context(nc.psum_tensor(f"bank{i}", [P, NW], F32)) for i in range(8)]

        ident = con[:, C_ID:C_ID + P]
        blk1 = con[:, C_BO:C_BO + P]
        blkm = con[:, C_BM:C_BM + P]
        ones = con[:, C_ONE:C_ONE + P]
        mhalf = con[:, C_HALF:C_HALF + 1]

        with ExitStack() as ph:
            prm = sb("prm", [P, 3, P], F32, ph)
            rows1 = sb("rows1", [4, 2, NW], F32, ph)
            xs1 = sb("xs1", [P, 2, D], F32, ph)
            tf1 = sb("tf1", [P, 2, NW], F32, ph)
            csf = sb("csf", [P, 3, P], F32, ph)
        with ExitStack() as ph:
            uT = sb("uT", [P, 14, 2, 130], F32, ph)
            with ExitStack() as ph2:
                proj = sb("proj", [P, 2, D_IN], F32, ph2)
                with ExitStack() as ph3:
                    chT = sb("chT", [P, 2, 4, P], F32, ph3)
                    mT = sb("mT", [P, 4, 2, 130], F32, ph3)
                    cv = sb("cv", [P, 4, 2, P], F32, ph3)
                with ExitStack() as ph3:
                    qk = sb("qk", [P, 10, HD], F32, ph3)
                    scr = sb("scr", [P, 20, HD], F32, ph3)
                    qst = sb("qst", [P, 64], F32, ph3)
                    qT = sb("qT", [P, NH, P], F32, ph3)
                    kT = sb("kT", [P, NKV, 256], F32, ph3)
                    pr = sb("pr", [P, NH, 256], F32, ph3)
            with ExitStack() as ph2:
                tmp3 = sb("tmp3", [P, 3, 2, P], F32, ph2)
                rkv = sb("rkv", [P, 3, 2, P], F32, ph2)
                kk = sb("kk", [P, 2, P], F32, ph2)
                ksq = sb("ksq", [P, 2, P], F32, ph2)
                nrm = sb("nrm", [P, 2, P], F32, ph2)
                xwa = sb("xwa", [64, 2, P], F32, ph2)
                xg = sb("xg", [GATE_RANK, 2, P], F32, ph2)
                wS = sb("wS", [64, 2, P], F32, ph2)
                gS = sb("gS", [GATE_RANK, P], F32, ph2)
                sa_ = sb("sigaa", [P, 4, 2, P], F32, ph2)
                gT = sb("gT", [P, 2, P], F32, ph2)
                cs = sb("cs", [P, 2, 2, 129], F32, ph2)
                E1 = sb("E1", [P, 2, 2, 129], F32, ph2)
                E2 = sb("E2", [P, 2, 2, 129], F32, ph2)
                amid = sb("amid", [P, 8], F32, ph2)
                kd = sb("kd", [P, 2, 2, P], F32, ph2)
                KR = sb("KR", [P, 2, 2, 2, P], F32, ph2)
                be = sb("be", [P, 2, 2, P], F32, ph2)
                ga = sb("ga", [P, 2, 2, P], F32, ph2)
                AE = sb("AE", [P, 2, 4, 256], F32, ph2)
                BF = sb("BF", [P, 2, 4, 256], F32, ph2)
                AC = sb("AC", [P, 2, 4, HALF], F32, ph2)
                X = sb("X", [P, 2, 4, P], F32, ph2)
                CT = sb("CT", [P, 2, 4, HALF], F32, ph2)
                U = sb("U", [P, 2, 4, HALF], F32, ph2)
                rows3 = sb("rows3", [4, NW], F32, ph2)
                Rs = sb("Rs", [P, 4, P], F32, ph2)
                SA = sb("SA", [P, 4, P], F32, ph2)
                Vt = sb("Vt", [P, 2, P], F32, ph2)
                S0s = sb("S0s", [P, 2, P], F32, ph2)
                STs = sb("STs", [P, 2, RH], F32, ph2)
        with ExitStack() as ph:
            o = sb("o", [P, 2, D], F32, ph)
            with ExitStack() as ph2:
                xs2 = sb("xs2", [P, 2, D], F32, ph2)
                tf2 = sb("tf2", [P, 2, NW], F32, ph2)
            with ExitStack() as ph2:
                sg = sb("sg", [P, 2, NW], F32, ph2)
                ff = sb("ff", [P, 2, NW], F32, ph2)
                ffH = sb("ffH", [P, 4, 256], F32R, ph2)
                ffL = sb("ffL", [P, 4, 256], F32R, ph2)
        qc, qs = scr[:, 0:10], scr[:, 10:20]
        pT = scr[:, 0:16].rearrange("p (k h) t -> p k h t", k=2)
        sig = [sa_[:, d].rearrange("p g t -> p (g t)") for d in range(2)]
        aa = [sa_[:, 2 + d].rearrange("p g t -> p (g t)") for d in range(2)]
        yy = sig + aa
        bg0 = kd
        bgt = cs[:].rearrange("p d g t -> p (d g t)")[:, 0:4 * P].rearrange("p (d n j) -> p d n j", d=2, n=2)

        passed = sem("passed")
        con_in, c_in, x_in = sem("con_in"), sem("c_in"), sem("x_in")
        cs_done = sem("cs_done")
        raw_full = [sem(f"raw_full{n}") for n in range(LEAD)]
        hi_ready, lo_ready = sem("hi_ready"), sem("lo_ready")
        chunk_used = sem("chunk_used")
        rows_out, ada_post = sem("rows_out"), sem("ada_post")
        evac_v, evac_s = sem("evac_v"), sem("evac_s")
        par_rows, par_tabs = sem("par_rows"), sem("par_tabs")
        prm_zero, cols_T = sem("prm_zero"), sem("cols_T")
        end_pe, end_act, end_dve, end_pool = sem("end_pe"), sem("end_act"), sem("end_dve"), sem("end_pool")
        vsteps, fsteps = sem("vsteps"), sem("fsteps")
        sq_in, ms_in, rs_in, xs_in = sem("sq_in"), sem("ms_in"), sem("rs_in"), sem("xs_in")
        nt_T, nt_f, nt_hi = sem("nt_T"), sem("nt_f"), sem("nt_hi")
        rg_m, rg_T = sem("rg_m"), sem("rg_T")
        rr_v, rp_T = sem("rr_v"), sem("rp_T")
        ac_v, rw_S1, rw_S1s, rw_W2, rw_R2 = (sem(n) for n in ("ac_v", "rw_S1", "rw_S1s", "rw_W2", "rw_R2"))
        cv_T, cv_ch, cv_z, cv_out, cv_hi = sem("cv_T"), sem("cv_ch"), sem("cv_z"), sem("cv_out"), sem("cv_hi")
        at_ms, at_rs, at_qk, at_T = sem("at_ms"), sem("at_rs"), sem("at_qk"), sem("at_T")
        at_ca, at_cv, at_S, at_mx = sem("at_ca"), sem("at_cv"), sem("at_S"), sem("at_mx")
        at_P, at_Pn, at_PT, at_pa, at_pv = sem("at_P"), sem("at_Pn"), sem("at_PT"), sem("at_pa"), sem("at_pv")
        at_O, at_hi, kv_out = sem("at_O"), sem("at_hi"), sem("kv_out")
        u_T = sem("u_T")
        lr_mix, lr_act, ab_z = sem("lr_mix"), sem("lr_act"), sem("ab_z")
        rw_v, rw_sq, rw_nrm, rw_ns, rw_rs = sem("rw_v"), sem("rw_sq"), sem("rw_nrm"), sem("rw_ns"), sem("rw_rs")
        rw_stage, rw_lr, rw_sig, rw_aa = sem("rw_stage"), sem("rw_lr"), sem("rw_sig"), sem("rw_aa")
        rw_s0, rw_VS, rw_Vt, rw_c, rw_E = sem("rw_s0"), sem("rw_VS"), sem("rw_Vt"), sem("rw_c"), sem("rw_E")
        rw_kr, rw_A, rw_m, rw_S0s = sem("rw_kr"), sem("rw_A"), sem("rw_m"), sem("rw_S0s")
        rw_bo, rw_bon, rw_bg, rw_bgT, rw_bgs = sem("rw_bo"), sem("rw_bon"), sem("rw_bg"), sem("rw_bgT"), sem("rw_bgs")
        rw_bv = sem("rw_bv")
        rw_R, rw_Rs, rw_SA, rw_SAs = sem("rw_R"), sem("rw_Rs"), sem("rw_SA"), sem("rw_SAs")
        lv_X0, lv_C, lv_U, lv_Us, lv_XM, lv_X = (sem(n) for n in ("lv_X0", "lv_C", "lv_U", "lv_Us", "lv_XM", "lv_X"))
        rw_Y, rw_ST, rw_y, rw_mean, rw_yc, rw_y2 = (sem(n) for n in ("rw_Y", "rw_ST", "rw_y", "rw_mean", "rw_yc", "rw_y2"))
        rw_var, rw_vs, rw_vr, rw_o, rw_hi = (sem(n) for n in ("rw_var", "rw_vs", "rw_vr", "rw_o", "rw_hi"))
        ST_v, st_out, y_out = sem("ST_v"), sem("st_out"), sem("y_out")
        ff_s, ff_g, ff_u, ff_T, ff_hi, ff_lo, dn_out = (sem(n) for n in (
            "ff_s", "ff_g", "ff_u", "ff_T", "ff_hi", "ff_lo", "dn_out"))
        ENDS = {"pe": end_pe, "act": end_act, "dve": end_dve, "pool": end_pool}

        halves = ((slice(0, HALF), slice(HALF, P)), (slice(HALF, P), slice(0, HALF)))

        def settle(eng):
            eng.sem_inc(passed, 1)

        def phase_end(eng, who, l, k):
            settle(eng)
            eng.drain().then_inc(ENDS[who], 1)
            for name, s in ENDS.items():
                if name != who:
                    eng.wait_ge(s, l * BARS + k + 1)
            settle(eng)

        class Steps:

            def __init__(self, eng, s, per):
                self.eng, self.s, self.per, self.n = eng, s, per, 0

            def start(self, it):
                self.base, self.n = it * self.per, 0

            def mark(self, ins):
                ins.then_inc(self.s, 1)
                self.n += 1

            def sync(self):
                self.eng.wait_ge(self.s, self.base + self.n)

            def step(self, ins):
                self.mark(ins)
                self.sync()

            def end(self):
                assert self.n == self.per, (self.n, self.per)

        def col1(c):
            return col[:, c:c + 1]

        def dyn(ap, start, size):
            return ap[:, bass.ds(start, size)]

        block = ctx.enter_context(nc.Block())

        @block.sync
        def _(sp):
            sp.dma_start(con[:], A["consts"]).then_inc(con_in, 16)
            sp.dma_start(csf[0:KT, 0, :], A["c_ctx"].rearrange("(k p) -> k p", p=P)).then_inc(c_in, 16)
            sp.dma_start(csf[KT:2 * KT, 0, :], A["c"][0].rearrange("(k p) -> k p", p=P)).then_inc(c_in, 16)
            sp.dma_start(x[:, 0, :], A["x_prompt"][0]).then_inc(x_in, 16)
            sp.dma_start(x[:, 1, :], A["x_sample"][0]).then_inc(x_in, 16)

            def load(q, c, src, width=NW):
                sp.wait_ge(lo_ready, q * 4 + (c + 1))
                sp.dma_start(rawW[:, c % LEAD, :, 0:width], src).then_inc(raw_full[c % LEAD], 16)

            def load_tile(q, w, n0, width=NW):
                for c in range(CPT):
                    load(q, c, w[:, 2 * c:2 * c + 2, bass.ds(n0, width)], width)

            def load_down(q, w, j):
                for c in range(2 * OUT_TILES):
                    n0 = (c // 2) * NW
                    load(q, c, w[:, bass.ds(j * 4 + 2 * (c % 2), 2), n0:n0 + NW])

            with sp.Fori(0, LAYERS) as l:
                wada, win, wout, wgate, wup, wdown = (A[n][l].rearrange("(k p) n -> p k n", p=P) for n in (
                    "w_ada", "w_in", "w_out", "w_gate", "w_up", "w_down"))
                ql = l * Q_LAYER
                with sp.Fori(0, 8) as i:
                    load_tile(ql + Q_ADA01 + i * 2, wada, i * NW)
                with sp.Fori(0, WIN_TILES - 1) as i:
                    load_tile(ql + Q_WIN + i * 2, win, i * NW)
                load_tile(ql + Q_WIN + (WIN_TILES - 1) * 2, win, (WIN_TILES - 1) * NW, WIN_LAST)
                with sp.Fori(0, 16) as i:
                    load_tile(ql + Q_ADA2 + i * 2, wada, i * NW + 2 * D)
                with sp.Fori(0, OUT_TILES) as i:
                    load_tile(ql + Q_WOUT + i * 2, wout, i * NW)
                load_tile(ql + Q_FFN, wgate, 0)
                load_tile(ql + Q_FFN + 2, wup, 0)
                with sp.Fori(1, FF_TILES) as j:
                    qb = ql + (Q_FFN - 2) + j * 6
                    load_tile(qb, wgate, j * NW)
                    load_tile(qb + 2, wup, j * NW)
                    load_down(qb + 4, wdown, j - 1)
                load_down(ql + (Q_FFN + 4 + 6 * (FF_TILES - 1)), wdown, FF_TILES - 1)

        @block.scalar
        def _(act):
            def hi(q, c0, c1, width=NW):
                for c in range(c0, c1):
                    s = c % LEAD
                    act.wait_ge(raw_full[s], q * 16 + 16 * (c // LEAD + 1))
                    act.wait_ge(chunk_used, q * 4 + (c + 1))
                    act.activation(hiW[:, s, :, 0:width], rawW[:, s, :, 0:width], ACT.Copy).then_inc(hi_ready, 1)

            def tile_done(q):
                act.wait_ge(chunk_used, q * 4 + (CPT + LEAD))

            def evac(q, out, b, width=NW):
                tile_done(q)
                act.activation(out, bank[b][:, 0:width], ACT.Copy).then_inc(evac_s, 1)

            def ada(q):
                hi(q, 4, 12)
                hi(q + 2, 4, 12)

            def norm(it, xs, tf):
                for g in range(2):
                    act.activation(xs[:, g], x[:, g], ACT.Square, accum_out=ss[:, g:g + 1]).then_inc(sq_in, 1)
                for b in range(8):
                    g, kq = b // 4, b % 4
                    act.wait_ge(nt_f, it * 8 + (b + 1))
                    act.activation(actH[:, 4 * kq:4 * kq + 4, g * P:(g + 1) * P],
                                   tf[:, b % 2].rearrange("p (k t) -> p k t", k=4), ACT.Copy).then_inc(nt_hi, 1)

            def residual():
                for g in range(2):
                    act.activation(xs2[:, g], o[:, g], ACT.Square, accum_out=ss[:, g:g + 1]).then_inc(sq_in, 1)

            def parameters(l):
                act.wait_ge(prm_zero, l + 1)
                put = lambda dst, src: act.dma_start(dst, src).then_inc(par_rows, 16)
                row = lambda ap: ap.rearrange("(r c) -> r c", c=P)
                mu = A["rwkv_mu"][l]
                put(prm[0:12, 0, :], row(mu[0:12 * P]))
                put(prm[12:13, 0, 0:64], mu[12 * P:12 * P + 64].unsqueeze(0))
                put(prm[13:14, 0, 0:GATE_RANK], mu[12 * P + 64:D_RWIN].unsqueeze(0))
                for c, name in ((COL_W0, "rwkv_w0"), (COL_A0, "rwkv_a0")):
                    put(prm[c:c + 8, 0, :], A[name][l].rearrange("d (r c) -> (d r) c", c=P))
                for c, name in ((COL_KK, "rwkv_k_k"), (COL_KA, "rwkv_k_a"), (COL_LG, "rwkv_ln_g"), (COL_LB, "rwkv_ln_b")):
                    put(prm[c:c + 4, 0, :], row(A[name][l]))
                put(prm[COL_RK:COL_RK + 4, 0, :], A["rwkv_r_k"][l].rearrange("(r a) b -> r (a b)", a=2))
                put(prm[COL_CV:COL_CV + 12, 0, :], A["conv_w"][l].rearrange("w (r c) -> (w r) c", c=P))
                put(prm[0:64, 1, :], A["norm_g"][l].rearrange("n (r c) -> (n r) c", c=P))
                put(prm[0:96, 2, :], row(A["b_ada"][l]))
                put = lambda dst, src: act.dma_start(dst, src).then_inc(par_tabs, 16)
                put(wla[0:32], A["rwkv_w_up"][l].rearrange("d r n -> r d n"))
                put(wla[32:64], A["rwkv_a_up"][l].rearrange("d r n -> r d n"))
                put(wg[:], A["rwkv_g_up"][l])
                put(ctxk[:], A["cache_k"][0][l])
                put(ctxv[:], A["cache_v"][0][l])
                put(qkw[:, 0], A["q_norm"][l].partition_broadcast(P))
                put(qkw[:, 1], A["k_norm"][l].partition_broadcast(P))
                for d in range(2):
                    put(s0all[:, d], A["state_rwkv"][0][l][d].rearrange("(f h) i j -> (h i) f j", h=2))

            def conv(l):
                for g in range(2):
                    act.wait_ge(cv_T, l * 6 + (g + 1))
                    act.activation(chT[:, g], bank[4 + g][:].rearrange("p (f t) -> p f t", f=4), ACT.Copy).then_inc(cv_ch, 1)
                for g in range(2):
                    act.wait_ge(cv_out, l * 2 + (g + 1))
                    act.activation(actH[:, 8:12, g * P:(g + 1) * P], cv[:, :, g], ACT.Copy).then_inc(cv_hi, 1)

            def attention(l, g):
                it = l * 2 + g
                nk = P if g == 0 else 2 * P
                if g == 0:
                    act.wait_ge(at_qk, it + 1)
                    act.dma_start(O["new_k"][0][l], qk[:, NH:NH + NKV]).then_inc(kv_out, 16)
                    act.dma_start(O["new_v"][0][l], proj[:, 0, D_QK:D_ATT].rearrange("p (h d) -> p h d", h=NKV)).then_inc(kv_out, 16)
                act.wait_ge(at_T, it * 3 + 1)
                act.activation(qT[:, 0:4], bank[0][:].rearrange("p (h t) -> p h t", h=4), ACT.Copy).then_inc(at_ca, 1)
                act.wait_ge(at_T, it * 3 + 3)
                act.activation(kT[:, :, 0:nk].rearrange("p v (s t) -> p s v t", t=P),
                               bank[2][:, 0:2 * nk].rearrange("p (s v t) -> p s v t", v=2, t=P), ACT.Copy).then_inc(at_ca, 1)
                act.wait_ge(at_mx, it + 1)
                for h in range(NH):
                    e = act.activation(pr[:, h, 0:nk], bank[3 + h // 2][:, (h % 2) * 256:(h % 2) * 256 + nk], ACT.Exp,
                                       bias=qst[:, 40 + h:41 + h], scale=SCALE, accum_out=qst[:, 48 + h:49 + h])
                e.then_inc(at_P, 1)
                act.wait_ge(at_PT, it * 2 + 1)
                for k in range(nk // P):
                    e = act.activation(pT[:, k, 0:4], bank[2 * k][:].rearrange("p (h t) -> p h t", h=4), ACT.Copy)
                e.then_inc(at_pa, 1)
                for v in range(NKV):
                    act.wait_ge(at_O, it * 2 + (v + 1))
                    act.activation(actH[:, 4 * v:4 * v + 4, g * P:(g + 1) * P],
                                   bank[4 + v][:].rearrange("p (h t) -> p h t", h=4), ACT.Copy).then_inc(at_hi, 1)
                if g == 0:
                    act.wait_ge(kv_out, l * 32 + 32)

            def turn_u(l):
                for b in range(3):
                    act.wait_ge(u_T, l * 7 + (b + 1))
                    act.activation(uT[:, 4 * b:4 * b + 4, 0, 1:129], bank[b][:].rearrange("p (f t) -> p f t", f=4), ACT.Copy)
                act.wait_ge(u_T, l * 7 + 7)
                act.activation(uT[0:64, 12, :, 1:129], bank[6][0:64, 0:256].rearrange("p (g t) -> p g t", g=2), ACT.Copy)
                act.activation(uT[0:GATE_RANK, 13, :, 1:129],
                               bank[6][0:GATE_RANK, 256:512].rearrange("p (g t) -> p g t", g=2), ACT.Copy)

            def rwkv(l):
                act.wait_ge(lr_mix, l + 1)
                act.activation(xwa[0:32], xwa[0:32], ACT.Tanh)
                act.activation(xg[:], xg[:], ACT.Sigmoid).then_inc(lr_act, 1)
                with act.Fori(0, FT) as f:
                    it = act.snap(l * FT + f)
                    qa = act.snap(l * Q_LAYER + Q_ADA2 + f * 8)
                    act.activation(wS[:], wla[:, :, bass.ds(f * P, P)], ACT.Copy)
                    act.activation(gS[:], wg[:, bass.ds(f * P, P)], ACT.Copy).then_inc(rw_stage, 1)
                    act.wait_ge(rw_ns, it + 1)
                    act.activation(ksq[:], nrm[:], ACT.Sqrt).then_inc(rw_rs, 1)
                    hi(qa, 4, 8)
                    act.wait_ge(rw_lr, it + 1)
                    for d in range(2):
                        e = act.activation(sig[d], bank[1][:, d * 256:(d + 1) * 256], ACT.Sigmoid,
                                           bias=dyn(col, f + (COL_W0 + 4 * d), 1))
                    e.then_inc(rw_sig, 1)
                    for d in range(2):
                        e = act.activation(aa[d], bank[2][:, d * 256:(d + 1) * 256], ACT.Sigmoid,
                                           bias=dyn(col, f + (COL_A0 + 4 * d), 1))
                    e.then_inc(rw_aa, 1)
                    act.wait_ge(rw_VS, it + 1)
                    act.activation(Vt[:], bank[3][:, 0:256].rearrange("p (g c) -> p g c", g=2), ACT.Copy).then_inc(rw_Vt, 1)
                    act.wait_ge(rw_c, it + 1)
                    for d in range(2):
                        for g in range(2):
                            n = 2 * d + g
                            act.activation(E1[:, d, g], cs[:, d, g], ACT.Exp, bias=amid[:, n:n + 1], scale=-ALPHA)
                            e = act.activation(E2[:, d, g], cs[:, d, g], ACT.Exp, bias=amid[:, 4 + n:5 + n], scale=ALPHA)
                    e.then_inc(rw_E, 1)
                    hi(qa, 8, 12)
                    act.wait_ge(rw_R, it + 1)
                    act.activation(Rs[:], bank[6][:].rearrange("p (n i) -> p n i", n=4), ACT.Copy).then_inc(rw_Rs, 1)
                    act.wait_ge(rw_bgT, it + 1)
                    act.activation(bgt, bank[7][:].rearrange("p (d n j) -> p d n j", d=2, n=2), ACT.Copy).then_inc(rw_bgs, 1)
                    with act.Fori(0, LEVELS // 2) as v:
                        n = act.snap(it * (2 * LEVELS) + v * 4)
                        q = act.snap(qa + 2 + v * 2)
                        for w in range(2):
                            for d in range(2):
                                act.wait_ge(lv_U, n + (2 * w + d + 3))
                                act.activation(U[:, d], bank[d][:, 0:4 * HALF].rearrange("p (s t) -> p s t", s=4),
                                               ACT.Copy).then_inc(lv_Us, 1)
                            hi(q, 4 + 4 * w, 8 + 4 * w)
                    for half, (done, said) in enumerate(((rw_S1, rw_S1s), (rw_SA, rw_SAs))):
                        act.wait_ge(done, it + 1)
                        for d in range(2):
                            hs = halves[d][half]
                            e = act.activation(SA[hs, 2 * d:2 * d + 2], bank[7][hs, 2 * d * P:(2 * d + 2) * P].rearrange(
                                "p (n i) -> p n i", n=2), ACT.Copy, scale=-1.0)
                        e.then_inc(said, 1)
                    act.wait_ge(rw_ST, it + 1)
                    act.activation(STs[:], bank[1][:, 0:2 * RH].rearrange("p (d j) -> p d j", d=2), ACT.Copy).then_inc(ST_v, 1)
                    act.wait_ge(ST_v, it + 1)
                    for d in range(2):
                        act.dma_start(O["new_rwkv"][0][l][d].rearrange("(f h) i j -> f (h i) j", h=2)[f],
                                      STs[:, d]).then_inc(st_out, 16)
                    act.wait_ge(rw_yc, it + 1)
                    act.activation(yy[1], yy[0], ACT.Square).then_inc(rw_y2, 1)
                    act.wait_ge(rw_vs, it + 1)
                    act.activation(yy[3], yy[2], ACT.Sqrt).then_inc(rw_vr, 1)
                    act.wait_ge(rw_o, it + 1)
                    act.activation(actH[:, bass.ds(f + 12, 1), :], yy[0].unsqueeze(1), ACT.Copy).then_inc(rw_hi, 1)
                    act.wait_ge(st_out, it * 32 + 32)
                    settle(act)

            def ffn(l):
                ql = l * Q_LAYER

                def gate(q, j):
                    tile_done(q)
                    for g in range(2):
                        act.activation(sg[:, g], bank[g][:], ACT.Sigmoid).then_inc(ff_s, 1)

                def turned(j):
                    for g in range(2):
                        act.wait_ge(ff_T, l * (2 * FF_TILES) + j * 2 + (g + 1))
                        act.activation(ffH[:, :, g * P:(g + 1) * P],
                                       bank[4 + g][:].rearrange("p (k t) -> p k t", k=4), ACT.Copy).then_inc(ff_hi, 1)

                hi(ql + Q_FFN, 4, 12)
                gate(ql + Q_FFN, 0)
                hi(ql + Q_FFN + 2, 4, 12)
                with act.Fori(1, FF_TILES) as j:
                    qb = act.snap(ql + (Q_FFN - 2) + j * 6)
                    hi(qb, 4, 12)
                    act.wait_ge(ff_u, l * FF_TILES + j)
                    gate(qb, j)
                    turned(j - 1)
                    hi(qb + 2, 4, 12)
                    hi(qb + 4, 4, 12)
                turned(FF_TILES - 1)
                hi(ql + (Q_FFN + 4 + 6 * (FF_TILES - 1)), 4, 8)

            act.wait_ge(c_in, 32)
            act.activation(csf[0:2 * KT, 1], csf[0:2 * KT, 0], ACT.Sigmoid).then_inc(cs_done, 1)
            act.wait_ge(cs_done, 4)
            csv = csR[:, 0:4 * KT].rearrange("p (k c) -> p c k", c=4)
            act.activation(csv[:, 0:2], bank[0][:, 0:2 * KT].rearrange("p (g k) -> p g k", g=2), ACT.Copy).then_inc(cs_done, 1)
            act.wait_ge(x_in, 32)
            with act.Fori(0, LAYERS) as l:
                ql = act.snap(l * Q_LAYER)
                parameters(l)
                hi(ql, 0, 4)
                phase_end(act, "act", l, 0)
                with act.Fori(0, 4) as i:
                    ada(act.snap(ql + Q_ADA01 + i * 4))
                phase_end(act, "act", l, 1)
                norm(l * 2, xs1, tf1)
                phase_end(act, "act", l, 2)
                with act.Fori(0, 4) as i:
                    q = act.snap(ql + Q_WIN + i * 4)
                    hi(q, 4, 12)
                    evac(q, proj[:, 1, bass.ds(i * (2 * NW), NW)], 1)
                    hi(q + 2, 4, 12)
                    evac(q + 2, proj[:, 1, bass.ds(i * (2 * NW) + NW, NW)], 3)
                q = ql + Q_WIN + 16
                hi(q, 4, 8)
                hi(q, 8, 12, WIN_LAST)
                evac(q, proj[:, 1, 8 * NW:9 * NW], 1)
                hi(q + 2, 4, 8, WIN_LAST)
                hi(q + 2, 8, 12)
                evac(q + 2, proj[:, 1, 9 * NW:D_IN], 3, WIN_LAST)
                phase_end(act, "act", l, 3)
                act.wait_ge(par_tabs, l * (9 * 16) + 9 * 16)
                conv(l)
                phase_end(act, "act", l, 4)
                for g in range(2):
                    attention(l, g)
                    phase_end(act, "act", l, 5 + g)
                turn_u(l)
                phase_end(act, "act", l, 7)
                rwkv(l)
                phase_end(act, "act", l, 8)
                for i in range(2):
                    q = ql + Q_WOUT + i * 4
                    hi(q, 4, 12)
                    evac(q, o[:, 1, 2 * i * NW:(2 * i + 1) * NW], 1)
                    hi(q + 2, 4, 12)
                    evac(q + 2, o[:, 1, (2 * i + 1) * NW:(2 * i + 2) * NW], 3)
                phase_end(act, "act", l, 9)
                residual()
                phase_end(act, "act", l, 10)
                norm(l * 2 + 1, xs2, tf2)
                phase_end(act, "act", l, 11)
                ffn(l)
                phase_end(act, "act", l, 12)
                residual()
                phase_end(act, "act", l, 13)
            act.dma_start(O["y_prompt"][0], x[:, 0, :]).then_inc(y_out, 16)
            act.dma_start(O["y_sample"][0], x[:, 1, :]).then_inc(y_out, 16)
            act.wait_ge(y_out, 32)

        @block.gpsimd
        def _(pool):
            def power(out, in_):
                n = in_.shape[1]
                return pool.tensor_tensor(out, in_, mhalf.to_broadcast([P, n]), ALU.pow)

            def stats(n, l):
                pool.wait_ge(ms_in, l * 4 + (n + 1))
                power(rstd, ms).then_inc(rs_in, 1)

            pool.wait_ge(con_in, 16)
            pool.memset(s0bd[:], 0.0).then_inc(rw_s0, 1)
            with pool.Fori(0, LAYERS) as l:
                phase_end(pool, "pool", l, 0)
                phase_end(pool, "pool", l, 1)
                stats(0, l)
                phase_end(pool, "pool", l, 2)
                phase_end(pool, "pool", l, 3)
                pool.memset(mT[:], 0.0).then_inc(cv_z, 1)
                phase_end(pool, "pool", l, 4)
                for g in range(2):
                    pool.wait_ge(at_ms, l * 2 + (g + 1))
                    power(qst[:, 20:30], qst[:, 10:20]).then_inc(at_rs, 1)
                    phase_end(pool, "pool", l, 5 + g)
                pool.memset(uT[:, :, :, 0:1], 0.0)
                pool.memset(uT[:, :, :, 129:130], 0.0)
                phase_end(pool, "pool", l, 7)
                pool.memset(AE[:], 0.0)
                pool.memset(BF[:], 0.0).then_inc(ab_z, 1)
                pool.wait_ge(ab_z, l + 1)
                settle(pool)
                with pool.Fori(0, FT) as f:
                    it = pool.snap(l * FT + f)
                    for h in range(2):
                        hs = slice(RH * h, RH * h + RH)
                        e = pool.tensor_copy(s0bd[hs, :, hs], s0all[hs, :, bass.ds(f, 1), :].rearrange("p d f j -> p (d f) j"))
                    e.then_inc(rw_s0, 1)
                    pool.wait_ge(rw_s0, it + 2)
                    for d in range(2):
                        pool.wait_ge(rw_m, it * 2 + (d + 1))
                        for k, hs in enumerate(halves[0]):
                            settle(pool)
                            pool.tensor_copy(AC[hs, d], AE[hs, d, :, hs]).then_inc(ac_v, 1)
                            pool.wait_ge(ac_v, it * 4 + (2 * d + k + 1))
                    settle(pool)
                    for d in range(2):
                        e = pool.tensor_copy(X[:, d].rearrange("p s (a t) -> p (s a) t", a=2),
                                             con[:, C_I2:C_I2 + HALF].unsqueeze(1).broadcast_to([P, 8, HALF]))
                    e.then_inc(lv_X0, 1)
                    with pool.Fori(0, LEVELS) as v:
                        n = pool.snap(it * (2 * LEVELS) + v * 2)
                        for d in range(2):
                            pool.wait_ge(lv_U, n + (d + 1))
                            settle(pool)
                            pool.tensor_tensor(CT[:, d], AC[:, d],
                                               con[:, bass.ds(v * HALF + C_LV, HALF)].unsqueeze(1).broadcast_to([P, 4, HALF]),
                                               ALU.mult).then_inc(lv_C, 1)
                    pool.wait_ge(lv_C, it * (2 * LEVELS) + 2 * LEVELS)
                    settle(pool)
                phase_end(pool, "pool", l, 8)
                phase_end(pool, "pool", l, 9)
                stats(1, l)
                phase_end(pool, "pool", l, 10)
                pool.memset(o[:], 0.0)
                stats(2, l)
                phase_end(pool, "pool", l, 11)
                phase_end(pool, "pool", l, 12)
                stats(3, l)
                phase_end(pool, "pool", l, 13)

        @block.tensor
        def _(pe):
            def mm(out, a, b, start=True, stop=True):
                return pe.matmul(out, a, b, start=start, stop=stop, skip_group_check=True)

            def gemm(q, banks, H=actH, L=actL, width=NW):
                for c in range(CPT):
                    s = c % LEAD
                    pe.wait_ge(lo_ready, q * 4 + (c + 1 + LEAD))
                    for n in range(2):
                        k = 2 * c + n
                        for g in range(2):
                            out = bank[banks[g]][:, 0:width]
                            Hk, Lk = H[:, k, g * P:(g + 1) * P], L[:, k, g * P:(g + 1) * P]
                            mm(out, Hk, hiW[:, s, n, 0:width], k == 0, False)
                            mm(out, Hk, loW[:, s, n, 0:width], False, False)
                            e = mm(out, Lk, hiW[:, s, n, 0:width], False, k == KT - 1)
                    e.then_inc(chunk_used, 1)

            def free(l, t):
                pe.wait_ge(evac_v, l * (WIN_TILES + OUT_TILES) + (t + 1))
                pe.wait_ge(evac_s, l * (WIN_TILES + OUT_TILES) + (t + 1))

            def ada_chunks(q, c0, c1, b):
                for c in range(c0, c1):
                    s = c % LEAD
                    pe.wait_ge(lo_ready, q * 4 + (c + 1 + LEAD))
                    for n in range(2):
                        k = 2 * c + n
                        mm(bank[b][:], csR[:, 4 * k:4 * k + P], hiW[:, s, n], k == 0, False)
                        e = mm(bank[b][:], csR[:, 4 * k:4 * k + P], loW[:, s, n], False, k == KT - 1)
                    e.then_inc(chunk_used, 1)

            def turn_rows(rows, b):
                for j in range(4):
                    e = mm(bank[b][:, 2 * j:2 * j + 2], rows[:, j * P:(j + 1) * P], con[0:4, C_SELT:C_SELT + 2])
                return e

            def ada(q, a):
                for t in range(2):
                    pe.wait_ge(rows_out, a + (t + 1))
                    ada_chunks(q + 2 * t, 0, CPT, 2 * t)
                for t in range(2):
                    pe.wait_ge(rows_out, a + (t + 3))
                    turn_rows(rows1[0:4, t], 4 + t).then_inc(ada_post, 1)

            def residual(it, part):
                pe.wait_ge(rg_m, it + 1)
                for g in range(2):
                    for n in range(4):
                        for j in range(4):
                            e = mm(bank[4 * g + n][:, j * P:(j + 1) * P],
                                   modT[:, part, 4 * n + j, g:g + 1].broadcast_to([P, P]), ident)
                        e.then_inc(rg_T, 1)

            def norm(it, xs):
                for b in range(8):
                    g, kq = b // 4, b % 4
                    if kq == 0:
                        pe.wait_ge(xs_in, it * 2 + (g + 1))
                    if g == 1:
                        pe.wait_ge(nt_f, it * 8 + (b - 3))
                    for j in range(4):
                        e = pe.transpose(bank[4 + kq][:, j * P:(j + 1) * P], xs[:, g, (4 * kq + j) * P:(4 * kq + j + 1) * P], ident)
                    e.then_inc(nt_T, 1)

            def conv(l):
                for which, b0 in ((2, 4), (1, 2), (0, 0)):
                    for g in range(2):
                        for f in range(4):
                            c = OFF_CONV + which * D_CONV + f * P
                            e = pe.transpose(bank[b0 + g][:, f * P:(f + 1) * P], proj[:, g, c:c + P], ident)
                        e.then_inc(cv_T, 1)

            def attention(l, g):
                it = l * 2 + g
                pe.wait_ge(at_qk, it + 1)
                for b in range(2):
                    for j in range(4):
                        e = pe.transpose(bank[b][:, j * P:(j + 1) * P], qk[:, 4 * b + j], ident)
                    e.then_inc(at_T, 1)
                for v in range(NKV):
                    e = pe.transpose(bank[2][:, v * P:(v + 1) * P], qk[:, NH + v], ident)
                if g == 1:
                    for v in range(NKV):
                        e = pe.transpose(bank[2][:, (2 + v) * P:(3 + v) * P], ctxk[:, v], ident)
                e.then_inc(at_T, 1)
                nk = P if g == 0 else 2 * P
                pe.wait_ge(at_ca, it * 2 + 2)
                for h in range(NH):
                    if h == 4:
                        pe.wait_ge(at_cv, it + 1)
                    e = mm(bank[3 + h // 2][:, (h % 2) * 256:(h % 2) * 256 + nk], qT[:, h], kT[:, h // 4, 0:nk])
                    if h % 2:
                        e.then_inc(at_S, 1)
                pe.wait_ge(at_Pn, it + 1)
                for b in range(2):
                    for k in range(nk // P):
                        for j in range(4):
                            e = pe.transpose(bank[2 * k + b][:, j * P:(j + 1) * P], pr[:, 4 * b + j, k * P:(k + 1) * P], ident)
                    e.then_inc(at_PT, 1)
                for v in range(NKV):
                    pe.wait_ge((at_pa, at_pv)[v], it + 1)
                    for k in range(nk // P):
                        V = proj[:, g, D_QK + v * HD:D_QK + (v + 1) * HD] if k == 0 else ctxv[:, v]
                        e = mm(bank[4 + v][:], V, pT[:, k, 4 * v:4 * v + 4].rearrange("p h t -> p (h t)"), k == 0, k == nk // P - 1)
                    e.then_inc(at_O, 1)

            def turn_u(l):
                for g in range(2):
                    for b in range(3):
                        for j in range(4):
                            c = OFF_RW + (4 * b + j) * P
                            e = pe.transpose(bank[3 * g + b][:, j * P:(j + 1) * P], proj[:, g, c:c + P], ident)
                        e.then_inc(u_T, 1)
                for g in range(2):
                    c = OFF_RW + 12 * P
                    pe.transpose(bank[6][0:64, g * P:(g + 1) * P], proj[:, g, c:c + 64], ident)
                    e = pe.transpose(bank[6][0:GATE_RANK, 256 + g * P:256 + (g + 1) * P], proj[:, g, c + 64:c + 160], ident)
                e.then_inc(u_T, 1)

            def rwkv(l):
                pe.wait_ge(lr_act, l + 1)
                settle(pe)
                with pe.Fori(0, FT) as f:
                    it = pe.snap(l * FT + f)
                    qa = pe.snap(l * Q_LAYER + Q_ADA2 + f * 8)
                    flat = lambda t: t.rearrange("p g t -> p (g t)")
                    pe.wait_ge(rw_sq, it + 1)
                    mm(bank[0][:, 0:256], blk1, flat(ksq[:])).then_inc(rw_nrm, 1)
                    ada_chunks(qa, 0, 4, 7)
                    pe.wait_ge(rw_stage, it + 1)
                    for d in range(2):
                        mm(bank[1][:, d * 256:(d + 1) * 256], wS[0:32, d], flat(xwa[0:32]))
                        mm(bank[2][:, d * 256:(d + 1) * 256], wS[32:64, d], flat(xwa[32:64]))
                    pe.wait_ge(rw_ns, it + 1)
                    mm(bank[0][:, 256:512], gS[:], flat(xg[:])).then_inc(rw_lr, 1)
                    pe.wait_ge(rw_v, it + 1)
                    pe.wait_ge(rw_s0, it + 2)
                    for g in range(2):
                        pe.transpose(bank[3][:, g * P:(g + 1) * P], rkv[:, 2, g], ident)
                    for d in range(2):
                        e = pe.transpose(bank[3][:, 256 + d * P:256 + (d + 1) * P], s0bd[:, d], ident)
                    e.then_inc(rw_VS, 1)
                    ada_chunks(qa, 4, 8, 7)
                    for d in range(2):
                        pe.wait_ge(rw_kr, it * 2 + (d + 1))
                        if d == 0:
                            pe.wait_ge(rr_v, it * 4 + 1)
                        if d == 1:
                            pe.wait_ge(rw_m, it * 2 + 1)
                        for m, left in ((4, be), (6, ga)):
                            for g in range(2):
                                for h in range(2):
                                    hs = slice(RH * h, RH * h + RH)
                                    e = mm(bank[m + h][:, g * 256:(g + 1) * 256], left[hs, d, g],
                                           KR[hs, d, g].rearrange("p a t -> p (a t)"))
                        e.then_inc(rw_A, 1)
                    pe.wait_ge(rw_bo, it + 1)
                    pe.wait_ge(rw_Vt, it + 1)
                    mm(bank[3][:, 0:256], blk1, flat(nrm[:])).then_inc(rw_bon, 1)
                    pe.wait_ge(rw_m, it * 2 + 2)
                    pe.wait_ge(rw_S0s, it + 1)
                    for d in range(2):
                        for g in range(2):
                            n = 2 * d + g
                            if g == 1:
                                mm(bank[6][:, n * P:(n + 1) * P], KR[:, d, g, 0], S0s[:, d], True, False)
                            for h in range(2):
                                e = mm(bank[6][:, n * P + h * RH:n * P + (h + 1) * RH], BF[:, d, 2 * g + h, 0:P],
                                       Vt[:, g, h * RH:(h + 1) * RH], g == 0, True)
                    e.then_inc(rw_R, 1)
                    pe.wait_ge(rw_bg, it + 1)
                    for d in range(2):
                        for n in range(2):
                            e = pe.transpose(bank[7][:, (2 * d + n) * P:(2 * d + n + 1) * P], bg0[:, d, n], ident)
                    e.then_inc(rw_bgT, 1)
                    pe.wait_ge(lv_X0, it + 1)
                    pe.wait_ge(rw_bv, it + 1)
                    settle(pe)
                    with pe.Fori(0, LEVELS // 2) as v:
                        n = pe.snap(it * (2 * LEVELS) + v * 4)
                        for w in range(2):
                            for d in range(2):
                                pe.wait_ge(lv_C, n + (2 * w + d + 1))
                                pe.wait_ge(lv_X, n + (2 * w + d + 1))
                                settle(pe)
                                for s in range(4):
                                    for hs in halves[0]:
                                        e = mm(bank[d][hs, s * HALF:(s + 1) * HALF], CT[hs, d, s], X[hs, d, s, 0:HALF])
                                e.then_inc(lv_U, 1)
                            for d in range(2):
                                pe.wait_ge(lv_Us, n + (2 * w + d + 1))
                                settle(pe)
                                for s in range(4):
                                    for hs in halves[0]:
                                        out = bank[2 + d][hs, s * P:(s + 1) * P]
                                        mm(out[:, 0:HALF], X[hs, d, s, HALF:P], U[hs, d, s])
                                        e = mm(out[:, HALF:P], U[hs, d, s], X[hs, d, s, HALF:P])
                                e.then_inc(lv_XM, 1)
                            if w == 0:
                                pe.wait_ge(rr_v, it * 4 + v + 1)
                                turn_rows(rows3[0:4], 5).then_inc(rp_T, 1)
                            ada_chunks(qa + 2 + v * 2, 4 * w, 4 * w + 4, 4)
                    pe.wait_ge(rw_bgs, it + 1)
                    pe.wait_ge(lv_X, it * (2 * LEVELS) + (2 * LEVELS + 2))
                    for half, (ready, done) in enumerate(((rw_Rs, rw_S1), (rw_R2, rw_SA))):
                        pe.wait_ge(ready, it + 1)
                        settle(pe)
                        for g in range(2):
                            for h in range(2):
                                for d in range(2):
                                    n, hs = 2 * d + g, halves[d][half]
                                    e = mm(bank[7][hs, n * P + h * RH:n * P + (h + 1) * RH], X[hs, d, 2 * g + h, HALF:P],
                                           Rs[hs, n, h * RH:(h + 1) * RH])
                        e.then_inc(done, 1)
                        if half == 0:
                            pe.wait_ge(rr_v, it * 4 + 4)
                            turn_rows(rows3[0:4], 5).then_inc(rp_T, 1)
                            pe.wait_ge(rw_S1s, it + 1)
                            settle(pe)
                            for g in range(2):
                                for h in range(2):
                                    for d in range(2):
                                        n, (one, two) = 2 * d + g, halves[d]
                                        e = mm(bank[6][two, n * P + h * RH:n * P + (h + 1) * RH],
                                               AE[one, d, 2 * g + h, two], SA[one, n, h * RH:(h + 1) * RH])
                            e.then_inc(rw_W2, 1)
                    pe.wait_ge(rw_SAs, it + 1)
                    for g in range(2):
                        if g == 1:
                            mm(bank[0][:, P:256], S0s[:, 0], KR[:, 0, 1, 1], True, False)
                            mm(bank[0][:, P:256], S0s[:, 1], KR[:, 1, 1, 1], False, False)
                        for h in range(2):
                            hs = slice(RH * h, RH * h + RH)
                            for d in range(2):
                                mm(bank[0][hs, g * P:(g + 1) * P], SA[:, 2 * d + g, hs], AE[:, d, 2 * g + h, P:256],
                                   g == 0 and d == 0, False)
                                e = mm(bank[0][hs, g * P:(g + 1) * P], Vt[:, g, hs], BF[:, d, 2 * g + h, P:256], False, d == 1)
                    e.then_inc(rw_Y, 1)
                    for d in range(2):
                        for h in range(2):
                            hs = slice(RH * h, RH * h + RH)
                            mm(bank[1][hs, d * RH:(d + 1) * RH], SA[:, 2 * d, hs], bgt[:, d, 0, hs], True, False)
                            e = mm(bank[1][hs, d * RH:(d + 1) * RH], Vt[:, 0, hs], bgt[:, d, 1, hs], False, True)
                    e.then_inc(rw_ST, 1)
                    pe.wait_ge(rw_y, it + 1)
                    mm(bank[2][:, 0:256], blkm, yy[0]).then_inc(rw_mean, 1)
                    pe.wait_ge(rw_y2, it + 1)
                    mm(bank[2][:, 256:512], blkm, yy[1]).then_inc(rw_var, 1)

            def ffn(l):
                ql = l * Q_LAYER

                def turn(j):
                    pe.wait_ge(ff_u, l * FF_TILES + (j + 1))
                    for g in range(2):
                        for k in range(4):
                            e = pe.transpose(bank[4 + g][:, k * P:(k + 1) * P], ff[:, g, k * P:(k + 1) * P], ident)
                        e.then_inc(ff_T, 1)

                def down(q, j):
                    pe.wait_ge(ff_hi, l * (2 * FF_TILES) + (j * 2 + 2))
                    pe.wait_ge(ff_lo, l * (2 * FF_TILES) + (j * 2 + 2))
                    for n in range(4):
                        if n >= 2:
                            pe.wait_ge(dn_out, l * (4 * FF_TILES) + (j * 4 + (n + 3)))
                        for c in range(2):
                            i = 2 * n + c
                            s = i % LEAD
                            pe.wait_ge(lo_ready, q * 4 + (i + 1 + LEAD))
                            for m in range(2):
                                k = 2 * c + m
                                for g in range(2):
                                    out = bank[(6 if n % 2 == 0 else 4) + g][:]
                                    Hk, Lk = ffH[:, k, g * P:(g + 1) * P], ffL[:, k, g * P:(g + 1) * P]
                                    mm(out, Hk, hiW[:, s, m], k == 0, False)
                                    mm(out, Hk, loW[:, s, m], False, False)
                                    e = mm(out, Lk, hiW[:, s, m], False, k == 3)
                            e.then_inc(chunk_used, 1)

                gemm(ql + Q_FFN, (0, 1))
                gemm(ql + Q_FFN + 2, (2, 3))
                with pe.Fori(1, FF_TILES) as j:
                    qb = pe.snap(ql + (Q_FFN - 2) + j * 6)
                    pe.wait_ge(ff_g, l * FF_TILES + j)
                    gemm(qb, (0, 1))
                    pe.wait_ge(dn_out, l * (4 * FF_TILES) + j * 4)
                    turn(j - 1)
                    gemm(qb + 2, (2, 3))
                    down(qb + 4, j - 1)
                pe.wait_ge(dn_out, l * (4 * FF_TILES) + 4 * FF_TILES)
                turn(FF_TILES - 1)
                down(ql + (Q_FFN + 4 + 6 * (FF_TILES - 1)), FF_TILES - 1)

            pe.sem_inc(chunk_used, LEAD)
            pe.sem_inc(lv_U, 2)
            pe.wait_ge(con_in, 16)
            pe.wait_ge(cs_done, 3)
            pe.transpose(bank[0][:, 0:2 * KT], csf[0:2 * KT, 2], con[0:2 * KT, C_ID:C_ID + 2 * KT]).then_inc(cs_done, 1)
            pe.wait_ge(cs_done, 6)
            with pe.Fori(0, LAYERS) as l:
                ql = pe.snap(l * Q_LAYER)
                pe.wait_ge(par_rows, l * (13 * 16) + 13 * 16)
                settle(pe)
                for r, n, c in ((0, ROWS_P, 0), (1, 64, COL_NG), (2, 96, COL_B)):
                    e = pe.transpose(bank[0][:, c:c + n], prm[0:n, r], con[0:n, C_ID:C_ID + n])
                e.then_inc(cols_T, 1)
                phase_end(pe, "pe", l, 0)
                with pe.Fori(0, 4) as i:
                    ada(pe.snap(ql + Q_ADA01 + i * 4), pe.snap(l * 8 + i * 2))
                phase_end(pe, "pe", l, 1)
                norm(l * 2, xs1)
                phase_end(pe, "pe", l, 2)
                with pe.Fori(0, 4) as i:
                    q = pe.snap(ql + Q_WIN + i * 4)
                    free(l, i * 2)
                    gemm(q, (0, 1))
                    free(l, i * 2 + 1)
                    gemm(q + 2, (2, 3))
                free(l, 8)
                gemm(ql + Q_WIN + 16, (0, 1))
                free(l, 9)
                gemm(ql + Q_WIN + 18, (2, 3), width=WIN_LAST)
                phase_end(pe, "pe", l, 3)
                conv(l)
                phase_end(pe, "pe", l, 4)
                for g in range(2):
                    attention(l, g)
                    phase_end(pe, "pe", l, 5 + g)
                turn_u(l)
                phase_end(pe, "pe", l, 7)
                rwkv(l)
                phase_end(pe, "pe", l, 8)
                for i in range(4):
                    free(l, WIN_TILES + i)
                    gemm(ql + Q_WOUT + i * 2, (0, 1) if i % 2 == 0 else (2, 3))
                phase_end(pe, "pe", l, 9)
                residual(l * 2, 2)
                phase_end(pe, "pe", l, 10)
                norm(l * 2 + 1, xs2)
                phase_end(pe, "pe", l, 11)
                ffn(l)
                phase_end(pe, "pe", l, 12)
                residual(l * 2 + 1, 5)
                phase_end(pe, "pe", l, 13)

        @block.vector
        def _(dve):
            S = Steps(dve, vsteps, VSTEPS)
            R = Steps(dve, fsteps, FSTEPS)
            TT, TS, STT = dve.tensor_tensor, dve.tensor_scalar, dve.scalar_tensor_tensor

            def lo(q, c0, c1, width=NW):
                for c in range(c0, c1):
                    s = c % LEAD
                    dve.wait_ge(hi_ready, q * 4 + (c + 1))
                    TT(loW[:, s, :, 0:width], rawW[:, s, :, 0:width], hiW[:, s, :, 0:width].bitcast(F32),
                       ALU.subtract).then_inc(lo_ready, 1)

            def tile_done(q):
                dve.wait_ge(chunk_used, q * 4 + (CPT + LEAD))

            def evac(q, out, b, width=NW):
                tile_done(q)
                dve.tensor_copy(out, bank[b][:, 0:width]).then_inc(evac_v, 1)

            mod = modT[:].rearrange("p m k g -> p (m k g)")

            def ada(q, i, a):
                for t in range(2):
                    qt = q + 2 * t
                    lo(qt, 4, 12)
                    tile_done(qt)
                    dve.tensor_copy(rows1[0:4, t], bank[2 * t][0:4, :]).then_inc(rows_out, 1)
                for t in range(2):
                    dve.wait_ge(ada_post, a + (t + 1))
                    dve.tensor_copy(mod[:, bass.ds(i * 16 + 8 * t, 8)], bank[4 + t][:, 0:8])

            def norm(it, xs, tf, sh, ng):
                bias = lambda p: col[:, COL_B + p * KT:COL_B + (p + 1) * KT].unsqueeze(2).broadcast_to([P, KT, 2])
                S.step(TT(modT[:, sh], modT[:, sh], bias(sh), ALU.add))
                S.step(TT(modT[:, sh + 1], modT[:, sh + 1], bias(sh + 1), ALU.add))
                S.step(TS(modT[:, sh + 1], modT[:, sh + 1], 1.0, None, ALU.add))
                S.step(TT(modT[:, sh + 1], modT[:, sh + 1],
                          col[:, COL_NG + ng * KT:COL_NG + (ng + 1) * KT].unsqueeze(2).broadcast_to([P, KT, 2]), ALU.mult))
                dve.wait_ge(sq_in, it * 4 + 2)
                TS(ms, ss, 1.0 / D, EPS, ALU.mult, ALU.add).then_inc(ms_in, 1)
                dve.wait_ge(rs_in, it * 2 + 1)
                for g in range(2):
                    TS(xs[:, g], x[:, g], rstd[:, g:g + 1], None, ALU.mult).then_inc(xs_in, 1)

                def low(b):
                    g, kq = b // 4, b % 4
                    dve.wait_ge(nt_hi, it * 8 + (b + 1))
                    a = slice(4 * kq, 4 * kq + 4), slice(g * P, (g + 1) * P)
                    S.mark(TT(actL[:, a[0], a[1]], tf[:, b % 2].rearrange("p (k t) -> p k t", k=4),
                              actH[:, a[0], a[1]].bitcast(F32), ALU.subtract))

                for b in range(8):
                    g, kq = b // 4, b % 4
                    dve.wait_ge(nt_T, it * 8 + (b + 1))
                    if b >= 2:
                        S.sync()
                    for j in range(4):
                        k = 4 * kq + j
                        e = TS(tf[:, b % 2, j * P:(j + 1) * P], bank[4 + kq][:, j * P:(j + 1) * P],
                               modT[:, sh + 1, k, g:g + 1], modT[:, sh, k, g:g + 1], ALU.mult, ALU.add)
                    e.then_inc(nt_f, 1)
                    if b:
                        low(b - 1)
                low(7)

            def residual(it, part, ng):
                cols = lambda c: col[:, c:c + KT].unsqueeze(2).broadcast_to([P, KT, 2])
                S.step(TT(modT[:, part], modT[:, part], cols(COL_B + part * KT), ALU.add))
                TT(modT[:, part], modT[:, part], cols(COL_NG + ng * KT), ALU.mult).then_inc(rg_m, 1)
                dve.wait_ge(sq_in, it * 4 + 4)
                TS(ms, ss, 1.0 / D, EPS, ALU.mult, ALU.add).then_inc(ms_in, 1)
                dve.wait_ge(rs_in, it * 2 + 2)
                for g in range(2):
                    for n in range(4):
                        c = slice(n * NW, (n + 1) * NW)
                        dve.wait_ge(rg_T, it * 8 + (4 * g + n + 1))
                        S.mark(STT(xs2[:, g, c], o[:, g, c], rstd[:, g:g + 1], bank[4 * g + n][:], ALU.mult, ALU.mult))
                    S.sync()
                    S.mark(TT(x[:, g], x[:, g], xs2[:, g], ALU.add))

            def conv(l):
                dve.wait_ge(cv_z, l + 1)
                for g in range(2):
                    dve.wait_ge(cv_T, l * 6 + (3 + g))
                    dve.wait_ge(cv_ch, l * 2 + (g + 1))
                    S.mark(TT(mT[:, :, g, 1:129], bank[2 + g][:].rearrange("p (f t) -> p f t", f=4), chT[:, g], ALU.mult))
                S.sync()
                for f in range(4):
                    S.mark(TS(cv[:, f], mT[:, f, :, 0:128], col1(COL_CV + f), None, ALU.mult))
                for w in (1, 2):
                    S.sync()
                    for f in range(4):
                        S.mark(STT(cv[:, f], mT[:, f, :, w:w + 128], col1(COL_CV + 4 * w + f), cv[:, f], ALU.mult, ALU.add))
                S.sync()
                for g in range(2):
                    dve.wait_ge(cv_T, l * 6 + (5 + g))
                    TT(cv[:, :, g], cv[:, :, g], bank[g][:].rearrange("p (f t) -> p f t", f=4), ALU.mult).then_inc(cv_out, 1)
                for g in range(2):
                    dve.wait_ge(cv_hi, l * 2 + (g + 1))
                    TT(actL[:, 8:12, g * P:(g + 1) * P], cv[:, :, g], actH[:, 8:12, g * P:(g + 1) * P].bitcast(F32), ALU.subtract)

            def attention(l, g):
                it = l * 2 + g
                nk = P if g == 0 else 2 * P
                raw = proj[:, g, 0:D_QK].rearrange("p (h d) -> p h d", d=HD)
                per_head = lambda v, n, w: v.unsqueeze(2).broadcast_to([P, n, w])
                S.step(TT(qc, raw, raw, ALU.mult))
                S.step(dve.tensor_reduce(qst[:, 0:10], qc, AX, ALU.add))
                TS(qst[:, 10:20], qst[:, 0:10], 1.0 / HD, EPS, ALU.mult, ALU.add).then_inc(at_ms, 1)
                dve.wait_ge(at_rs, it + 1)
                S.step(TT(qk[:], raw, per_head(qst[:, 20:30], 10, HD), ALU.mult))
                S.mark(TT(qk[:, 0:NH], qk[:, 0:NH], qkw[:, 0:1].broadcast_to([P, NH, HD]), ALU.mult))
                e = TT(qk[:, NH:], qk[:, NH:], qkw[:, 1:2].broadcast_to([P, NKV, HD]), ALU.mult)
                if g == 1:
                    S.step(e)
                    table = lambda c: con[:, c:c + HD].unsqueeze(1).broadcast_to([P, 10, HD])
                    S.mark(TT(qc, qk[:], table(C_COS), ALU.mult))
                    for b in range(2):
                        part = lambda t, b: t.rearrange("p h (a b c) -> p h a b c", a=2, b=2)[:, :, :, b]
                        sin = con[:, C_SIN:C_SIN + HD].rearrange("p (a b c) -> p a b c", a=2, b=2)[:, :, b]
                        S.mark(TT(part(qs, b), part(qk[:], 1 - b), sin.unsqueeze(1).broadcast_to([P, 10, 2, 32]), ALU.mult))
                    S.sync()
                    e = TT(qk[:], qc, qs, ALU.add)
                e.then_inc(at_qk, 1)
                dve.wait_ge(at_T, it * 3 + 2)
                dve.tensor_copy(qT[:, 4:8], bank[1][:].rearrange("p (h t) -> p h t", h=4)).then_inc(at_cv, 1)
                for b in range(4):
                    dve.wait_ge(at_S, it * 4 + (b + 1))
                    S.mark(dve.tensor_reduce(qst[:, 30 + 2 * b:32 + 2 * b],
                                             bank[3 + b][:].rearrange("p (h s) -> p h s", h=2)[:, :, 0:nk], AX, ALU.max))
                S.sync()
                TS(qst[:, 40:48], qst[:, 30:38], -SCALE, None, ALU.mult).then_inc(at_mx, 1)
                dve.wait_ge(at_P, it + 1)
                S.step(dve.reciprocal(qst[:, 56:64], qst[:, 48:56]))
                TT(pr[:, :, 0:nk], pr[:, :, 0:nk], per_head(qst[:, 56:64], NH, nk), ALU.mult).then_inc(at_Pn, 1)
                dve.wait_ge(at_PT, it * 2 + 2)
                for k in range(nk // P):
                    e = dve.tensor_copy(pT[:, k, 4:8], bank[2 * k + 1][:].rearrange("p (h t) -> p h t", h=4))
                e.then_inc(at_pv, 1)
                for v in range(NKV):
                    dve.wait_ge(at_hi, it * 2 + (v + 1))
                    a = slice(4 * v, 4 * v + 4), slice(g * P, (g + 1) * P)
                    TT(actL[:, a[0], a[1]], bank[4 + v][:].rearrange("p (h t) -> p h t", h=4),
                       actH[:, a[0], a[1]].bitcast(F32), ALU.subtract)

            def turn_u(l):
                for b in range(3):
                    dve.wait_ge(u_T, l * 7 + (b + 4))
                    dve.tensor_copy(uT[:, 4 * b:4 * b + 4, 1, 1:129], bank[3 + b][:].rearrange("p (f t) -> p f t", f=4))

            def rwkv(l):
                lr = ((12, 64, xwa), (13, GATE_RANK, xg))
                for n, (k, w, out) in enumerate(lr):
                    S.mark(TT(tmp3[0:w, n], uT[0:w, k, :, 0:128], uT[0:w, k, :, 2:130], ALU.add))
                S.sync()
                for n, (k, w, out) in enumerate(lr):
                    S.mark(TS(tmp3[0:w, n], tmp3[0:w, n], muh[0:w, k:k + 1], None, ALU.mult))
                S.sync()
                for n, (k, w, out) in enumerate(lr):
                    e = STT(out[:], uT[0:w, k, :, 1:129], omu[0:w, k:k + 1], tmp3[0:w, n], ALU.mult, ALU.add)
                e.then_inc(lr_mix, 1)
                dve.wait_ge(lr_mix, l + 1)
                settle(dve)
                flat = lambda t: t.rearrange("p g t -> p (g t)")
                with dve.Fori(0, FT) as f:
                    it = dve.snap(l * FT + f)
                    qa = dve.snap(l * Q_LAYER + Q_ADA2 + f * 8)
                    R.start(it)
                    for n in range(3):
                        a = uT[:, bass.ds(f + 4 * n, 1)]
                        R.mark(TT(tmp3[:, n:n + 1], a[:, :, :, 0:128], a[:, :, :, 2:130], ALU.add))
                    R.sync()
                    for n in range(3):
                        R.mark(TS(tmp3[:, n], tmp3[:, n], dyn(muh, f + 4 * n, 1), None, ALU.mult))
                    R.sync()
                    for n in range(3):
                        a = uT[:, bass.ds(f + 4 * n, 1), :, 1:129].rearrange("p f g t -> p (f g) t")
                        e = STT(rkv[:, n], a, dyn(omu, f + 4 * n, 1), tmp3[:, n], ALU.mult, ALU.add)
                    e.then_inc(rw_v, 1)
                    dve.wait_ge(rw_v, it + 1)
                    r_, k_, v_ = (rkv[:, n] for n in range(3))
                    R.step(TS(kk[:], k_, dyn(col, f + COL_KK, 1), None, ALU.mult))
                    TT(ksq[:], kk[:], kk[:], ALU.mult).then_inc(rw_sq, 1)
                    dve.wait_ge(rw_nrm, it + 1)
                    TS(flat(nrm[:]), bank[0][:, 0:256], KK_EPS, None, ALU.add).then_inc(rw_ns, 1)
                    dve.wait_ge(rw_rs, it + 1)
                    R.step(dve.reciprocal(ksq[:], ksq[:]))
                    R.step(TT(kk[:], kk[:], ksq[:], ALU.mult))
                    lo(qa, 4, 8)
                    dve.wait_ge(rw_lr, it + 1)
                    R.mark(dve.tensor_copy(flat(gT[:]), bank[0][:, 256:512]))
                    R.mark(dve.memset(cs[:, :, :, 0:1], 0.0))
                    dve.wait_ge(rw_sig, it + 1)
                    for d in range(2):
                        for g in range(2):
                            R.mark(dve.tensor_tensor_scan(cs[:, d, g, 1:129], ones, sig[d][:, g * P:(g + 1) * P], 0.0,
                                                          ALU.mult, ALU.add))
                    R.sync()
                    mid = cs[:, :, :, 64:65].rearrange("p d g o -> p d (g o)")
                    TS(amid[:, 0:4].rearrange("p (d g) -> p d g", d=2), mid, ALPHA, None, ALU.mult)
                    TS(amid[:, 4:8].rearrange("p (d g) -> p d g", d=2), mid, -ALPHA, None, ALU.mult).then_inc(rw_c, 1)
                    dve.wait_ge(rw_aa, it + 1)
                    for d in range(2):
                        R.mark(TS(flat(kd[:, d]), aa[d], dyn(col, f + COL_KA, 1), dyn(oka, f, 1), ALU.mult, ALU.add))
                        R.mark(TT(flat(be[:, d]), flat(kk[:]), aa[d], ALU.mult))
                    R.sync()
                    for d in range(2):
                        R.mark(TT(kd[:, d], kd[:, d], k_, ALU.mult))
                    R.sync()
                    dve.wait_ge(rw_E, it + 1)
                    for d in range(2):
                        Ei, Ex, Ev = ((E1[:, d, :, 1:129], E1[:, d, :, 0:128], E2[:, d, :, 1:129]) if d == 0 else
                                      (E2[:, d, :, 0:128], E2[:, d, :, 1:129], E1[:, d, :, 0:128]))
                        TT(KR[:, d, :, 0], kk[:], Ex, ALU.mult)
                        TT(KR[:, d, :, 1], r_, Ei, ALU.mult)
                        TT(ga[:, d], kd[:, d], Ev, ALU.mult)
                        TT(be[:, d], be[:, d], Ev, ALU.mult).then_inc(rw_kr, 1)
                    lo(qa, 8, 12)
                    tile_done(qa)
                    dve.tensor_copy(rows3[0:4], bank[7][0:4, :]).then_inc(rr_v, 1)
                    for d in range(2):
                        dve.wait_ge(rw_A, it * 2 + (d + 1))
                        if d == 0:
                            dve.wait_ge(ab_z, l + 1)
                        mask = con[:, C_TRI + d * 256:C_TRI + (d + 1) * 256].bitcast(U32).unsqueeze(1).broadcast_to([P, 2, 256])
                        settle(dve)
                        for m, dst in ((4, AE), (6, BF)):
                            for h in range(2):
                                e = dve.copy_predicated(dst[:, d, h:4:2], mask,
                                                        bank[m + h][:].rearrange("p (g t) -> p g t", g=2))
                        e.then_inc(rw_m, 1)
                    dve.wait_ge(rw_Vt, it + 1)
                    for d, mid in ((0, E2[:, 0, 1, 0:1]), (1, E1[:, 1, 1, 128:129])):
                        e = TS(S0s[:, d], bank[3][:, 256 + d * P:256 + (d + 1) * P], mid, None, ALU.mult)
                    e.then_inc(rw_S0s, 1)
                    R.mark(TT(nrm[:], kd[:, 0], kd[:, 1], ALU.add))
                    R.step(TS(ksq[:], r_, dyn(col, f + COL_RK, 1), None, ALU.mult))
                    TT(nrm[:], nrm[:], ksq[:], ALU.mult).then_inc(rw_bo, 1)
                    for d, end in ((0, E1[:, 0, 0, 128:129]), (1, E2[:, 1, 0, 0:1])):
                        TS(bg0[:, d, 0], be[:, d, 0], end, None, ALU.mult)
                        e = TS(bg0[:, d, 1], ga[:, d, 0], end, None, ALU.mult)
                    e.then_inc(rw_bg, 1)
                    dve.wait_ge(rw_bon, it + 1)
                    TT(flat(nrm[:]), bank[3][:, 0:256], flat(v_), ALU.mult).then_inc(rw_bv, 1)
                    dve.wait_ge(lv_X0, it + 1)
                    settle(dve)
                    with dve.Fori(0, LEVELS // 2) as v:
                        n = dve.snap(it * (2 * LEVELS) + v * 4)
                        q = dve.snap(qa + 2 + v * 2)
                        for w in range(2):
                            for d in range(2):
                                dve.wait_ge(lv_XM, n + (2 * w + d + 1))
                                TT(X[:, d], X[:, d], bank[2 + d][:].rearrange("p (s t) -> p s t", s=4), ALU.add).then_inc(lv_X, 1)
                            if w == 0:
                                dve.wait_ge(rp_T, it * 4 + v + 1)
                                dve.tensor_copy(mod[:, bass.ds(f * 32 + v * 8 + 64, 8)], bank[5][:, 0:8])
                            lo(q, 4 + 4 * w, 8 + 4 * w)
                        tile_done(q)
                        dve.tensor_copy(rows3[0:4], bank[4][0:4, :]).then_inc(rr_v, 1)
                    dve.wait_ge(rw_W2, it + 1)
                    for d in range(2):
                        two = halves[d][1]
                        e = TT(Rs[two, 2 * d:2 * d + 2], Rs[two, 2 * d:2 * d + 2],
                               bank[6][two, 2 * d * P:(2 * d + 2) * P].rearrange("p (n i) -> p n i", n=2), ALU.add)
                    e.then_inc(rw_R2, 1)
                    dve.wait_ge(rp_T, it * 4 + 4)
                    dve.tensor_copy(mod[:, bass.ds(f * 32 + 88, 8)], bank[5][:, 0:8])
                    y0, y1, y2, y3 = yy
                    dve.wait_ge(rw_Y, it + 1)
                    dve.tensor_copy(y0, bank[0][:, 0:256]).then_inc(rw_y, 1)
                    dve.wait_ge(rw_y, it + 1)
                    dve.wait_ge(rw_mean, it + 1)
                    TT(y0, y0, bank[2][:, 0:256], ALU.subtract).then_inc(rw_yc, 1)
                    dve.wait_ge(rw_yc, it + 1)
                    dve.wait_ge(rw_var, it + 1)
                    TS(y2, bank[2][:, 256:512], GN_EPS, None, ALU.add).then_inc(rw_vs, 1)
                    dve.wait_ge(rw_vr, it + 1)
                    R.step(dve.reciprocal(y3, y3))
                    R.step(TT(y0, y0, y3, ALU.mult))
                    R.step(TS(y0, y0, dyn(col, f + COL_LG, 1), dyn(col, f + COL_LB, 1), ALU.mult, ALU.add))
                    R.step(TT(y0, y0, flat(nrm[:]), ALU.add))
                    TT(y0, y0, flat(gT[:]), ALU.mult).then_inc(rw_o, 1)
                    dve.wait_ge(rw_hi, it + 1)
                    TT(actL[:, bass.ds(f + 12, 1)], y0.unsqueeze(1), actH[:, bass.ds(f + 12, 1)].bitcast(F32), ALU.subtract)
                    R.end()

            def ffn(l):
                ql = l * Q_LAYER

                def gate(q):
                    tile_done(q)
                    for g in range(2):
                        dve.wait_ge(ff_s, gate.base + (g + 1))
                        e = TT(sg[:, g], sg[:, g], bank[g][:], ALU.mult)
                    e.then_inc(ff_g, 1)

                def up(q, j):
                    tile_done(q)
                    dve.wait_ge(ff_g, l * FF_TILES + (j + 1))
                    for g in range(2):
                        e = TT(ff[:, g], sg[:, g], bank[2 + g][:], ALU.mult)
                    e.then_inc(ff_u, 1)

                def turned(j):
                    for g in range(2):
                        dve.wait_ge(ff_hi, l * (2 * FF_TILES) + (j * 2 + (g + 1)))
                        TT(ffL[:, :, g * P:(g + 1) * P], bank[4 + g][:].rearrange("p (k t) -> p k t", k=4),
                           ffH[:, :, g * P:(g + 1) * P].bitcast(F32), ALU.subtract).then_inc(ff_lo, 1)

                def down(q, n):
                    dve.wait_ge(chunk_used, q * 4 + (2 * n + 2 + LEAD))
                    for g in range(2):
                        out = o[:, g, n * NW:(n + 1) * NW]
                        e = TT(out, out, bank[(6 if n % 2 == 0 else 4) + g][:], ALU.add)
                    e.then_inc(dn_out, 1)

                def down_all(q, last=False):
                    for n in range(4):
                        if n < 2 or not last:
                            lo(q, 4 + 2 * n, 6 + 2 * n)
                        down(q, n)

                lo(ql + Q_FFN, 4, 12)
                gate.base = l * (2 * FF_TILES)
                gate(ql + Q_FFN)
                lo(ql + Q_FFN + 2, 4, 12)
                up(ql + Q_FFN + 2, 0)
                with dve.Fori(1, FF_TILES) as j:
                    qb = dve.snap(ql + (Q_FFN - 2) + j * 6)
                    lo(qb, 4, 12)
                    gate.base = l * (2 * FF_TILES) + j * 2
                    gate(qb)
                    turned(j - 1)
                    lo(qb + 2, 4, 12)
                    up(qb + 2, j)
                    dve.wait_ge(dn_out, l * (4 * FF_TILES) + (j * 4))
                    down_all(qb + 4)
                turned(FF_TILES - 1)
                dve.wait_ge(dn_out, l * (4 * FF_TILES) + 4 * FF_TILES)
                down_all(ql + (Q_FFN + 4 + 6 * (FF_TILES - 1)), last=True)

            dve.sem_inc(lo_ready, LEAD)
            dve.sem_inc(rows_out, 2)
            dve.sem_inc(evac_v, 2)
            dve.sem_inc(evac_s, 2)
            dve.sem_inc(lv_X, 2)
            dve.sem_inc(dn_out, 4)
            csv = csR[:, 0:4 * KT].rearrange("p (k c) -> p c k", c=4)
            dve.memset(csR[:].bitcast(F32), 0.0).then_inc(cs_done, 1)
            dve.wait_ge(cs_done, 2)
            TT(csf[0:2 * KT, 2], csf[0:2 * KT, 0], csf[0:2 * KT, 1], ALU.mult).then_inc(cs_done, 1)
            dve.wait_ge(cs_done, 5)
            TT(csv[:, 2:4], bank[0][:, 0:2 * KT].rearrange("p (g k) -> p g k", g=2), csv[:, 0:2].bitcast(F32),
               ALU.subtract).then_inc(cs_done, 1)
            with dve.Fori(0, LAYERS) as l:
                ql = dve.snap(l * Q_LAYER)
                S.start(l)
                dve.memset(prm[:, 0], 0.0).then_inc(prm_zero, 1)
                lo(ql, 0, 4)
                dve.wait_ge(cols_T, l + 1)
                S.step(dve.tensor_copy(col[:], bank[0][:, 0:COLS]))
                S.mark(TS(muh[:], col[:, COL_MU:COL_MU + 14], 0.5, None, ALU.mult))
                S.mark(TS(omu[:], col[:, COL_MU:COL_MU + 14], -1.0, 1.0, ALU.mult, ALU.add))
                S.step(TS(oka[:], col[:, COL_KA:COL_KA + 4], -1.0, 1.0, ALU.mult, ALU.add))
                phase_end(dve, "dve", l, 0)
                with dve.Fori(0, 4) as i:
                    ada(dve.snap(ql + Q_ADA01 + i * 4), i, dve.snap(l * 8 + i * 2))
                phase_end(dve, "dve", l, 1)
                norm(l * 2, xs1, tf1, 0, 0)
                phase_end(dve, "dve", l, 2)
                with dve.Fori(0, 4) as i:
                    q = dve.snap(ql + Q_WIN + i * 4)
                    lo(q, 4, 12)
                    evac(q, proj[:, 0, bass.ds(i * (2 * NW), NW)], 0)
                    lo(q + 2, 4, 12)
                    evac(q + 2, proj[:, 0, bass.ds(i * (2 * NW) + NW, NW)], 2)
                q = ql + Q_WIN + 16
                lo(q, 4, 8)
                lo(q, 8, 12, WIN_LAST)
                evac(q, proj[:, 0, 8 * NW:9 * NW], 0)
                lo(q + 2, 4, 8, WIN_LAST)
                lo(q + 2, 8, 12)
                evac(q + 2, proj[:, 0, 9 * NW:D_IN], 2, WIN_LAST)
                phase_end(dve, "dve", l, 3)
                dve.wait_ge(par_tabs, l * (9 * 16) + 9 * 16)
                conv(l)
                phase_end(dve, "dve", l, 4)
                for g in range(2):
                    attention(l, g)
                    phase_end(dve, "dve", l, 5 + g)
                turn_u(l)
                phase_end(dve, "dve", l, 7)
                rwkv(l)
                phase_end(dve, "dve", l, 8)
                for i in range(2):
                    q = ql + Q_WOUT + i * 4
                    lo(q, 4, 12)
                    evac(q, o[:, 0, 2 * i * NW:(2 * i + 1) * NW], 0)
                    lo(q + 2, 4, 12)
                    evac(q + 2, o[:, 0, (2 * i + 1) * NW:(2 * i + 2) * NW], 2)
                phase_end(dve, "dve", l, 9)
                residual(l * 2, 2, 1)
                phase_end(dve, "dve", l, 10)
                norm(l * 2 + 1, xs2, tf2, 3, 2)
                phase_end(dve, "dve", l, 11)
                ffn(l)
                phase_end(dve, "dve", l, 12)
                residual(l * 2 + 1, 5, 3)
                S.end()
                phase_end(dve, "dve", l, 13)


INS = ["x_prompt", "x_sample", "cache_k", "cache_v", "state_rwkv", "c", "c_ctx", "w_ada", "b_ada", "norm_g", "w_in",
       "q_norm", "k_norm", "conv_w", "rwkv_mu", "rwkv_w0", "rwkv_w_up", "rwkv_a0", "rwkv_a_up", "rwkv_g_up",
       "rwkv_k_k", "rwkv_k_a", "rwkv_r_k", "rwkv_ln_g", "rwkv_ln_b", "w_out", "w_gate", "w_up", "w_down"]
OUTS = {"y_prompt": (1, P, D), "y_sample": (1, P, D), "new_k": (1, LAYERS, P, NKV, HD), "new_v": (1, LAYERS, P, NKV, HD),
        "new_rwkv": (1, LAYERS, 2, RW_HEADS, RH, RH)}


def build(nc, shapes):
    A = {n: nc.dram_tensor(f"in_{n}", shapes[n], F32, kind="ExternalInput").ap() for n in INS + ["consts"]}
    O = {n: nc.dram_tensor(f"out_{n}", s, F32, kind="ExternalOutput").ap() for n, s in OUTS.items()}
    hybrid_trunk(nc, A, O)


def kernel(**inputs):
    import concourse.bacc as bacc
    from concourse.bass_utils import run_bass_kernel_spmd

    nc = bacc.Bacc("TRN2", target_bir_lowering=False, num_devices=1)
    arrays = {n: np.ascontiguousarray(inputs[n]) for n in INS}
    arrays["consts"] = constants()
    build(nc, {n: a.shape for n, a in arrays.items()})
    r = run_bass_kernel_spmd(nc, [{f"in_{n}": a for n, a in arrays.items()}], core_ids=[0])
    return tuple(r.results[0][f"out_{n}"] for n in OUTS)
```

```python
from contextlib import ExitStack

import numpy as np
import concourse.bass as bass
from concourse import mybir

F32 = mybir.dt.float32
F32R = mybir.dt.float32r
U32 = mybir.dt.uint32
ALU = mybir.AluOpType
ACT = mybir.ActivationFunctionType
AX = mybir.AxisListType.X

P = 128
LAYERS = 2
D = 2048
KT = D // P
NW = 512
HD = 128
NH, NKV = 8, 2
D_QK = (NH + NKV) * HD
D_ATT = D_QK + NKV * HD
D_CONV = 512
D_RW = 512
RW_HEADS, RH = 8, 64
FT = D_RW // P
OFF_CONV = D_ATT
OFF_RW = OFF_CONV + 3 * D_CONV
RANK, GATE_RANK = 32, 96
D_RWIN = 3 * D_RW + 2 * RANK + GATE_RANK
D_IN = OFF_RW + D_RWIN
D_FF = 5632
EPS, GN_EPS, KK_EPS = 1e-6, 64e-5, 1e-12
ALPHA = float(np.exp(-0.5))
SCALE = float(HD) ** -0.5
HALF = P // 2
LEVELS = 6

CPT = KT // 2
LEAD = 4
SLOTS = 2 * LEAD
WIN_TILES = -(-D_IN // NW)
WIN_LAST = D_IN - (WIN_TILES - 1) * NW
OUT_TILES = D // NW
FF_TILES = D_FF // NW
Q_ADA01 = 0
Q_WIN = Q_ADA01 + 8 * 2
Q_ADA2 = Q_WIN + WIN_TILES * 2
Q_WOUT = Q_ADA2 + 16 * 2
Q_FFN = Q_WOUT + OUT_TILES * 2
Q_LAYER = Q_FFN + FF_TILES * 6

C_ID, C_BO, C_BM, C_LV = 0, 128, 256, 384
C_I2 = C_LV + LEVELS * HALF
C_TRI = C_I2 + HALF
C_COS = C_TRI + 2 * 256
C_SIN = C_COS + P
C_SELT = C_SIN + P
C_ONE = C_SELT + 2
C_HALF = C_ONE + P
C_ALL = C_HALF + 1

COL_MU, COL_W0, COL_A0, COL_KK, COL_KA, COL_RK, COL_LG, COL_LB, COL_CV = 0, 14, 22, 30, 34, 38, 42, 46, 50
ROWS_P = 62
COL_NG = ROWS_P
COL_B = COL_NG + 4 * KT
COLS = COL_B + 6 * KT
VSTEPS, FSTEPS = 74, 27
BARS = 9


def constants():
    c = np.zeros((P, C_ALL), np.float32)
    i = np.arange(P)
    same = lambda b: (i[:, None] // b == i[None, :] // b).astype(np.float32)
    c[:, C_ID:C_ID + P] = np.eye(P)
    c[:, C_BO:C_BO + P] = same(RH)
    c[:, C_BM:C_BM + P] = same(RH) / RH
    for n in range(LEVELS):
        both = same(1 << n) - same(2 << n)
        c[:, C_LV + n * HALF:C_LV + (n + 1) * HALF] = np.concatenate([both[:HALF, :HALF]] * 2)
    c[:, C_I2:C_I2 + HALF] = np.concatenate([np.eye(HALF)] * 2)
    s, t = i[:, None], i[None, :]
    for d, (excl, incl) in enumerate([(s < t, s <= t), (s > t, s >= t)]):
        c[:, C_TRI + d * 256:C_TRI + d * 256 + P] = excl
        c[:, C_TRI + d * 256 + P:C_TRI + (d + 1) * 256] = incl
    half = HD // 2
    inv = (np.float32(1.0) / (np.float32(10000.0) ** (np.arange(0, half, 2, dtype=np.float32) / np.float32(half))))
    ar = (i // 64).astype(np.float32)[:, None] * inv
    ac = (i % 64).astype(np.float32)[:, None] * inv
    ang = np.concatenate([ar, ar, ac, ac], axis=-1).astype(np.float32)
    sign = np.repeat(np.array([-1, 1, -1, 1], np.float32), 32)
    c[:, C_COS:C_COS + P] = np.cos(ang)
    c[:, C_SIN:C_SIN + P] = np.sin(ang) * sign
    for row in range(4):
        c[row, C_SELT + row % 2] = 1
    c[:, C_ONE:C_ONE + P] = 1
    c[:, C_HALF] = -0.5
    return c


def hybrid_trunk(nc, A, O):
    ctx = ExitStack()
    with ctx:
        def sb(name, shape, dt=F32, at=ctx):
            return at.enter_context(nc.sbuf_tensor(name, shape, dt))

        def sem(name):
            return ctx.enter_context(nc.semaphore(name))

        x = sb("x", [P, 2, D])
        actH = sb("actH", [P, KT, 256], F32R)
        actL = sb("actL", [P, KT, 256], F32R)
        with ExitStack() as over:
            loW = sb("loW", [P, SLOTS, 2, NW], F32R, over)
        rawW = sb("rawW", [P, SLOTS, 2, NW])
        hiW = sb("hiW", [P, LEAD, 2, NW], F32R)
        con = sb("con", [P, C_ALL])
        col = sb("col", [P, COLS])
        muh = sb("muh", [P, 14])
        omu = sb("omu", [P, 14])
        oka = sb("oka", [P, 4])
        wla = sb("wla", [64, 2, D_RW])
        wg = sb("wg", [GATE_RANK, D_RW])
        ctxk = sb("ctxk", [P, NKV, HD])
        ctxv = sb("ctxv", [P, NKV, HD])
        qkw = sb("qkw", [P, 2, HD])
        s0all = sb("s0all", [P, 2, FT, RH])
        s0bd = sb("s0bd", [P, 2, P])
        csR = sb("csR", [P, 192], F32R)
        modT = sb("modT", [P, 6, KT, 2])
        st = sb("st", [P, 8])
        ss, ms, rstd = st[:, 0:2], st[:, 2:4], st[:, 4:6]
        bank = [ctx.enter_context(nc.psum_tensor(f"bank{i}", [P, NW], F32)) for i in range(8)]

        ident = con[:, C_ID:C_ID + P]
        blk1 = con[:, C_BO:C_BO + P]
        blkm = con[:, C_BM:C_BM + P]
        ones = con[:, C_ONE:C_ONE + P]
        mhalf = con[:, C_HALF:C_HALF + 1]

        with ExitStack() as ph:
            prm = sb("prm", [P, 3, P], F32, ph)
            rows1 = sb("rows1", [4, 2, NW], F32, ph)
            xs1 = sb("xs1", [P, 2, D], F32, ph)
            tf1 = sb("tf1", [P, 2, NW], F32, ph)
            csf = sb("csf", [P, 3, P], F32, ph)
        with ExitStack() as ph:
            uT = sb("uT", [P, 14, 2, 130], F32, ph)
            with ExitStack() as ph2:
                proj = sb("proj", [P, 2, D_IN], F32, ph2)
                qk = sb("qk", [P, 10, HD], F32, ph2)
                scr = sb("scr", [P, 20, HD], F32, ph2)
                qst = sb("qst", [P, 124], F32, ph2)
                with ExitStack() as ph3:
                    chT = sb("chT", [P, 2, 4, P], F32, ph3)
                    mT = sb("mT", [P, 4, 2, 130], F32, ph3)
                    cv = sb("cv", [P, 4, 2, P], F32, ph3)
                with ExitStack() as ph3:
                    qT = sb("qT", [P, NH, P], F32, ph3)
                    kT = sb("kT", [P, NKV, 256], F32, ph3)
                    pr = sb("pr", [P, NH, 256], F32, ph3)
            with ExitStack() as ph2:
                tmp3 = sb("tmp3", [P, 3, 2, P], F32, ph2)
                rkv = sb("rkv", [P, 3, 2, P], F32, ph2)
                kk = sb("kk", [P, 2, P], F32, ph2)
                ksq = sb("ksq", [P, 2, P], F32, ph2)
                nrm = sb("nrm", [P, 2, P], F32, ph2)
                xwa = sb("xwa", [64, 2, P], F32, ph2)
                xg = sb("xg", [GATE_RANK, 2, P], F32, ph2)
                wS = sb("wS", [64, 2, P], F32, ph2)
                gS = sb("gS", [GATE_RANK, P], F32, ph2)
                sa_ = sb("sigaa", [P, 4, 2, P], F32, ph2)
                gT = sb("gT", [P, 2, P], F32, ph2)
                cs = sb("cs", [P, 2, 2, 129], F32, ph2)
                E1 = sb("E1", [P, 2, 2, 129], F32, ph2)
                E2 = sb("E2", [P, 2, 2, 129], F32, ph2)
                amid = sb("amid", [P, 8], F32, ph2)
                kd = sb("kd", [P, 2, 2, P], F32, ph2)
                KR = sb("KR", [P, 2, 2, 2, P], F32, ph2)
                be = sb("be", [P, 2, 2, P], F32, ph2)
                ga = sb("ga", [P, 2, 2, P], F32, ph2)
                AE = sb("AE", [P, 2, 4, 256], F32, ph2)
                BF = sb("BF", [P, 2, 4, 256], F32, ph2)
                AC = sb("AC", [P, 2, 4, HALF], F32, ph2)
                X = sb("X", [P, 2, 4, P], F32, ph2)
                CT = sb("CT", [P, 2, 4, HALF], F32, ph2)
                U = sb("U", [P, 2, 4, HALF], F32, ph2)
                rows3 = sb("rows3", [4, NW], F32, ph2)
                Rs = sb("Rs", [P, 4, P], F32, ph2)
                SA = sb("SA", [P, 4, P], F32, ph2)
                Vt = sb("Vt", [P, 2, P], F32, ph2)
                S0s = sb("S0s", [P, 2, P], F32, ph2)
                STs = sb("STs", [P, 2, RH], F32, ph2)
        with ExitStack() as ph:
            o = sb("o", [P, 2, D], F32, ph)
            with ExitStack() as ph2:
                xs2 = sb("xs2", [P, 2, D], F32, ph2)
                tf2 = sb("tf2", [P, 2, NW], F32, ph2)
            with ExitStack() as ph2:
                sg = sb("sg", [P, 2, NW], F32, ph2)
                ff = sb("ff", [P, 2, NW], F32, ph2)
                ffH = sb("ffH", [P, 4, 256], F32R, ph2)
                ffL = sb("ffL", [P, 4, 256], F32R, ph2)
        qc, qs = scr[:, 0:10], scr[:, 10:20]
        pT = scr[:, 0:16].rearrange("p (k h) t -> p k h t", k=2)
        sig = [sa_[:, d].rearrange("p g t -> p (g t)") for d in range(2)]
        aa = [sa_[:, 2 + d].rearrange("p g t -> p (g t)") for d in range(2)]
        yy = sig + aa
        bg0 = kd
        bgt = cs[:].rearrange("p d g t -> p (d g t)")[:, 0:4 * P].rearrange("p (d n j) -> p d n j", d=2, n=2)

        passed = sem("passed")
        con_in, c_in, x_in = sem("con_in"), sem("c_in"), sem("x_in")
        cs_done = sem("cs_done")
        raw_full = [sem(f"raw_full{n}") for n in range(SLOTS)]
        hi_ready, lo_ready = sem("hi_ready"), sem("lo_ready")
        chunk_used = sem("chunk_used")
        rows_out, ada_post = sem("rows_out"), sem("ada_post")
        evac_v, evac_s = sem("evac_v"), sem("evac_s")
        par_rows, par_tabs = sem("par_rows"), sem("par_tabs")
        prm_zero, cols_T = sem("prm_zero"), sem("cols_T")
        end_pe, end_act, end_dve, end_pool = sem("end_pe"), sem("end_act"), sem("end_dve"), sem("end_pool")
        vsteps, fsteps = sem("vsteps"), sem("fsteps")
        sq_in, ms_in, rs_in, xs_in = sem("sq_in"), sem("ms_in"), sem("rs_in"), sem("xs_in")
        nt_T, nt_f, nt_hi, nt_lo = sem("nt_T"), sem("nt_f"), sem("nt_hi"), sem("nt_lo")
        rg_m, rg_T = sem("rg_m"), sem("rg_T")
        rr_v, rp_T = sem("rr_v"), sem("rp_T")
        ac_v, rw_S1, rw_S1s, rw_W2, rw_R2 = (sem(n) for n in ("ac_v", "rw_S1", "rw_S1s", "rw_W2", "rw_R2"))
        cv_T, cv_ch, cv_z, cv_out, cv_hi = sem("cv_T"), sem("cv_ch"), sem("cv_z"), sem("cv_out"), sem("cv_hi")
        at_ms, at_rs, at_qk, at_T = sem("at_ms"), sem("at_rs"), sem("at_qk"), sem("at_T")
        at_ca, at_cv, at_S, at_mx = sem("at_ca"), sem("at_cv"), sem("at_S"), sem("at_mx")
        at_P, at_Pn, at_PT, at_pa, at_pv = sem("at_P"), sem("at_Pn"), sem("at_PT"), sem("at_pa"), sem("at_pv")
        at_O, at_hi, kv_out = sem("at_O"), sem("at_hi"), sem("kv_out")
        u_T, at_lo = sem("u_T"), sem("at_lo")
        lr_mix, lr_act, ab_z = sem("lr_mix"), sem("lr_act"), sem("ab_z")
        rw_v, rw_sq, rw_nrm, rw_ns, rw_rs = sem("rw_v"), sem("rw_sq"), sem("rw_nrm"), sem("rw_ns"), sem("rw_rs")
        rw_stage, rw_lr, rw_sig, rw_aa = sem("rw_stage"), sem("rw_lr"), sem("rw_sig"), sem("rw_aa")
        rw_s0, rw_VS, rw_Vt, rw_c, rw_E = sem("rw_s0"), sem("rw_VS"), sem("rw_Vt"), sem("rw_c"), sem("rw_E")
        rw_kr, rw_A, rw_m, rw_S0s = sem("rw_kr"), sem("rw_A"), sem("rw_m"), sem("rw_S0s")
        rw_bo, rw_bon, rw_bg, rw_bgT, rw_bgs = sem("rw_bo"), sem("rw_bon"), sem("rw_bg"), sem("rw_bgT"), sem("rw_bgs")
        rw_mA = sem("rw_mA")
        rw_bv, rw_lo = sem("rw_bv"), sem("rw_lo")
        rw_R, rw_Rs, rw_SA, rw_SAs = sem("rw_R"), sem("rw_Rs"), sem("rw_SA"), sem("rw_SAs")
        lv_X0, lv_C, lv_U, lv_Us, lv_XM, lv_X = (sem(n) for n in ("lv_X0", "lv_C", "lv_U", "lv_Us", "lv_XM", "lv_X"))
        rw_Y, rw_ST, rw_y, rw_mean, rw_yc, rw_y2 = (sem(n) for n in ("rw_Y", "rw_ST", "rw_y", "rw_mean", "rw_yc", "rw_y2"))
        rw_var, rw_vs, rw_vr, rw_o, rw_hi = (sem(n) for n in ("rw_var", "rw_vs", "rw_vr", "rw_o", "rw_hi"))
        ST_v, st_out, y_out = sem("ST_v"), sem("st_out"), sem("y_out")
        ff_s, ff_g, ff_u, ff_T, ff_hi, ff_lo, dn_out = (sem(n) for n in (
            "ff_s", "ff_g", "ff_u", "ff_T", "ff_hi", "ff_lo", "dn_out"))
        ENDS = {"pe": end_pe, "act": end_act, "dve": end_dve, "pool": end_pool}

        AB_BANK = (((4, 5), (6, 0)), ((1, 2), (3, 4)))
        halves = ((slice(0, HALF), slice(HALF, P)), (slice(HALF, P), slice(0, HALF)))

        def settle(eng):
            eng.sem_inc(passed, 1)

        def phase_end(eng, who, l, k):
            settle(eng)
            eng.drain().then_inc(ENDS[who], 1)
            for name, s in ENDS.items():
                if name != who:
                    eng.wait_ge(s, l * BARS + k + 1)
            settle(eng)

        class Steps:

            def __init__(self, eng, s, per):
                self.eng, self.s, self.per, self.n = eng, s, per, 0

            def start(self, it):
                self.base, self.n = it * self.per, 0

            def mark(self, ins):
                ins.then_inc(self.s, 1)
                self.n += 1

            def sync(self):
                self.eng.wait_ge(self.s, self.base + self.n)

            def step(self, ins):
                self.mark(ins)
                self.sync()

            def end(self):
                assert self.n == self.per, (self.n, self.per)

        def col1(c):
            return col[:, c:c + 1]

        def dyn(ap, start, size):
            return ap[:, bass.ds(start, size)]

        block = ctx.enter_context(nc.Block())

        @block.sync
        def _(sp):
            sp.dma_start(con[:], A["consts"]).then_inc(con_in, 16)
            sp.dma_start(csf[0:KT, 0, :], A["c_ctx"].rearrange("(k p) -> k p", p=P)).then_inc(c_in, 16)
            sp.dma_start(csf[KT:2 * KT, 0, :], A["c"][0].rearrange("(k p) -> k p", p=P)).then_inc(c_in, 16)
            sp.dma_start(x[:, 0, :], A["x_prompt"][0]).then_inc(x_in, 16)
            sp.dma_start(x[:, 1, :], A["x_sample"][0]).then_inc(x_in, 16)

            def load(q, c, src, width=NW):
                sp.wait_ge(chunk_used, q * 4 + (c + 1))
                sp.dma_start(rawW[:, c % SLOTS, :, 0:width], src).then_inc(raw_full[c % SLOTS], 16)

            def load_tile(q, w, n0, width=NW):
                for c in range(CPT):
                    load(q, c, w[:, 2 * c:2 * c + 2, bass.ds(n0, width)], width)

            def load_down(q, w, j):
                for c in range(2 * OUT_TILES):
                    n0 = (c // 2) * NW
                    load(q, c, w[:, bass.ds(j * 4 + 2 * (c % 2), 2), n0:n0 + NW])

            with sp.Fori(0, LAYERS) as l:
                wada, win, wout, wgate, wup, wdown = (A[n][l].rearrange("(k p) n -> p k n", p=P) for n in (
                    "w_ada", "w_in", "w_out", "w_gate", "w_up", "w_down"))
                ql = l * Q_LAYER
                with sp.Fori(0, 8) as i:
                    load_tile(ql + Q_ADA01 + i * 2, wada, i * NW)
                with sp.Fori(0, WIN_TILES - 1) as i:
                    load_tile(ql + Q_WIN + i * 2, win, i * NW)
                load_tile(ql + Q_WIN + (WIN_TILES - 1) * 2, win, (WIN_TILES - 1) * NW, WIN_LAST)
                with sp.Fori(0, 16) as i:
                    load_tile(ql + Q_ADA2 + i * 2, wada, i * NW + 2 * D)
                with sp.Fori(0, OUT_TILES) as i:
                    load_tile(ql + Q_WOUT + i * 2, wout, i * NW)
                load_tile(ql + Q_FFN, wgate, 0)
                load_tile(ql + Q_FFN + 2, wup, 0)
                with sp.Fori(1, FF_TILES) as j:
                    qb = ql + (Q_FFN - 2) + j * 6
                    load_tile(qb, wgate, j * NW)
                    load_tile(qb + 2, wup, j * NW)
                    load_down(qb + 4, wdown, j - 1)
                load_down(ql + (Q_FFN + 4 + 6 * (FF_TILES - 1)), wdown, FF_TILES - 1)

        @block.scalar
        def _(act):
            def hi(q, c0, c1, width=NW):
                for c in range(c0, c1):
                    act.wait_ge(raw_full[c % SLOTS], q * 8 + 16 * (c // SLOTS + 1))
                    act.wait_ge(chunk_used, q * 4 + (c + 1 + SLOTS - LEAD))
                    act.activation(hiW[:, c % LEAD, :, 0:width], rawW[:, c % SLOTS, :, 0:width],
                                   ACT.Copy).then_inc(hi_ready, 1)

            def tile_done(q):
                act.wait_ge(chunk_used, q * 4 + (CPT + SLOTS))

            def evac(q, out, b, width=NW):
                tile_done(q)
                act.activation(out, bank[b][:, 0:width], ACT.Copy).then_inc(evac_s, 1)

            def ada(q):
                hi(q, 4, 12)
                hi(q + 2, 4, 12)

            def squares(xs, src):
                for g in range(2):
                    act.activation(xs[:, g], src[:, g], ACT.Square, accum_out=ss[:, g:g + 1]).then_inc(sq_in, 1)

            def norm(it, tf):
                for b in range(8):
                    g, kq = b % 2, b // 2
                    act.wait_ge(nt_f, it * 8 + (b + 1))
                    act.activation(actH[:, 4 * kq:4 * kq + 4, g * P:(g + 1) * P],
                                   tf[:, b % 2].rearrange("p (k t) -> p k t", k=4), ACT.Copy).then_inc(nt_hi, 1)

            def parameters(l):
                act.wait_ge(prm_zero, l + 1)
                put = lambda dst, src: act.dma_start(dst, src).then_inc(par_rows, 16)
                row = lambda ap: ap.rearrange("(r c) -> r c", c=P)
                mu = A["rwkv_mu"][l]
                put(prm[0:12, 0, :], row(mu[0:12 * P]))
                put(prm[12:13, 0, 0:64], mu[12 * P:12 * P + 64].unsqueeze(0))
                put(prm[13:14, 0, 0:GATE_RANK], mu[12 * P + 64:D_RWIN].unsqueeze(0))
                for c, name in ((COL_W0, "rwkv_w0"), (COL_A0, "rwkv_a0")):
                    put(prm[c:c + 8, 0, :], A[name][l].rearrange("d (r c) -> (d r) c", c=P))
                for c, name in ((COL_KK, "rwkv_k_k"), (COL_KA, "rwkv_k_a"), (COL_LG, "rwkv_ln_g"), (COL_LB, "rwkv_ln_b")):
                    put(prm[c:c + 4, 0, :], row(A[name][l]))
                put(prm[COL_RK:COL_RK + 4, 0, :], A["rwkv_r_k"][l].rearrange("(r a) b -> r (a b)", a=2))
                put(prm[COL_CV:COL_CV + 12, 0, :], A["conv_w"][l].rearrange("w (r c) -> (w r) c", c=P))
                put(prm[0:64, 1, :], A["norm_g"][l].rearrange("n (r c) -> (n r) c", c=P))
                put(prm[0:96, 2, :], row(A["b_ada"][l]))
                put = lambda dst, src: act.dma_start(dst, src).then_inc(par_tabs, 16)
                put(wla[0:32], A["rwkv_w_up"][l].rearrange("d r n -> r d n"))
                put(wla[32:64], A["rwkv_a_up"][l].rearrange("d r n -> r d n"))
                put(wg[:], A["rwkv_g_up"][l])
                put(ctxk[:], A["cache_k"][0][l])
                put(ctxv[:], A["cache_v"][0][l])
                put(qkw[:, 0], A["q_norm"][l].partition_broadcast(P))
                put(qkw[:, 1], A["k_norm"][l].partition_broadcast(P))
                for d in range(2):
                    put(s0all[:, d], A["state_rwkv"][0][l][d].rearrange("(f h) i j -> (h i) f j", h=2))

            def conv(l):
                for g in range(2):
                    act.wait_ge(cv_T, l * 6 + (g + 1))
                    act.activation(chT[:, g], bank[4 + g][:].rearrange("p (f t) -> p f t", f=4), ACT.Copy).then_inc(cv_ch, 1)
                for g in range(2):
                    act.wait_ge(cv_out, l * 2 + (g + 1))
                    act.activation(actH[:, 8:12, g * P:(g + 1) * P], cv[:, :, g], ACT.Copy).then_inc(cv_hi, 1)

            def attention(l, g):
                it = l * 2 + g
                nk = P if g == 0 else 2 * P
                if g == 0:
                    act.wait_ge(at_qk, it + 1)
                    act.dma_start(O["new_k"][0][l], qk[:, NH:NH + NKV]).then_inc(kv_out, 16)
                    act.dma_start(O["new_v"][0][l], proj[:, 0, D_QK:D_ATT].rearrange("p (h d) -> p h d", h=NKV)).then_inc(kv_out, 16)
                act.wait_ge(at_T, it * 3 + 1)
                act.activation(qT[:, 0:4], bank[0][:].rearrange("p (h t) -> p h t", h=4), ACT.Copy).then_inc(at_ca, 1)
                act.wait_ge(at_T, it * 3 + 3)
                act.activation(kT[:, :, 0:nk].rearrange("p v (s t) -> p s v t", t=P),
                               bank[2][:, 0:2 * nk].rearrange("p (s v t) -> p s v t", v=2, t=P), ACT.Copy).then_inc(at_ca, 1)
                act.wait_ge(at_mx, it + 1)
                for h in range(NH):
                    e = act.activation(pr[:, h, 0:nk], bank[3 + h // 2][:, (h % 2) * 256:(h % 2) * 256 + nk], ACT.Exp,
                                       bias=qst[:, 40 + h:41 + h], scale=SCALE, accum_out=qst[:, 48 + h:49 + h])
                e.then_inc(at_P, 1)
                act.wait_ge(at_PT, it * 2 + 1)
                for k in range(nk // P):
                    e = act.activation(pT[:, k, 0:4], bank[2 * k][:].rearrange("p (h t) -> p h t", h=4), ACT.Copy)
                e.then_inc(at_pa, 1)
                for v in range(NKV):
                    act.wait_ge(at_O, it * 2 + (v + 1))
                    act.activation(actH[:, 4 * v:4 * v + 4, g * P:(g + 1) * P],
                                   bank[4 + v][:].rearrange("p (h t) -> p h t", h=4), ACT.Copy).then_inc(at_hi, 1)
                if g == 0:
                    act.wait_ge(kv_out, l * 32 + 32)

            def turn_u(l):
                for b in range(3):
                    act.wait_ge(u_T, l * 7 + (b + 1))
                    act.activation(uT[:, 4 * b:4 * b + 4, 0, 1:129], bank[b][:].rearrange("p (f t) -> p f t", f=4), ACT.Copy)
                act.wait_ge(u_T, l * 7 + 7)
                act.activation(uT[0:64, 12, :, 1:129], bank[4][0:64, 0:256].rearrange("p (g t) -> p g t", g=2), ACT.Copy)
                act.activation(uT[0:GATE_RANK, 13, :, 1:129],
                               bank[4][0:GATE_RANK, 256:512].rearrange("p (g t) -> p g t", g=2), ACT.Copy)

            def rwkv(l):
                act.wait_ge(lr_mix, l + 1)
                act.activation(xwa[0:32], xwa[0:32], ACT.Tanh)
                act.activation(xg[:], xg[:], ACT.Sigmoid).then_inc(lr_act, 1)
                with act.Fori(0, FT) as f:
                    it = act.snap(l * FT + f)
                    qa = act.snap(l * Q_LAYER + Q_ADA2 + f * 8)
                    act.activation(wS[:], wla[:, :, bass.ds(f * P, P)], ACT.Copy)
                    act.activation(gS[:], wg[:, bass.ds(f * P, P)], ACT.Copy).then_inc(rw_stage, 1)
                    act.wait_ge(rw_lo, it + 1)
                    act.wait_ge(rw_lr, it + 1)
                    for d in range(2):
                        e = act.activation(sig[d], bank[1][:, d * 256:(d + 1) * 256], ACT.Sigmoid,
                                           bias=dyn(col, f + (COL_W0 + 4 * d), 1))
                    e.then_inc(rw_sig, 1)
                    for d in range(2):
                        e = act.activation(aa[d], bank[2][:, d * 256:(d + 1) * 256], ACT.Sigmoid,
                                           bias=dyn(col, f + (COL_A0 + 4 * d), 1))
                    e.then_inc(rw_aa, 1)
                    act.wait_ge(rw_ns, it + 1)
                    act.activation(ksq[:], nrm[:], ACT.Sqrt).then_inc(rw_rs, 1)
                    act.wait_ge(rw_VS, it + 1)
                    act.activation(Vt[:], bank[3][:, 0:256].rearrange("p (g c) -> p g c", g=2), ACT.Copy).then_inc(rw_Vt, 1)
                    act.wait_ge(rw_c, it + 1)
                    for d in range(2):
                        for g in range(2):
                            n = 2 * d + g
                            act.activation(E1[:, d, g], cs[:, d, g], ACT.Exp, bias=amid[:, n:n + 1], scale=-ALPHA)
                            e = act.activation(E2[:, d, g], cs[:, d, g], ACT.Exp, bias=amid[:, 4 + n:5 + n], scale=ALPHA)
                    e.then_inc(rw_E, 1)
                    hi(qa, 4, 8)
                    act.wait_ge(rw_R, it + 1)
                    act.activation(Rs[:], bank[6][:].rearrange("p (n i) -> p n i", n=4), ACT.Copy).then_inc(rw_Rs, 1)
                    hi(qa, 8, 12)

                    def levels(n, q, first=False):
                        for w in range(2):
                            for d in range(2):
                                if w or not first:
                                    act.wait_ge(lv_U, n + (2 * w + d + 3))
                                    act.activation(U[:, d], bank[d][:, 0:4 * HALF].rearrange("p (s t) -> p s t", s=4),
                                                   ACT.Copy).then_inc(lv_Us, 1)
                            hi(q, 4 + 4 * w, 8 + 4 * w)
                            if w == 0 and first:
                                act.wait_ge(rw_bgT, it + 1)
                                act.activation(bgt, bank[7][:].rearrange("p (d n j) -> p d n j", d=2, n=2),
                                               ACT.Copy).then_inc(rw_bgs, 1)

                    levels(it * (2 * LEVELS), qa + 2, first=True)
                    with act.Fori(1, LEVELS // 2) as v:
                        levels(act.snap(it * (2 * LEVELS) + v * 4), act.snap(qa + 2 + v * 2))
                    for half, (done, said) in enumerate(((rw_S1, rw_S1s), (rw_SA, rw_SAs))):
                        act.wait_ge(done, it + 1)
                        for d in range(2):
                            hs = halves[d][half]
                            e = act.activation(SA[hs, 2 * d:2 * d + 2], bank[7][hs, 2 * d * P:(2 * d + 2) * P].rearrange(
                                "p (n i) -> p n i", n=2), ACT.Copy, scale=-1.0)
                        e.then_inc(said, 1)
                    act.wait_ge(rw_ST, it + 1)
                    act.activation(STs[:], bank[1][:, 0:2 * RH].rearrange("p (d j) -> p d j", d=2), ACT.Copy).then_inc(ST_v, 1)
                    act.wait_ge(ST_v, it + 1)
                    for d in range(2):
                        act.dma_start(O["new_rwkv"][0][l][d].rearrange("(f h) i j -> f (h i) j", h=2)[f],
                                      STs[:, d]).then_inc(st_out, 16)
                    act.wait_ge(rw_yc, it + 1)
                    act.activation(yy[1], yy[0], ACT.Square).then_inc(rw_y2, 1)
                    act.wait_ge(rw_vs, it + 1)
                    act.activation(yy[3], yy[2], ACT.Sqrt).then_inc(rw_vr, 1)
                    act.wait_ge(rw_o, it + 1)
                    act.activation(actH[:, bass.ds(f + 12, 1), :], yy[0].unsqueeze(1), ACT.Copy).then_inc(rw_hi, 1)
                    act.wait_ge(st_out, it * 32 + 32)
                    settle(act)

            def ffn(l):
                ql = l * Q_LAYER

                def gate(q, j):
                    tile_done(q)
                    for g in range(2):
                        act.activation(sg[:, g], bank[g][:], ACT.Sigmoid).then_inc(ff_s, 1)

                def turned(j):
                    for g in range(2):
                        act.wait_ge(ff_T, l * (2 * FF_TILES) + j * 2 + (g + 1))
                        act.activation(ffH[:, :, g * P:(g + 1) * P],
                                       bank[4 + g][:].rearrange("p (k t) -> p k t", k=4), ACT.Copy).then_inc(ff_hi, 1)

                hi(ql + Q_FFN, 4, 12)
                gate(ql + Q_FFN, 0)
                hi(ql + Q_FFN + 2, 4, 12)
                with act.Fori(1, FF_TILES) as j:
                    qb = act.snap(ql + (Q_FFN - 2) + j * 6)
                    hi(qb, 4, 12)
                    act.wait_ge(ff_u, l * FF_TILES + j)
                    gate(qb, j)
                    turned(j - 1)
                    hi(qb + 2, 4, 12)
                    hi(qb + 4, 4, 12)
                turned(FF_TILES - 1)
                hi(ql + (Q_FFN + 4 + 6 * (FF_TILES - 1)), 4, 8)

            act.wait_ge(c_in, 32)
            act.activation(csf[0:2 * KT, 1], csf[0:2 * KT, 0], ACT.Sigmoid).then_inc(cs_done, 1)
            act.wait_ge(cs_done, 4)
            csv = csR[:, 0:4 * KT].rearrange("p (k c) -> p c k", c=4)
            act.activation(csv[:, 0:2], bank[0][:, 0:2 * KT].rearrange("p (g k) -> p g k", g=2), ACT.Copy).then_inc(cs_done, 1)
            act.wait_ge(x_in, 32)
            with act.Fori(0, LAYERS) as l:
                ql = act.snap(l * Q_LAYER)
                hi(ql, 0, 4)
                squares(xs1, x)
                ada(ql + Q_ADA01)
                parameters(l)
                with act.Fori(1, 4) as i:
                    ada(act.snap(ql + Q_ADA01 + i * 4))
                phase_end(act, "act", l, 0)
                norm(l * 2, tf1)
                with act.Fori(0, 4) as i:
                    q = act.snap(ql + Q_WIN + i * 4)
                    hi(q, 4, 12)
                    evac(q, proj[:, 1, bass.ds(i * (2 * NW), NW)], 1)
                    hi(q + 2, 4, 12)
                    evac(q + 2, proj[:, 1, bass.ds(i * (2 * NW) + NW, NW)], 3)
                q = ql + Q_WIN + 16
                hi(q, 4, 8)
                hi(q, 8, 12, WIN_LAST)
                evac(q, proj[:, 1, 8 * NW:9 * NW], 1)
                hi(q + 2, 4, 8, WIN_LAST)
                hi(q + 2, 8, 12)
                evac(q + 2, proj[:, 1, 9 * NW:D_IN], 3, WIN_LAST)
                phase_end(act, "act", l, 1)
                act.wait_ge(par_tabs, l * (9 * 16) + 9 * 16)
                conv(l)
                for g in range(2):
                    attention(l, g)
                    if g == 0:
                        phase_end(act, "act", l, 2)
                turn_u(l)
                phase_end(act, "act", l, 3)
                rwkv(l)
                phase_end(act, "act", l, 4)
                for i in range(2):
                    q = ql + Q_WOUT + i * 4
                    hi(q, 4, 12)
                    evac(q, o[:, 1, 2 * i * NW:(2 * i + 1) * NW], 1)
                    hi(q + 2, 4, 12)
                    evac(q + 2, o[:, 1, (2 * i + 1) * NW:(2 * i + 2) * NW], 3)
                phase_end(act, "act", l, 5)
                squares(xs2, o)
                phase_end(act, "act", l, 6)
                squares(xs2, x)
                norm(l * 2 + 1, tf2)
                ffn(l)
                phase_end(act, "act", l, 7)
                squares(xs2, o)
                phase_end(act, "act", l, 8)
            act.dma_start(O["y_prompt"][0], x[:, 0, :]).then_inc(y_out, 16)
            act.dma_start(O["y_sample"][0], x[:, 1, :]).then_inc(y_out, 16)
            act.wait_ge(y_out, 32)

        @block.gpsimd
        def _(pool):
            def power(out, in_):
                n = in_.shape[1]
                return pool.tensor_tensor(out, in_, mhalf.to_broadcast([P, n]), ALU.pow)

            def stats(n, l):
                pool.wait_ge(ms_in, l * 4 + (n + 1))
                power(rstd, ms).then_inc(rs_in, 1)

            pool.wait_ge(con_in, 16)
            pool.memset(s0bd[:], 0.0).then_inc(rw_s0, 1)
            with pool.Fori(0, LAYERS) as l:
                pool.wait_ge(sq_in, l * 8 + 2)
                settle(pool)
                pool.tensor_scalar(ms, ss, 1.0 / D, EPS, ALU.mult, ALU.add).then_inc(ms_in, 1)
                stats(0, l)
                pool.wait_ge(rs_in, l * 4 + 1)
                settle(pool)
                for g in range(2):
                    pool.tensor_scalar(xs1[:, g], x[:, g], rstd[:, g:g + 1], None, ALU.mult).then_inc(xs_in, 1)
                phase_end(pool, "pool", l, 0)
                phase_end(pool, "pool", l, 1)
                pool.memset(mT[:], 0.0).then_inc(cv_z, 1)
                pool.wait_ge(at_ms, l + 1)
                power(qst[:, 104:124], qst[:, 84:104]).then_inc(at_rs, 1)
                phase_end(pool, "pool", l, 2)
                pool.memset(uT[:, :, :, 0:1], 0.0)
                pool.memset(uT[:, :, :, 129:130], 0.0)
                phase_end(pool, "pool", l, 3)
                pool.memset(AE[:], 0.0)
                pool.memset(BF[:], 0.0).then_inc(ab_z, 1)
                pool.wait_ge(ab_z, l + 1)
                settle(pool)
                with pool.Fori(0, FT) as f:
                    it = pool.snap(l * FT + f)
                    for h in range(2):
                        hs = slice(RH * h, RH * h + RH)
                        e = pool.tensor_copy(s0bd[hs, :, hs], s0all[hs, :, bass.ds(f, 1), :].rearrange("p d f j -> p (d f) j"))
                    e.then_inc(rw_s0, 1)
                    pool.wait_ge(rw_s0, it + 2)
                    unit = con[:, C_I2:C_I2 + HALF].unsqueeze(1).broadcast_to([P, 4, HALF])
                    pool.wait_ge(rw_v, it + 1)
                    settle(pool)
                    for d in range(2):
                        pool.tensor_copy(X[:, d, :, 0:HALF], unit)
                    for d in range(2):
                        pool.wait_ge(rw_mA, it * 2 + (d + 1))
                        for k, hs in enumerate(halves[0]):
                            settle(pool)
                            pool.tensor_copy(AC[hs, d], AE[hs, d, :, hs]).then_inc(ac_v, 1)
                            pool.wait_ge(ac_v, it * 4 + (2 * d + k + 1))
                    settle(pool)
                    for d in range(2):
                        pool.tensor_tensor(CT[:, d], AC[:, d],
                                           con[:, C_LV:C_LV + HALF].unsqueeze(1).broadcast_to([P, 4, HALF]),
                                           ALU.mult).then_inc(lv_C, 1)
                    pool.wait_ge(lv_C, it * (2 * LEVELS) + 2)
                    settle(pool)
                    for d in range(2):
                        e = pool.tensor_tensor(X[:, d, :, HALF:P], CT[:, d], unit, ALU.add)
                    e.then_inc(lv_X0, 1)
                    pool.wait_ge(lv_X0, it + 1)
                    settle(pool)
                    with pool.Fori(1, LEVELS) as v:
                        n = pool.snap(it * (2 * LEVELS) + v * 2)
                        for d in range(2):
                            pool.wait_ge(lv_U, n + (d + 1))
                            settle(pool)
                            pool.tensor_tensor(CT[:, d], AC[:, d],
                                               con[:, bass.ds(v * HALF + C_LV, HALF)].unsqueeze(1).broadcast_to([P, 4, HALF]),
                                               ALU.mult).then_inc(lv_C, 1)
                    pool.wait_ge(lv_C, it * (2 * LEVELS) + 2 * LEVELS)
                    settle(pool)
                phase_end(pool, "pool", l, 4)
                phase_end(pool, "pool", l, 5)
                stats(1, l)
                phase_end(pool, "pool", l, 6)
                pool.memset(o[:], 0.0)
                stats(2, l)
                phase_end(pool, "pool", l, 7)
                stats(3, l)
                phase_end(pool, "pool", l, 8)

        @block.tensor
        def _(pe):
            def mm(out, a, b, start=True, stop=True):
                return pe.matmul(out, a, b, start=start, stop=stop, skip_group_check=True)

            def gemm(q, banks, width=NW, normed=None):
                for c in range(CPT):
                    if normed is not None:
                        pe.wait_ge(nt_lo, normed + 2 * (c // 2) + 2)
                    pe.wait_ge(lo_ready, q * 4 + (c + 1 + LEAD))
                    for n in range(2):
                        k = 2 * c + n
                        for g in range(2):
                            out = bank[banks[g]][:, 0:width]
                            Hk, Lk = actH[:, k, g * P:(g + 1) * P], actL[:, k, g * P:(g + 1) * P]
                            mm(out, Hk, hiW[:, c % LEAD, n, 0:width], k == 0, False)
                            mm(out, Hk, loW[:, c % SLOTS, n, 0:width], False, False)
                            e = mm(out, Lk, hiW[:, c % LEAD, n, 0:width], False, k == KT - 1)
                    e.then_inc(chunk_used, 1)

            def free(l, t):
                pe.wait_ge(evac_v, l * (WIN_TILES + OUT_TILES) + (t + 1))
                pe.wait_ge(evac_s, l * (WIN_TILES + OUT_TILES) + (t + 1))

            def ada_chunks(q, c0, c1, b):
                for c in range(c0, c1):
                    pe.wait_ge(lo_ready, q * 4 + (c + 1 + LEAD))
                    for n in range(2):
                        k = 2 * c + n
                        mm(bank[b][:], csR[:, 4 * k:4 * k + P], hiW[:, c % LEAD, n], k == 0, False)
                        e = mm(bank[b][:], csR[:, 4 * k:4 * k + P], loW[:, c % SLOTS, n], False, k == KT - 1)
                    e.then_inc(chunk_used, 1)

            def turn_rows(rows, b):
                for j in range(4):
                    e = mm(bank[b][:, 2 * j:2 * j + 2], rows[:, j * P:(j + 1) * P], con[0:4, C_SELT:C_SELT + 2])
                return e

            def ada(q, a):
                for t in range(2):
                    pe.wait_ge(rows_out, a + (t + 1))
                    ada_chunks(q + 2 * t, 0, CPT, 2 * t)
                for t in range(2):
                    pe.wait_ge(rows_out, a + (t + 3))
                    turn_rows(rows1[0:4, t], 4 + t).then_inc(ada_post, 1)

            def residual(it, part):
                pe.wait_ge(rg_m, it + 1)
                for g in range(2):
                    for n in range(4):
                        for j in range(4):
                            e = mm(bank[4 * g + n][:, j * P:(j + 1) * P],
                                   modT[:, part, 4 * n + j, g:g + 1].broadcast_to([P, P]), ident)
                        e.then_inc(rg_T, 1)

            def norm(it, xs):
                for b in range(8):
                    g, kq = b % 2, b // 2
                    if b < 2:
                        pe.wait_ge(xs_in, it * 2 + (g + 1))
                    if b >= 4:
                        pe.wait_ge(nt_f, it * 8 + (b - 3))
                    for j in range(4):
                        e = pe.transpose(bank[4 + b % 4][:, j * P:(j + 1) * P], xs[:, g, (4 * kq + j) * P:(4 * kq + j + 1) * P], ident)
                    e.then_inc(nt_T, 1)

            def conv(l):
                for which, b0 in ((2, 4), (1, 2), (0, 0)):
                    for g in range(2):
                        for f in range(4):
                            c = OFF_CONV + which * D_CONV + f * P
                            e = pe.transpose(bank[b0 + g][:, f * P:(f + 1) * P], proj[:, g, c:c + P], ident)
                        e.then_inc(cv_T, 1)

            def attention(l, g):
                it = l * 2 + g
                pe.wait_ge(at_qk, it + 1)
                for b in range(2):
                    for j in range(4):
                        e = pe.transpose(bank[b][:, j * P:(j + 1) * P], qk[:, 4 * b + j], ident)
                    e.then_inc(at_T, 1)
                for v in range(NKV):
                    e = pe.transpose(bank[2][:, v * P:(v + 1) * P], qk[:, NH + v], ident)
                if g == 1:
                    for v in range(NKV):
                        e = pe.transpose(bank[2][:, (2 + v) * P:(3 + v) * P], ctxk[:, v], ident)
                e.then_inc(at_T, 1)
                nk = P if g == 0 else 2 * P
                pe.wait_ge(at_ca, it * 2 + 2)
                for h in range(NH):
                    if h == 4:
                        pe.wait_ge(at_cv, it + 1)
                    e = mm(bank[3 + h // 2][:, (h % 2) * 256:(h % 2) * 256 + nk], qT[:, h], kT[:, h // 4, 0:nk])
                    if h % 2:
                        e.then_inc(at_S, 1)
                pe.wait_ge(at_Pn, it + 1)
                for b in range(2):
                    for k in range(nk // P):
                        for j in range(4):
                            e = pe.transpose(bank[2 * k + b][:, j * P:(j + 1) * P], pr[:, 4 * b + j, k * P:(k + 1) * P], ident)
                    e.then_inc(at_PT, 1)
                for v in range(NKV):
                    pe.wait_ge((at_pa, at_pv)[v], it + 1)
                    for k in range(nk // P):
                        V = proj[:, g, D_QK + v * HD:D_QK + (v + 1) * HD] if k == 0 else ctxv[:, v]
                        e = mm(bank[4 + v][:], V, pT[:, k, 4 * v:4 * v + 4].rearrange("p h t -> p (h t)"), k == 0, k == nk // P - 1)
                    e.then_inc(at_O, 1)

            def turn_u(l):
                for g in range(2):
                    for b in range(3):
                        for j in range(4):
                            c = OFF_RW + (4 * b + j) * P
                            e = pe.transpose(bank[(0, 1, 2, 3, 6, 7)[3 * g + b]][:, j * P:(j + 1) * P],
                                             proj[:, g, c:c + P], ident)
                        e.then_inc(u_T, 1)
                pe.wait_ge(at_lo, l * 4 + 4)
                settle(pe)
                for g in range(2):
                    c = OFF_RW + 12 * P
                    pe.transpose(bank[4][0:64, g * P:(g + 1) * P], proj[:, g, c:c + 64], ident)
                    e = pe.transpose(bank[4][0:GATE_RANK, 256 + g * P:256 + (g + 1) * P], proj[:, g, c + 64:c + 160], ident)
                e.then_inc(u_T, 1)

            def rwkv(l):
                pe.wait_ge(lr_act, l + 1)
                settle(pe)
                with pe.Fori(0, FT) as f:
                    it = pe.snap(l * FT + f)
                    qa = pe.snap(l * Q_LAYER + Q_ADA2 + f * 8)
                    flat = lambda t: t.rearrange("p g t -> p (g t)")
                    pe.wait_ge(rw_stage, it + 1)
                    for d in range(2):
                        mm(bank[1][:, d * 256:(d + 1) * 256], wS[0:32, d], flat(xwa[0:32]))
                        mm(bank[2][:, d * 256:(d + 1) * 256], wS[32:64, d], flat(xwa[32:64]))
                    mm(bank[6][:, 0:256], gS[:], flat(xg[:])).then_inc(rw_lr, 1)
                    pe.wait_ge(rw_sq, it + 1)
                    mm(bank[0][:, 0:256], blk1, flat(ksq[:])).then_inc(rw_nrm, 1)
                    pe.wait_ge(rw_v, it + 1)
                    pe.wait_ge(rw_s0, it + 2)
                    for g in range(2):
                        pe.transpose(bank[3][:, g * P:(g + 1) * P], rkv[:, 2, g], ident)
                    for d in range(2):
                        e = pe.transpose(bank[3][:, 256 + d * P:256 + (d + 1) * P], s0bd[:, d], ident)
                    e.then_inc(rw_VS, 1)
                    pe.wait_ge(rw_sig, it + 1)
                    ada_chunks(qa, 0, 4, 7)
                    for d in range(2):
                        pe.wait_ge(rw_kr, it * 2 + (d + 1))
                        if d == 1:
                            pe.wait_ge(rw_Vt, it + 1)
                            pe.wait_ge(rw_S0s, it + 1)
                        for m, left in enumerate((be, ga)):
                            if d == 1 and m == 1:
                                pe.wait_ge(rw_mA, it * 2 + 1)
                                settle(pe)
                            for g in range(2):
                                for h in range(2):
                                    hs = slice(RH * h, RH * h + RH)
                                    e = mm(bank[AB_BANK[d][m][h]][:, g * 256:(g + 1) * 256], left[hs, d, g],
                                           KR[hs, d, g].rearrange("p a t -> p (a t)"))
                        e.then_inc(rw_A, 1)
                    ada_chunks(qa, 4, 6, 7)
                    pe.wait_ge(rw_m, it * 2 + 2)
                    for d in range(2):
                        for g in range(2):
                            n = 2 * d + g
                            if g == 1:
                                mm(bank[6][:, n * P:(n + 1) * P], KR[:, d, g, 0], S0s[:, d], True, False)
                            for h in range(2):
                                e = mm(bank[6][:, n * P + h * RH:n * P + (h + 1) * RH], BF[:, d, 2 * g + h, 0:P],
                                       Vt[:, g, h * RH:(h + 1) * RH], g == 0, True)
                    e.then_inc(rw_R, 1)
                    pe.wait_ge(rw_bo, it + 1)
                    mm(bank[3][:, 0:256], blk1, flat(nrm[:])).then_inc(rw_bon, 1)
                    ada_chunks(qa, 6, 8, 7)
                    pe.wait_ge(rw_bv, it + 1)
                    settle(pe)

                    def levels(n, m, q, v, first=False):
                        for w in range(2):
                            for d in range(2):
                                pe.wait_ge(lv_C, n + (2 * w + d + 1))
                                pe.wait_ge(lv_X, n + (2 * w + d + 1))
                                settle(pe)
                                for s in range(4):
                                    for hs in halves[0]:
                                        e = mm(bank[d][hs, s * HALF:(s + 1) * HALF], CT[hs, d, s], X[hs, d, s, 0:HALF])
                                e.then_inc(lv_U, 1)
                            if w == 1 and first:
                                pe.wait_ge(lv_X0, it + 1)
                            for d in range(2):
                                if w == 0 and first:
                                    continue
                                pe.wait_ge(lv_Us, m + (2 * w + d - 1))
                                settle(pe)
                                for s in range(4):
                                    for hs in halves[0]:
                                        out = bank[2 + d][hs, s * P:(s + 1) * P]
                                        mm(out[:, 0:HALF], X[hs, d, s, HALF:P], U[hs, d, s])
                                        e = mm(out[:, HALF:P], U[hs, d, s], X[hs, d, s, HALF:P])
                                e.then_inc(lv_XM, 1)
                            if w == 0:
                                pe.wait_ge(rr_v, it * 4 + v + 1)
                                turn_rows(rows3[0:4], 5).then_inc(rp_T, 1)
                            if w == 0 and first:
                                pe.wait_ge(rw_bg, it + 1)
                                for d in range(2):
                                    for k in range(2):
                                        e = pe.transpose(bank[7][:, (2 * d + k) * P:(2 * d + k + 1) * P], bg0[:, d, k], ident)
                                e.then_inc(rw_bgT, 1)
                            ada_chunks(q, 4 * w, 4 * w + 4, 4)

                    levels(it * (2 * LEVELS), it * (2 * LEVELS - 2), qa + 2, 0, first=True)
                    with pe.Fori(1, LEVELS // 2) as v:
                        levels(pe.snap(it * (2 * LEVELS) + v * 4), pe.snap(it * (2 * LEVELS - 2) + v * 4),
                               pe.snap(qa + 2 + v * 2), v)
                    pe.wait_ge(rw_bgs, it + 1)
                    pe.wait_ge(lv_X, it * (2 * LEVELS) + (2 * LEVELS + 2))
                    for half, (ready, done) in enumerate(((rw_Rs, rw_S1), (rw_R2, rw_SA))):
                        pe.wait_ge(ready, it + 1)
                        settle(pe)
                        for g in range(2):
                            for h in range(2):
                                for d in range(2):
                                    n, hs = 2 * d + g, halves[d][half]
                                    e = mm(bank[7][hs, n * P + h * RH:n * P + (h + 1) * RH], X[hs, d, 2 * g + h, HALF:P],
                                           Rs[hs, n, h * RH:(h + 1) * RH])
                        e.then_inc(done, 1)
                        if half == 0:
                            pe.wait_ge(rr_v, it * 4 + 4)
                            turn_rows(rows3[0:4], 5).then_inc(rp_T, 1)
                            pe.wait_ge(rw_S1s, it + 1)
                            settle(pe)
                            for g in range(2):
                                for h in range(2):
                                    for d in range(2):
                                        n, (one, two) = 2 * d + g, halves[d]
                                        e = mm(bank[6][two, n * P + h * RH:n * P + (h + 1) * RH],
                                               AE[one, d, 2 * g + h, two], SA[one, n, h * RH:(h + 1) * RH])
                            e.then_inc(rw_W2, 1)
                    pe.wait_ge(rw_SAs, it + 1)
                    for g in range(2):
                        if g == 1:
                            mm(bank[0][:, P:256], S0s[:, 0], KR[:, 0, 1, 1], True, False)
                            mm(bank[0][:, P:256], S0s[:, 1], KR[:, 1, 1, 1], False, False)
                        for h in range(2):
                            hs = slice(RH * h, RH * h + RH)
                            for d in range(2):
                                mm(bank[0][hs, g * P:(g + 1) * P], SA[:, 2 * d + g, hs], AE[:, d, 2 * g + h, P:256],
                                   g == 0 and d == 0, False)
                                e = mm(bank[0][hs, g * P:(g + 1) * P], Vt[:, g, hs], BF[:, d, 2 * g + h, P:256], False, d == 1)
                    e.then_inc(rw_Y, 1)
                    for d in range(2):
                        for h in range(2):
                            hs = slice(RH * h, RH * h + RH)
                            mm(bank[1][hs, d * RH:(d + 1) * RH], SA[:, 2 * d, hs], bgt[:, d, 0, hs], True, False)
                            e = mm(bank[1][hs, d * RH:(d + 1) * RH], Vt[:, 0, hs], bgt[:, d, 1, hs], False, True)
                    e.then_inc(rw_ST, 1)
                    pe.wait_ge(rw_y, it + 1)
                    mm(bank[2][:, 0:256], blkm, yy[0]).then_inc(rw_mean, 1)
                    pe.wait_ge(rw_y2, it + 1)
                    mm(bank[2][:, 256:512], blkm, yy[1]).then_inc(rw_var, 1)

            def ffn(l):
                ql = l * Q_LAYER

                def turn(j):
                    pe.wait_ge(ff_u, l * FF_TILES + (j + 1))
                    for g in range(2):
                        for k in range(4):
                            e = pe.transpose(bank[4 + g][:, k * P:(k + 1) * P], ff[:, g, k * P:(k + 1) * P], ident)
                        e.then_inc(ff_T, 1)

                def down(q, j):
                    pe.wait_ge(ff_hi, l * (2 * FF_TILES) + (j * 2 + 2))
                    pe.wait_ge(ff_lo, l * (2 * FF_TILES) + (j * 2 + 2))
                    for n in range(4):
                        if n >= 2:
                            pe.wait_ge(dn_out, l * (4 * FF_TILES) + (j * 4 + (n + 3)))
                        for c in range(2):
                            i = 2 * n + c
                            pe.wait_ge(lo_ready, q * 4 + (i + 1 + LEAD))
                            for m in range(2):
                                k = 2 * c + m
                                for g in range(2):
                                    out = bank[(6 if n % 2 == 0 else 4) + g][:]
                                    Hk, Lk = ffH[:, k, g * P:(g + 1) * P], ffL[:, k, g * P:(g + 1) * P]
                                    mm(out, Hk, hiW[:, i % LEAD, m], k == 0, False)
                                    mm(out, Hk, loW[:, i % SLOTS, m], False, False)
                                    e = mm(out, Lk, hiW[:, i % LEAD, m], False, k == 3)
                            e.then_inc(chunk_used, 1)

                gemm(ql + Q_FFN, (0, 1), normed=l * 16 + 8)
                gemm(ql + Q_FFN + 2, (2, 3))
                with pe.Fori(1, FF_TILES) as j:
                    qb = pe.snap(ql + (Q_FFN - 2) + j * 6)
                    pe.wait_ge(ff_g, l * FF_TILES + j)
                    gemm(qb, (0, 1))
                    pe.wait_ge(dn_out, l * (4 * FF_TILES) + j * 4)
                    turn(j - 1)
                    gemm(qb + 2, (2, 3))
                    down(qb + 4, j - 1)
                pe.wait_ge(dn_out, l * (4 * FF_TILES) + 4 * FF_TILES)
                turn(FF_TILES - 1)
                down(ql + (Q_FFN + 4 + 6 * (FF_TILES - 1)), FF_TILES - 1)

            pe.sem_inc(chunk_used, SLOTS)
            pe.sem_inc(lv_U, 2)
            pe.wait_ge(con_in, 16)
            pe.wait_ge(cs_done, 3)
            pe.transpose(bank[0][:, 0:2 * KT], csf[0:2 * KT, 2], con[0:2 * KT, C_ID:C_ID + 2 * KT]).then_inc(cs_done, 1)
            pe.wait_ge(cs_done, 6)
            with pe.Fori(0, LAYERS) as l:
                ql = pe.snap(l * Q_LAYER)
                with pe.Fori(0, 4) as i:
                    ada(pe.snap(ql + Q_ADA01 + i * 4), pe.snap(l * 8 + i * 2))
                pe.wait_ge(par_rows, l * (13 * 16) + 13 * 16)
                settle(pe)
                for r, n, c in ((0, ROWS_P, 0), (1, 64, COL_NG), (2, 96, COL_B)):
                    e = pe.transpose(bank[1][:, c:c + n], prm[0:n, r], con[0:n, C_ID:C_ID + n])
                e.then_inc(cols_T, 1)
                phase_end(pe, "pe", l, 0)
                norm(l * 2, xs1)
                with pe.Fori(0, 4) as i:
                    q = pe.snap(ql + Q_WIN + i * 4)
                    free(l, i * 2)
                    gemm(q, (0, 1), normed=l * 16)
                    free(l, i * 2 + 1)
                    gemm(q + 2, (2, 3))
                free(l, 8)
                gemm(ql + Q_WIN + 16, (0, 1))
                free(l, 9)
                gemm(ql + Q_WIN + 18, (2, 3), width=WIN_LAST)
                phase_end(pe, "pe", l, 1)
                conv(l)
                for g in range(2):
                    attention(l, g)
                    if g == 0:
                        phase_end(pe, "pe", l, 2)
                turn_u(l)
                phase_end(pe, "pe", l, 3)
                rwkv(l)
                phase_end(pe, "pe", l, 4)
                for i in range(4):
                    free(l, WIN_TILES + i)
                    gemm(ql + Q_WOUT + i * 2, (0, 1) if i % 2 == 0 else (2, 3))
                phase_end(pe, "pe", l, 5)
                residual(l * 2, 2)
                phase_end(pe, "pe", l, 6)
                norm(l * 2 + 1, xs2)
                ffn(l)
                phase_end(pe, "pe", l, 7)
                residual(l * 2 + 1, 5)
                phase_end(pe, "pe", l, 8)

        @block.vector
        def _(dve):
            S = Steps(dve, vsteps, VSTEPS)
            R = Steps(dve, fsteps, FSTEPS)
            TT, TS, STT = dve.tensor_tensor, dve.tensor_scalar, dve.scalar_tensor_tensor

            def lo(q, c0, c1, width=NW):
                for c in range(c0, c1):
                    dve.wait_ge(hi_ready, q * 4 + (c + 1))
                    s = c % SLOTS
                    TT(loW[:, s, :, 0:width], rawW[:, s, :, 0:width], hiW[:, c % LEAD, :, 0:width].bitcast(F32),
                       ALU.subtract).then_inc(lo_ready, 1)

            def tile_done(q):
                dve.wait_ge(chunk_used, q * 4 + (CPT + SLOTS))

            def evac(q, out, b, width=NW):
                tile_done(q)
                dve.tensor_copy(out, bank[b][:, 0:width]).then_inc(evac_v, 1)

            mod = modT[:].rearrange("p m k g -> p (m k g)")

            def ada(q, i, a):
                for t in range(2):
                    qt = q + 2 * t
                    lo(qt, 4, 12)
                    tile_done(qt)
                    dve.tensor_copy(rows1[0:4, t], bank[2 * t][0:4, :]).then_inc(rows_out, 1)
                for t in range(2):
                    dve.wait_ge(ada_post, a + (t + 1))
                    dve.tensor_copy(mod[:, bass.ds(i * 16 + 8 * t, 8)], bank[4 + t][:, 0:8])

            def scaled(it, xs):
                dve.wait_ge(sq_in, it * 4 + 2)
                TS(ms, ss, 1.0 / D, EPS, ALU.mult, ALU.add).then_inc(ms_in, 1)
                dve.wait_ge(rs_in, it * 2 + 1)
                for g in range(2):
                    TS(xs[:, g], x[:, g], rstd[:, g:g + 1], None, ALU.mult).then_inc(xs_in, 1)

            def norm(it, tf, sh, ng):
                bias = lambda p: col[:, COL_B + p * KT:COL_B + (p + 1) * KT].unsqueeze(2).broadcast_to([P, KT, 2])
                S.step(TT(modT[:, sh], modT[:, sh], bias(sh), ALU.add))
                S.step(TT(modT[:, sh + 1], modT[:, sh + 1], bias(sh + 1), ALU.add))
                S.step(TS(modT[:, sh + 1], modT[:, sh + 1], 1.0, None, ALU.add))
                S.step(TT(modT[:, sh + 1], modT[:, sh + 1],
                          col[:, COL_NG + ng * KT:COL_NG + (ng + 1) * KT].unsqueeze(2).broadcast_to([P, KT, 2]), ALU.mult))

                def low(b):
                    g, kq = b % 2, b // 2
                    dve.wait_ge(nt_hi, it * 8 + (b + 1))
                    a = slice(4 * kq, 4 * kq + 4), slice(g * P, (g + 1) * P)
                    TT(actL[:, a[0], a[1]], tf[:, b % 2].rearrange("p (k t) -> p k t", k=4),
                       actH[:, a[0], a[1]].bitcast(F32), ALU.subtract).then_inc(nt_lo, 1)

                for b in range(8):
                    g, kq = b % 2, b // 2
                    dve.wait_ge(nt_T, it * 8 + (b + 1))
                    if b >= 2:
                        dve.wait_ge(nt_lo, it * 8 + (b - 1))
                    for j in range(4):
                        k = 4 * kq + j
                        e = TS(tf[:, b % 2, j * P:(j + 1) * P], bank[4 + b % 4][:, j * P:(j + 1) * P],
                               modT[:, sh + 1, k, g:g + 1], modT[:, sh, k, g:g + 1], ALU.mult, ALU.add)
                    e.then_inc(nt_f, 1)
                    if b:
                        low(b - 1)
                low(7)

            def residual(it, part, ng):
                cols = lambda c: col[:, c:c + KT].unsqueeze(2).broadcast_to([P, KT, 2])
                S.step(TT(modT[:, part], modT[:, part], cols(COL_B + part * KT), ALU.add))
                TT(modT[:, part], modT[:, part], cols(COL_NG + ng * KT), ALU.mult).then_inc(rg_m, 1)
                dve.wait_ge(sq_in, it * 4 + 4)
                TS(ms, ss, 1.0 / D, EPS, ALU.mult, ALU.add).then_inc(ms_in, 1)
                dve.wait_ge(rs_in, it * 2 + 2)
                for g in range(2):
                    for n in range(4):
                        c = slice(n * NW, (n + 1) * NW)
                        dve.wait_ge(rg_T, it * 8 + (4 * g + n + 1))
                        S.mark(STT(xs2[:, g, c], o[:, g, c], rstd[:, g:g + 1], bank[4 * g + n][:], ALU.mult, ALU.mult))
                    S.sync()
                    S.mark(TT(x[:, g], x[:, g], xs2[:, g], ALU.add))

            def conv(l):
                dve.wait_ge(cv_z, l + 1)
                for g in range(2):
                    dve.wait_ge(cv_T, l * 6 + (3 + g))
                    dve.wait_ge(cv_ch, l * 2 + (g + 1))
                    S.mark(TT(mT[:, :, g, 1:129], bank[2 + g][:].rearrange("p (f t) -> p f t", f=4), chT[:, g], ALU.mult))
                S.sync()
                for f in range(4):
                    S.mark(TS(cv[:, f], mT[:, f, :, 0:128], col1(COL_CV + f), None, ALU.mult))
                for w in (1, 2):
                    S.sync()
                    for f in range(4):
                        S.mark(STT(cv[:, f], mT[:, f, :, w:w + 128], col1(COL_CV + 4 * w + f), cv[:, f], ALU.mult, ALU.add))
                S.sync()
                for g in range(2):
                    dve.wait_ge(cv_T, l * 6 + (5 + g))
                    TT(cv[:, :, g], cv[:, :, g], bank[g][:].rearrange("p (f t) -> p f t", f=4), ALU.mult).then_inc(cv_out, 1)
                for g in range(2):
                    dve.wait_ge(cv_hi, l * 2 + (g + 1))
                    TT(actL[:, 8:12, g * P:(g + 1) * P], cv[:, :, g], actH[:, 8:12, g * P:(g + 1) * P].bitcast(F32), ALU.subtract)

            def head_squares(l):
                for g in range(2):
                    raw = proj[:, g, 0:D_QK].rearrange("p (h d) -> p h d", d=HD)
                    S.mark(TT((qc, qs)[g], raw, raw, ALU.mult))
                S.sync()
                for g in range(2):
                    S.mark(dve.tensor_reduce(qst[:, 64 + 10 * g:74 + 10 * g], (qc, qs)[g], AX, ALU.add))
                S.sync()
                TS(qst[:, 84:104], qst[:, 64:84], 1.0 / HD, EPS, ALU.mult, ALU.add).then_inc(at_ms, 1)

            def attention(l, g):
                it = l * 2 + g
                nk = P if g == 0 else 2 * P
                raw = proj[:, g, 0:D_QK].rearrange("p (h d) -> p h d", d=HD)
                per_head = lambda v, n, w: v.unsqueeze(2).broadcast_to([P, n, w])
                if g == 0:
                    dve.wait_ge(at_rs, l + 1)
                S.step(TT(qk[:], raw, per_head(qst[:, 104 + 10 * g:114 + 10 * g], 10, HD), ALU.mult))
                S.mark(TT(qk[:, 0:NH], qk[:, 0:NH], qkw[:, 0:1].broadcast_to([P, NH, HD]), ALU.mult))
                e = TT(qk[:, NH:], qk[:, NH:], qkw[:, 1:2].broadcast_to([P, NKV, HD]), ALU.mult)
                if g == 1:
                    S.step(e)
                    table = lambda c: con[:, c:c + HD].unsqueeze(1).broadcast_to([P, 10, HD])
                    S.mark(TT(qc, qk[:], table(C_COS), ALU.mult))
                    for b in range(2):
                        part = lambda t, b: t.rearrange("p h (a b c) -> p h a b c", a=2, b=2)[:, :, :, b]
                        sin = con[:, C_SIN:C_SIN + HD].rearrange("p (a b c) -> p a b c", a=2, b=2)[:, :, b]
                        S.mark(TT(part(qs, b), part(qk[:], 1 - b), sin.unsqueeze(1).broadcast_to([P, 10, 2, 32]), ALU.mult))
                    S.sync()
                    e = TT(qk[:], qc, qs, ALU.add)
                e.then_inc(at_qk, 1)
                dve.wait_ge(at_T, it * 3 + 2)
                dve.tensor_copy(qT[:, 4:8], bank[1][:].rearrange("p (h t) -> p h t", h=4)).then_inc(at_cv, 1)
                for b in range(4):
                    dve.wait_ge(at_S, it * 4 + (b + 1))
                    S.mark(dve.tensor_reduce(qst[:, 30 + 2 * b:32 + 2 * b],
                                             bank[3 + b][:].rearrange("p (h s) -> p h s", h=2)[:, :, 0:nk], AX, ALU.max))
                S.sync()
                TS(qst[:, 40:48], qst[:, 30:38], -SCALE, None, ALU.mult).then_inc(at_mx, 1)
                dve.wait_ge(at_P, it + 1)
                S.step(dve.reciprocal(qst[:, 56:64], qst[:, 48:56]))
                TT(pr[:, :, 0:nk], pr[:, :, 0:nk], per_head(qst[:, 56:64], NH, nk), ALU.mult).then_inc(at_Pn, 1)
                dve.wait_ge(at_PT, it * 2 + 2)
                for k in range(nk // P):
                    e = dve.tensor_copy(pT[:, k, 4:8], bank[2 * k + 1][:].rearrange("p (h t) -> p h t", h=4))
                e.then_inc(at_pv, 1)
                for v in range(NKV):
                    dve.wait_ge(at_hi, it * 2 + (v + 1))
                    a = slice(4 * v, 4 * v + 4), slice(g * P, (g + 1) * P)
                    TT(actL[:, a[0], a[1]], bank[4 + v][:].rearrange("p (h t) -> p h t", h=4),
                       actH[:, a[0], a[1]].bitcast(F32), ALU.subtract).then_inc(at_lo, 1)

            def turn_u(l):
                for b in range(3):
                    dve.wait_ge(u_T, l * 7 + (b + 4))
                    dve.tensor_copy(uT[:, 4 * b:4 * b + 4, 1, 1:129], bank[(3, 6, 7)[b]][:].rearrange("p (f t) -> p f t", f=4))

            def rwkv(l):
                lr = ((12, 64, xwa), (13, GATE_RANK, xg))
                for n, (k, w, out) in enumerate(lr):
                    S.mark(TT(tmp3[0:w, n], uT[0:w, k, :, 0:128], uT[0:w, k, :, 2:130], ALU.add))
                S.sync()
                for n, (k, w, out) in enumerate(lr):
                    S.mark(TS(tmp3[0:w, n], tmp3[0:w, n], muh[0:w, k:k + 1], None, ALU.mult))
                S.sync()
                for n, (k, w, out) in enumerate(lr):
                    e = STT(out[:], uT[0:w, k, :, 1:129], omu[0:w, k:k + 1], tmp3[0:w, n], ALU.mult, ALU.add)
                e.then_inc(lr_mix, 1)
                dve.wait_ge(lr_mix, l + 1)
                settle(dve)
                flat = lambda t: t.rearrange("p g t -> p (g t)")
                with dve.Fori(0, FT) as f:
                    it = dve.snap(l * FT + f)
                    qa = dve.snap(l * Q_LAYER + Q_ADA2 + f * 8)
                    R.start(it)
                    for n in range(3):
                        a = uT[:, bass.ds(f + 4 * n, 1)]
                        R.mark(TT(tmp3[:, n:n + 1], a[:, :, :, 0:128], a[:, :, :, 2:130], ALU.add))
                    R.sync()
                    for n in range(3):
                        R.mark(TS(tmp3[:, n], tmp3[:, n], dyn(muh, f + 4 * n, 1), None, ALU.mult))
                    R.sync()
                    for n in range(3):
                        a = uT[:, bass.ds(f + 4 * n, 1), :, 1:129].rearrange("p f g t -> p (f g) t")
                        e = STT(rkv[:, n], a, dyn(omu, f + 4 * n, 1), tmp3[:, n], ALU.mult, ALU.add)
                    e.then_inc(rw_v, 1)
                    dve.wait_ge(rw_v, it + 1)
                    r_, k_, v_ = (rkv[:, n] for n in range(3))
                    R.step(TS(kk[:], k_, dyn(col, f + COL_KK, 1), None, ALU.mult))
                    TT(ksq[:], kk[:], kk[:], ALU.mult).then_inc(rw_sq, 1)
                    R.mark(dve.memset(cs[:, :, :, 0:1], 0.0))
                    dve.wait_ge(rw_sig, it + 1)
                    for d in range(2):
                        for g in range(2):
                            R.mark(dve.tensor_tensor_scan(cs[:, d, g, 1:129], ones, sig[d][:, g * P:(g + 1) * P], 0.0,
                                                          ALU.mult, ALU.add))
                    dve.wait_ge(rw_nrm, it + 1)
                    TS(flat(nrm[:]), bank[0][:, 0:256], KK_EPS, None, ALU.add).then_inc(rw_ns, 1)
                    R.sync()
                    mid = cs[:, :, :, 64:65].rearrange("p d g o -> p d (g o)")
                    TS(amid[:, 0:4].rearrange("p (d g) -> p d g", d=2), mid, ALPHA, None, ALU.mult)
                    TS(amid[:, 4:8].rearrange("p (d g) -> p d g", d=2), mid, -ALPHA, None, ALU.mult).then_inc(rw_c, 1)
                    dve.wait_ge(rw_aa, it + 1)
                    for d in range(2):
                        R.mark(TS(flat(kd[:, d]), aa[d], dyn(col, f + COL_KA, 1), dyn(oka, f, 1), ALU.mult, ALU.add))
                    R.mark(dve.tensor_copy(flat(gT[:]), bank[6][:, 0:256]))
                    R.sync()
                    for d in range(2):
                        R.mark(TT(kd[:, d], kd[:, d], k_, ALU.mult))
                    dve.wait_ge(rw_rs, it + 1)
                    R.step(dve.reciprocal(ksq[:], ksq[:]))
                    R.step(TT(kk[:], kk[:], ksq[:], ALU.mult))
                    for d in range(2):
                        R.mark(TT(flat(be[:, d]), flat(kk[:]), aa[d], ALU.mult))
                    R.sync()
                    dve.wait_ge(rw_E, it + 1)
                    for d in range(2):
                        Ei, Ex, Ev = ((E1[:, d, :, 1:129], E1[:, d, :, 0:128], E2[:, d, :, 1:129]) if d == 0 else
                                      (E2[:, d, :, 0:128], E2[:, d, :, 1:129], E1[:, d, :, 0:128]))
                        TT(KR[:, d, :, 0], kk[:], Ex, ALU.mult)
                        TT(KR[:, d, :, 1], r_, Ei, ALU.mult)
                        TT(ga[:, d], kd[:, d], Ev, ALU.mult)
                        TT(be[:, d], be[:, d], Ev, ALU.mult).then_inc(rw_kr, 1)
                    dve.wait_ge(rw_Vt, it + 1)
                    for d, mid in ((0, E2[:, 0, 1, 0:1]), (1, E1[:, 1, 1, 128:129])):
                        e = TS(S0s[:, d], bank[3][:, 256 + d * P:256 + (d + 1) * P], mid, None, ALU.mult)
                    e.then_inc(rw_S0s, 1)
                    lo(qa, 4, 6)
                    for d in range(2):
                        dve.wait_ge(rw_A, it * 2 + (d + 1))
                        if d == 0:
                            dve.wait_ge(ab_z, l + 1)
                        mask = con[:, C_TRI + d * 256:C_TRI + (d + 1) * 256].bitcast(U32).unsqueeze(1).broadcast_to([P, 2, 256])
                        settle(dve)
                        for m, (dst, done) in enumerate(((AE, rw_mA), (BF, rw_m))):
                            for h in range(2):
                                e = dve.copy_predicated(dst[:, d, h:4:2], mask,
                                                        bank[AB_BANK[d][m][h]][:].rearrange("p (g t) -> p g t", g=2))
                            e.then_inc(done, 1)
                    R.mark(TT(nrm[:], kd[:, 0], kd[:, 1], ALU.add))
                    R.step(TS(ksq[:], r_, dyn(col, f + COL_RK, 1), None, ALU.mult))
                    TT(nrm[:], nrm[:], ksq[:], ALU.mult).then_inc(rw_bo, 1)
                    for d, end in ((0, E1[:, 0, 0, 128:129]), (1, E2[:, 1, 0, 0:1])):
                        TS(bg0[:, d, 0], be[:, d, 0], end, None, ALU.mult)
                        e = TS(bg0[:, d, 1], ga[:, d, 0], end, None, ALU.mult)
                    e.then_inc(rw_bg, 1)
                    lo(qa, 6, 8)
                    dve.wait_ge(rw_bon, it + 1)
                    TT(flat(nrm[:]), bank[3][:, 0:256], flat(v_), ALU.mult).then_inc(rw_bv, 1)
                    tile_done(qa)
                    dve.tensor_copy(rows3[0:4], bank[7][0:4, :]).then_inc(rr_v, 1)
                    lo(qa, 8, 12)

                    def levels(n, m, q, v, first=False):
                        for w in range(2):
                            for d in range(2):
                                if w == 0 and first:
                                    dve.wait_ge(lv_U, n + (d + 3))
                                    TT(X[:, d, :, 0:HALF], X[:, d, :, 0:HALF],
                                       bank[d][:, 0:4 * HALF].rearrange("p (s t) -> p s t", s=4), ALU.add).then_inc(lv_X, 1)
                                else:
                                    dve.wait_ge(lv_XM, m + (2 * w + d - 1))
                                    TT(X[:, d], X[:, d], bank[2 + d][:].rearrange("p (s t) -> p s t", s=4),
                                       ALU.add).then_inc(lv_X, 1)
                            if w == 0:
                                dve.wait_ge(rp_T, it * 4 + v + 1)
                                dve.tensor_copy(mod[:, bass.ds(f * 32 + v * 8 + 64, 8)], bank[5][:, 0:8])
                            lo(q, 4 + 4 * w, 8 + 4 * w)
                        tile_done(q)
                        dve.tensor_copy(rows3[0:4], bank[4][0:4, :]).then_inc(rr_v, 1)

                    levels(it * (2 * LEVELS), it * (2 * LEVELS - 2), qa + 2, 0, first=True)
                    with dve.Fori(1, LEVELS // 2) as v:
                        levels(dve.snap(it * (2 * LEVELS) + v * 4), dve.snap(it * (2 * LEVELS - 2) + v * 4),
                               dve.snap(qa + 2 + v * 2), v)
                    dve.wait_ge(rw_W2, it + 1)
                    for d in range(2):
                        two = halves[d][1]
                        e = TT(Rs[two, 2 * d:2 * d + 2], Rs[two, 2 * d:2 * d + 2],
                               bank[6][two, 2 * d * P:(2 * d + 2) * P].rearrange("p (n i) -> p n i", n=2), ALU.add)
                    e.then_inc(rw_R2, 1)
                    dve.wait_ge(rp_T, it * 4 + 4)
                    dve.tensor_copy(mod[:, bass.ds(f * 32 + 88, 8)], bank[5][:, 0:8])
                    y0, y1, y2, y3 = yy
                    dve.wait_ge(rw_Y, it + 1)
                    dve.tensor_copy(y0, bank[0][:, 0:256]).then_inc(rw_y, 1)
                    dve.wait_ge(rw_y, it + 1)
                    dve.wait_ge(rw_mean, it + 1)
                    TT(y0, y0, bank[2][:, 0:256], ALU.subtract).then_inc(rw_yc, 1)
                    dve.wait_ge(rw_yc, it + 1)
                    dve.wait_ge(rw_var, it + 1)
                    TS(y2, bank[2][:, 256:512], GN_EPS, None, ALU.add).then_inc(rw_vs, 1)
                    dve.wait_ge(rw_vr, it + 1)
                    R.step(dve.reciprocal(y3, y3))
                    R.step(TT(y0, y0, y3, ALU.mult))
                    R.step(TS(y0, y0, dyn(col, f + COL_LG, 1), dyn(col, f + COL_LB, 1), ALU.mult, ALU.add))
                    R.step(TT(y0, y0, flat(nrm[:]), ALU.add))
                    TT(y0, y0, flat(gT[:]), ALU.mult).then_inc(rw_o, 1)
                    dve.wait_ge(rw_hi, it + 1)
                    TT(actL[:, bass.ds(f + 12, 1)], y0.unsqueeze(1), actH[:, bass.ds(f + 12, 1)].bitcast(F32),
                       ALU.subtract).then_inc(rw_lo, 1)
                    R.end()

            def ffn(l):
                ql = l * Q_LAYER

                def gate(q):
                    tile_done(q)
                    for g in range(2):
                        dve.wait_ge(ff_s, gate.base + (g + 1))
                        e = TT(sg[:, g], sg[:, g], bank[g][:], ALU.mult)
                    e.then_inc(ff_g, 1)

                def up(q, j):
                    tile_done(q)
                    dve.wait_ge(ff_g, l * FF_TILES + (j + 1))
                    for g in range(2):
                        e = TT(ff[:, g], sg[:, g], bank[2 + g][:], ALU.mult)
                    e.then_inc(ff_u, 1)

                def turned(j):
                    for g in range(2):
                        dve.wait_ge(ff_hi, l * (2 * FF_TILES) + (j * 2 + (g + 1)))
                        TT(ffL[:, :, g * P:(g + 1) * P], bank[4 + g][:].rearrange("p (k t) -> p k t", k=4),
                           ffH[:, :, g * P:(g + 1) * P].bitcast(F32), ALU.subtract).then_inc(ff_lo, 1)

                def down(q, n):
                    dve.wait_ge(chunk_used, q * 4 + (2 * n + 2 + SLOTS))
                    for g in range(2):
                        out = o[:, g, n * NW:(n + 1) * NW]
                        e = TT(out, out, bank[(6 if n % 2 == 0 else 4) + g][:], ALU.add)
                    e.then_inc(dn_out, 1)

                def down_all(q, last=False):
                    for n in range(4):
                        if n < 2 or not last:
                            lo(q, 4 + 2 * n, 6 + 2 * n)
                        down(q, n)

                lo(ql + Q_FFN, 4, 12)
                gate.base = l * (2 * FF_TILES)
                gate(ql + Q_FFN)
                lo(ql + Q_FFN + 2, 4, 12)
                up(ql + Q_FFN + 2, 0)
                with dve.Fori(1, FF_TILES) as j:
                    qb = dve.snap(ql + (Q_FFN - 2) + j * 6)
                    lo(qb, 4, 12)
                    gate.base = l * (2 * FF_TILES) + j * 2
                    gate(qb)
                    turned(j - 1)
                    lo(qb + 2, 4, 12)
                    up(qb + 2, j)
                    dve.wait_ge(dn_out, l * (4 * FF_TILES) + (j * 4))
                    down_all(qb + 4)
                turned(FF_TILES - 1)
                dve.wait_ge(dn_out, l * (4 * FF_TILES) + 4 * FF_TILES)
                down_all(ql + (Q_FFN + 4 + 6 * (FF_TILES - 1)), last=True)

            dve.sem_inc(lo_ready, LEAD)
            dve.sem_inc(rows_out, 2)
            dve.sem_inc(evac_v, 2)
            dve.sem_inc(evac_s, 2)
            dve.sem_inc(lv_X, 2)
            dve.sem_inc(rw_lo, 1)
            dve.sem_inc(dn_out, 4)
            csv = csR[:, 0:4 * KT].rearrange("p (k c) -> p c k", c=4)
            dve.memset(csR[:].bitcast(F32), 0.0).then_inc(cs_done, 1)
            dve.wait_ge(cs_done, 2)
            TT(csf[0:2 * KT, 2], csf[0:2 * KT, 0], csf[0:2 * KT, 1], ALU.mult).then_inc(cs_done, 1)
            dve.wait_ge(cs_done, 5)
            TT(csv[:, 2:4], bank[0][:, 0:2 * KT].rearrange("p (g k) -> p g k", g=2), csv[:, 0:2].bitcast(F32),
               ALU.subtract).then_inc(cs_done, 1)
            with dve.Fori(0, LAYERS) as l:
                ql = dve.snap(l * Q_LAYER)
                S.start(l)
                dve.memset(prm[:, 0], 0.0).then_inc(prm_zero, 1)
                lo(ql, 0, 4)
                with dve.Fori(0, 4) as i:
                    ada(dve.snap(ql + Q_ADA01 + i * 4), i, dve.snap(l * 8 + i * 2))
                dve.wait_ge(cols_T, l + 1)
                S.step(dve.tensor_copy(col[:], bank[1][:, 0:COLS]))
                S.mark(TS(muh[:], col[:, COL_MU:COL_MU + 14], 0.5, None, ALU.mult))
                S.mark(TS(omu[:], col[:, COL_MU:COL_MU + 14], -1.0, 1.0, ALU.mult, ALU.add))
                S.step(TS(oka[:], col[:, COL_KA:COL_KA + 4], -1.0, 1.0, ALU.mult, ALU.add))
                phase_end(dve, "dve", l, 0)
                norm(l * 2, tf1, 0, 0)
                with dve.Fori(0, 4) as i:
                    q = dve.snap(ql + Q_WIN + i * 4)
                    lo(q, 4, 12)
                    evac(q, proj[:, 0, bass.ds(i * (2 * NW), NW)], 0)
                    lo(q + 2, 4, 12)
                    evac(q + 2, proj[:, 0, bass.ds(i * (2 * NW) + NW, NW)], 2)
                q = ql + Q_WIN + 16
                lo(q, 4, 8)
                lo(q, 8, 12, WIN_LAST)
                evac(q, proj[:, 0, 8 * NW:9 * NW], 0)
                lo(q + 2, 4, 8, WIN_LAST)
                lo(q + 2, 8, 12)
                evac(q + 2, proj[:, 0, 9 * NW:D_IN], 2, WIN_LAST)
                phase_end(dve, "dve", l, 1)
                dve.wait_ge(par_tabs, l * (9 * 16) + 9 * 16)
                head_squares(l)
                conv(l)
                for g in range(2):
                    attention(l, g)
                    if g == 0:
                        phase_end(dve, "dve", l, 2)
                turn_u(l)
                phase_end(dve, "dve", l, 3)
                rwkv(l)
                phase_end(dve, "dve", l, 4)
                for i in range(2):
                    q = ql + Q_WOUT + i * 4
                    lo(q, 4, 12)
                    evac(q, o[:, 0, 2 * i * NW:(2 * i + 1) * NW], 0)
                    lo(q + 2, 4, 12)
                    evac(q + 2, o[:, 0, (2 * i + 1) * NW:(2 * i + 2) * NW], 2)
                phase_end(dve, "dve", l, 5)
                residual(l * 2, 2, 1)
                phase_end(dve, "dve", l, 6)
                scaled(l * 2 + 1, xs2)
                norm(l * 2 + 1, tf2, 3, 2)
                ffn(l)
                phase_end(dve, "dve", l, 7)
                residual(l * 2 + 1, 5, 3)
                S.end()
                phase_end(dve, "dve", l, 8)


INS = ["x_prompt", "x_sample", "cache_k", "cache_v", "state_rwkv", "c", "c_ctx", "w_ada", "b_ada", "norm_g", "w_in",
       "q_norm", "k_norm", "conv_w", "rwkv_mu", "rwkv_w0", "rwkv_w_up", "rwkv_a0", "rwkv_a_up", "rwkv_g_up",
       "rwkv_k_k", "rwkv_k_a", "rwkv_r_k", "rwkv_ln_g", "rwkv_ln_b", "w_out", "w_gate", "w_up", "w_down"]
OUTS = {"y_prompt": (1, P, D), "y_sample": (1, P, D), "new_k": (1, LAYERS, P, NKV, HD), "new_v": (1, LAYERS, P, NKV, HD),
        "new_rwkv": (1, LAYERS, 2, RW_HEADS, RH, RH)}


def build(nc, shapes):
    A = {n: nc.dram_tensor(f"in_{n}", shapes[n], F32, kind="ExternalInput").ap() for n in INS + ["consts"]}
    O = {n: nc.dram_tensor(f"out_{n}", s, F32, kind="ExternalOutput").ap() for n, s in OUTS.items()}
    hybrid_trunk(nc, A, O)


def kernel(**inputs):
    import concourse.bacc as bacc
    from concourse.bass_utils import run_bass_kernel_spmd

    nc = bacc.Bacc("TRN2", target_bir_lowering=False, num_devices=1)
    arrays = {n: np.ascontiguousarray(inputs[n]) for n in INS}
    arrays["consts"] = constants()
    build(nc, {n: a.shape for n, a in arrays.items()})
    r = run_bass_kernel_spmd(nc, [{f"in_{n}": a for n, a in arrays.items()}], core_ids=[0])
    return tuple(r.results[0][f"out_{n}"] for n in OUTS)
```
